# Optimizing a Trainium2 kernel written in Bass

```python
import jax, jax.numpy as jnp
from jax import lax
import numpy as np

D_MODEL = 1024
BATCH = 1
SEQ = 256
DEPTH = 2

RET_HEADS = 4
RET_DK = 128
RET_DV = 256
RET_QK = RET_HEADS * RET_DK
RET_V = RET_HEADS * RET_DV
RET_CHUNK = 128
ROPE_BASE = 10000.0
SB_HEADS = 8
SB_DH = 64
SB_W = SB_HEADS * SB_DH
SB_BLOCK = 128
FF = ((8 * D_MODEL + 3 * 256 - 1) // (3 * 256)) * 256
NORM_EPS = 1e-6
IN_SPLITS = (RET_QK, RET_QK, RET_V, RET_V, SB_W, SB_W, SB_W, D_MODEL, D_MODEL)
IN_COLS = sum(IN_SPLITS)


def _rmsnorm(x, g):
    x32 = x.astype(jnp.float32)
    y = x32 * lax.rsqrt(jnp.mean(x32 * x32, axis=-1, keepdims=True) + NORM_EPS)
    return (y * g.astype(jnp.float32)).astype(x.dtype)

def _split_cols(p):
    offs = np.cumsum(IN_SPLITS)[:-1].tolist()
    return jnp.split(p, offs, axis=-1)

def _rope(x):
    S, d = x.shape[1], x.shape[-1]
    half = d // 2
    pos = jnp.arange(S, dtype=jnp.float32)
    inv = 1.0 / (ROPE_BASE ** (jnp.arange(half, dtype=jnp.float32) / half))
    ang = pos[:, None] * inv[None, :]
    cos = jnp.cos(ang)[None, :, None, :]
    sin = jnp.sin(ang)[None, :, None, :]
    x32 = x.astype(jnp.float32)
    x1, x2 = x32[..., :half], x32[..., half:]
    return jnp.concatenate([x1 * cos - x2 * sin, x1 * sin + x2 * cos], axis=-1)

def _retention_chunkwise(q, k, v):
    B, S, H, DK = q.shape
    DV = v.shape[-1]
    C = RET_CHUNK
    N = S // C
    log_g = jnp.log1p(-jnp.exp2(-5.0 - jnp.arange(H, dtype=jnp.float32)))
    q = q.reshape(B, N, C, H, DK)
    k = k.reshape(B, N, C, H, DK)
    v = v.reshape(B, N, C, H, DV)
    i = jnp.arange(C, dtype=jnp.float32)
    diff = i[:, None] - i[None, :]
    dec = jnp.where(diff[None] >= 0,
                    jnp.exp(log_g[:, None, None] * jnp.maximum(diff, 0.0)[None]), 0.0)
    scores = jnp.einsum('bnihd,bnjhd->bnhij', q, k) * dec[None, None]
    o_intra = jnp.einsum('bnhij,bnjhe->bnihe', scores, v)
    k_dec = jnp.exp(log_g[:, None] * (C - 1.0 - i)[None, :])
    kv = jnp.einsum('bnjhd,hj,bnjhe->nbhde', k, k_dec, v)
    chunk_dec = jnp.exp(log_g * C)[None, :, None, None]

    def step(R, kv_n):
        return chunk_dec * R + kv_n, R

    _, R_prev = lax.scan(step, jnp.zeros((B, H, DK, DV), jnp.float32), kv)
    q_dec = jnp.exp(log_g[:, None] * (i + 1.0)[None, :])
    o_cross = jnp.einsum('bnihd,nbhde,hi->bnihe', q, R_prev, q_dec)
    return (o_intra + o_cross).reshape(B, S, H, DV)

def _head_norm(y):
    mu = jnp.mean(y, axis=-1, keepdims=True)
    var = jnp.mean(jnp.square(y - mu), axis=-1, keepdims=True)
    return (y - mu) * lax.rsqrt(var + NORM_EPS)

def _stick_breaking(q, k, v):
    B, S, H, d = q.shape
    scale = d ** -0.5
    outs = []
    for blk in range(S // SB_BLOCK):
        start, end = blk * SB_BLOCK, (blk + 1) * SB_BLOCK
        qb = q[:, start:end]
        kk = k[:, :end]
        vv = v[:, :end]
        z = jnp.einsum('bqhd,bkhd->bhqk', qb, kk).astype(jnp.float32) * scale
        q_pos = start + jnp.arange(SB_BLOCK)
        k_pos = jnp.arange(end)
        mask = (k_pos[None, :] < q_pos[:, None])[None, None]
        log_beta = jax.nn.log_sigmoid(z)
        log_one_minus = jnp.where(mask, jax.nn.log_sigmoid(-z), 0.0)
        suffix = lax.cumsum(log_one_minus, axis=3, reverse=True) - log_one_minus
        A = jnp.where(mask, jnp.exp(log_beta + suffix), 0.0)
        outs.append(jnp.einsum('bhqk,bkhd->bqhd', A.astype(v.dtype), vv))
    return jnp.concatenate(outs, axis=1)

def _mixer(h, w_in, w_ret_o, w_sb_o, w_out):
    B, S, _ = h.shape
    proj = jnp.einsum('bsd,df->bsf', h, w_in)
    rq, rk, rv, rg, sq, sk, sv, gr, gs = _split_cols(proj)
    rq = _rope(rq.reshape(B, S, RET_HEADS, RET_DK))
    rk = _rope(rk.reshape(B, S, RET_HEADS, RET_DK)) * (RET_DK ** -0.5)
    rv = rv.reshape(B, S, RET_HEADS, RET_DV).astype(jnp.float32)
    ret = _head_norm(_retention_chunkwise(rq, rk, rv)).reshape(B, S, RET_V).astype(h.dtype)
    ret = ret * jax.nn.silu(rg)
    ret = jnp.einsum('bsv,vd->bsd', ret, w_ret_o)
    sb = _stick_breaking(sq.reshape(B, S, SB_HEADS, SB_DH),
                         sk.reshape(B, S, SB_HEADS, SB_DH),
                         sv.reshape(B, S, SB_HEADS, SB_DH)).reshape(B, S, SB_W)
    sb = jnp.einsum('bsv,vd->bsd', sb, w_sb_o)
    merged = jax.nn.sigmoid(gr) * ret + jax.nn.sigmoid(gs) * sb
    return jnp.einsum('bsd,de->bse', merged, w_out)

def _swiglu(h, w_gate_up, w_down):
    gu = jnp.einsum('bsd,df->bsf', h, w_gate_up)
    g, u = gu[..., :FF], gu[..., FF:]
    return jnp.einsum('bsf,fd->bsd', jax.nn.silu(g) * u, w_down)

def first_inputs(seed: int = 0) -> dict:
    key = jax.random.key(seed)
    ks = jax.random.split(key, 10)
    f32 = jnp.float32

    def w(k, shape, fan_in):
        return jax.random.normal(k, shape, f32) * (fan_in ** -0.5)

    return {
        "x": jax.random.normal(ks[0], (BATCH, SEQ, D_MODEL), f32),
        "norm_mix": 1.0 + 0.02 * jax.random.normal(ks[1], (DEPTH, D_MODEL), f32),
        "w_in": w(ks[2], (DEPTH, D_MODEL, IN_COLS), D_MODEL),
        "w_ret_o": w(ks[3], (DEPTH, RET_V, D_MODEL), RET_V),
        "w_sb_o": w(ks[4], (DEPTH, SB_W, D_MODEL), SB_W),
        "w_out": w(ks[5], (DEPTH, D_MODEL, D_MODEL), D_MODEL),
        "norm_ffn": 1.0 + 0.02 * jax.random.normal(ks[6], (DEPTH, D_MODEL), f32),
        "w_gate_up": w(ks[7], (DEPTH, D_MODEL, 2 * FF), D_MODEL),
        "w_down": w(ks[8], (DEPTH, FF, D_MODEL), FF),
        "norm_final": 1.0 + 0.02 * jax.random.normal(ks[9], (D_MODEL,), f32),
    }

def first_block(x, norm_mix, w_in, w_ret_o, w_sb_o, w_out, norm_ffn, w_gate_up, w_down, norm_final):
    h = x
    for layer in range(DEPTH):
        hn = _rmsnorm(h, norm_mix[layer])
        h = h + _mixer(hn, w_in[layer], w_ret_o[layer], w_sb_o[layer], w_out[layer])
        hn = _rmsnorm(h, norm_ffn[layer])
        h = h + _swiglu(hn, w_gate_up[layer], w_down[layer])
    return _rmsnorm(h, norm_final)


HEAD_DIM = 64
MLA_HEADS = 8
MLA_Q_RANK = 256
MLA_KV_RANK = 128
MLA_NOPE = 64
MLA_ROPE = 32
MLA_V = 64
DSA_HEADS = 4
IDX_HEADS = 8
IDX_DIM = 32
DSA_TOPK_MAX = 256
DIL_CONFIGS = ((128, 1), (512, 4), (2048, 16))
DIL_HEADS = 4
MIX_WIDTH = (MLA_HEADS + DSA_HEADS + DIL_HEADS) * HEAD_DIM
ROPE_THETA = 500000.0
ROT_HEAD_DIMS = HEAD_DIM // 4
ROT_IDX_DIMS = IDX_DIM // 4
Q_BLOCK = 128
N_GROUPS = 4
EXPERTS_PER_GROUP = 8
TOP_K_IN_GROUP = 2
EXPERT_HIDDEN = 256
DEEPNORM_ALPHA = (2.0 * DEPTH) ** 0.25
DEEPNORM_BETA = (8.0 * DEPTH) ** -0.25
LN_EPS = 1e-5
RMS_EPS = 1e-6
NEG_INF = -1e30
IN_SPLITS_2 = (MLA_Q_RANK, MLA_KV_RANK, MLA_ROPE,
             DSA_HEADS * HEAD_DIM, HEAD_DIM, HEAD_DIM,
             IDX_HEADS * IDX_DIM, IDX_DIM, IDX_HEADS,
             3 * len(DIL_CONFIGS) * DIL_HEADS * HEAD_DIM)
IN_COLS_2 = sum(IN_SPLITS_2)


def layer_norm(x, g, b):
    xf = x.astype(jnp.float32)
    mu = jnp.mean(xf, -1, keepdims=True)
    var = jnp.mean(jnp.square(xf - mu), -1, keepdims=True)
    return ((xf - mu) * lax.rsqrt(var + LN_EPS) * g.astype(jnp.float32) + b.astype(jnp.float32)).astype(x.dtype)

def rms_norm(x, g):
    xf = x.astype(jnp.float32)
    y = xf * lax.rsqrt(jnp.mean(jnp.square(xf), -1, keepdims=True) + RMS_EPS)
    return (y * g.astype(jnp.float32)).astype(x.dtype)

def rope_table(positions, rot_dims):
    inv = ROPE_THETA ** (-jnp.arange(0, rot_dims, 2, dtype=jnp.float32) / rot_dims)
    ang = positions.astype(jnp.float32)[..., None] * inv
    return jnp.cos(ang), jnp.sin(ang)

def apply_rope(x, cos, sin):
    half = cos.shape[-1]
    r = 2 * half
    c, s = cos[:, :, None, :], sin[:, :, None, :]
    xf = x[..., :r].astype(jnp.float32)
    x1, x2 = xf[..., :half], xf[..., half:]
    rot = jnp.concatenate([x1 * c - x2 * s, x2 * c + x1 * s], -1).astype(x.dtype)
    return jnp.concatenate([rot, x[..., r:]], -1)

def _to_blocks(a):
    B, S = a.shape[:2]
    return jnp.moveaxis(a.reshape(B, S // Q_BLOCK, Q_BLOCK, *a.shape[2:]), 1, 0)

def _from_blocks(a):
    nb, B, qb = a.shape[:3]
    return jnp.moveaxis(a, 0, 1).reshape(B, nb * qb, *a.shape[3:])

def _block_starts(S):
    return jnp.arange(S // Q_BLOCK, dtype=jnp.int32) * Q_BLOCK

def mla_mixer(cq, ckv, kpe, q_norm, kv_norm, w_uq, w_ukv, cos, sin):
    B, S = cq.shape[:2]
    q = jnp.einsum('bsr,rc->bsc', rms_norm(cq, q_norm), w_uq).reshape(B, S, MLA_HEADS, MLA_NOPE + MLA_ROPE)
    q = jnp.concatenate([q[..., :MLA_NOPE], apply_rope(q[..., MLA_NOPE:], cos, sin)], -1)
    kv = jnp.einsum('bsr,rc->bsc', rms_norm(ckv, kv_norm), w_ukv).reshape(B, S, MLA_HEADS, MLA_NOPE + MLA_V)
    k_pe = apply_rope(kpe[:, :, None, :], cos, sin)
    k = jnp.concatenate([kv[..., :MLA_NOPE], jnp.broadcast_to(k_pe, (B, S, MLA_HEADS, MLA_ROPE))], -1)
    v = kv[..., MLA_NOPE:]
    scale = (MLA_NOPE + MLA_ROPE) ** -0.5
    key_pos = jnp.arange(S, dtype=jnp.int32)

    def block(args):
        q0, qb = args
        qpos = q0 + jnp.arange(Q_BLOCK, dtype=jnp.int32)
        s = jnp.einsum('bqhd,bkhd->bhqk', qb, k, preferred_element_type=jnp.float32) * scale
        s = jnp.where(key_pos[None, :] <= qpos[:, None], s, NEG_INF)
        p = jax.nn.softmax(s, -1).astype(v.dtype)
        return jnp.einsum('bhqk,bkhd->bqhd', p, v)

    o = _from_blocks(lax.map(block, (_block_starts(S), _to_blocks(q))))
    return o.reshape(B, S, MLA_HEADS * MLA_V)

def dsa_mixer(q, k, v, qi, ki, wi, cos_h, sin_h, cos_i, sin_i):
    B, S = q.shape[:2]
    q = apply_rope(q.reshape(B, S, DSA_HEADS, HEAD_DIM), cos_h, sin_h)
    k = apply_rope(k[:, :, None, :], cos_h, sin_h)[:, :, 0]
    qi = apply_rope(qi.reshape(B, S, IDX_HEADS, IDX_DIM), cos_i, sin_i)
    ki = apply_rope(ki[:, :, None, :], cos_i, sin_i)[:, :, 0]
    top_k = min(DSA_TOPK_MAX, S // 4)
    key_pos = jnp.arange(S, dtype=jnp.int32)
    gather = jax.vmap(lambda arr, idx: arr[idx])
    idx_scale = IDX_DIM ** -0.5 * IDX_HEADS ** -0.5

    def block(args):
        q0, qb, qib, wb = args
        qpos = q0 + jnp.arange(Q_BLOCK, dtype=jnp.int32)
        rel = jax.nn.relu(jnp.einsum('bqhd,bsd->bqhs', qib, ki, preferred_element_type=jnp.float32))
        score = jnp.einsum('bqhs,bqh->bqs', rel, wb.astype(jnp.float32)) * idx_scale
        score = jnp.where(key_pos[None, None, :] <= qpos[None, :, None], score, NEG_INF)
        _, sel = lax.top_k(score, top_k)
        k_sel = gather(k, sel)
        v_sel = gather(v, sel)
        valid = sel <= qpos[None, :, None]
        s = jnp.einsum('bqhd,bqkd->bhqk', qb, k_sel, preferred_element_type=jnp.float32) * HEAD_DIM ** -0.5
        s = jnp.where(valid[:, None], s, NEG_INF)
        p = jax.nn.softmax(s, -1).astype(v.dtype)
        return jnp.einsum('bhqk,bqkd->bqhd', p, v_sel)

    o = _from_blocks(lax.map(block, (_block_starts(S), _to_blocks(q), _to_blocks(qi), _to_blocks(wi))))
    return o.reshape(B, S, DSA_HEADS * HEAD_DIM)

def dilated_window_attention(q, k, v, window, dilation):
    S = q.shape[1]
    n_keys = window // dilation + 1
    offs = dilation * jnp.arange(n_keys, dtype=jnp.int32)

    def block(args):
        q0, qb = args
        qpos = q0 + jnp.arange(Q_BLOCK, dtype=jnp.int32)
        idx = qpos[:, None] - offs[None, :]
        valid = idx >= 0
        idx = jnp.maximum(idx, 0)
        k_sel = k[:, idx]
        v_sel = v[:, idx]
        s = jnp.einsum('bqhd,bqkhd->bqhk', qb, k_sel, preferred_element_type=jnp.float32) * HEAD_DIM ** -0.5
        s = jnp.where(valid[None, :, None, :], s, NEG_INF)
        lse = jax.nn.logsumexp(s, -1)
        p = jnp.exp(s - lse[..., None]).astype(v.dtype)
        return jnp.einsum('bqhk,bqkhd->bqhd', p, v_sel), lse

    o, lse = lax.map(block, (_block_starts(S), _to_blocks(q)))
    return _from_blocks(o), _from_blocks(lse)

def dilated_mixer(qkv, cos, sin):
    B, S = qkv.shape[:2]
    n_cfg = len(DIL_CONFIGS)
    qkv = qkv.reshape(B, S, 3, n_cfg * DIL_HEADS, HEAD_DIM)
    q = apply_rope(qkv[:, :, 0], cos, sin)
    k = apply_rope(qkv[:, :, 1], cos, sin)
    v = qkv[:, :, 2]
    outs, lses = [], []
    for g, (window, dilation) in enumerate(DIL_CONFIGS):
        sl = slice(g * DIL_HEADS, (g + 1) * DIL_HEADS)
        o, lse = dilated_window_attention(q[:, :, sl], k[:, :, sl], v[:, :, sl], window, dilation)
        outs.append(o)
        lses.append(lse)
    wts = jax.nn.softmax(jnp.stack(lses, 0), axis=0)
    o = jnp.sum(wts[..., None] * jnp.stack(outs, 0).astype(jnp.float32), 0).astype(qkv.dtype)
    return o.reshape(B, S, DIL_HEADS * HEAD_DIM)

def hybrid_mixer(x, tabs, w_in, q_norm, kv_norm, w_uq, w_ukv, w_o):
    (cos_m, sin_m), (cos_h, sin_h), (cos_i, sin_i) = tabs
    u = jnp.einsum('bsd,dc->bsc', x, w_in)
    cuts = [int(c) for c in np.cumsum(IN_SPLITS_2)[:-1]]
    a_cq, a_ckv, a_kpe, b_q, b_k, b_v, b_qi, b_ki, b_wi, c_qkv = jnp.split(u, cuts, axis=-1)
    o_a = mla_mixer(a_cq, a_ckv, a_kpe, q_norm, kv_norm, w_uq, w_ukv, cos_m, sin_m)
    o_b = dsa_mixer(b_q, b_k, b_v, b_qi, b_ki, b_wi, cos_h, sin_h, cos_i, sin_i)
    o_c = dilated_mixer(c_qkv, cos_h, sin_h)
    o = jnp.concatenate([o_a, o_b, o_c], -1)
    return jnp.einsum('bsc,cd->bsd', o, w_o)

def hier_moe(x, rg_w, rg_b, re_w, re_b, w_gate, w_up, w_down):
    B, S, D = x.shape
    t = x.reshape(B * S, D)
    lg = jnp.einsum('td,dg->tg', t, rg_w, preferred_element_type=jnp.float32) + rg_b.astype(jnp.float32)
    g_star = jnp.argmax(lg, -1)
    g_hot = jax.nn.one_hot(g_star, N_GROUPS, dtype=jnp.float32)
    p_top = jnp.sum(jax.nn.softmax(lg, -1) * g_hot, -1, keepdims=True)
    le = jnp.einsum('td,gde->tge', t, re_w, preferred_element_type=jnp.float32) + re_b.astype(jnp.float32)
    le = jnp.einsum('tge,tg->te', le, g_hot)
    top_v, top_i = lax.top_k(le, TOP_K_IN_GROUP)
    w_sel = jax.nn.softmax(top_v, -1)
    gate_e = jnp.sum(jax.nn.one_hot(top_i, EXPERTS_PER_GROUP, dtype=jnp.float32) * w_sel[..., None], 1)
    gate = (g_hot[:, :, None] * (p_top * gate_e)[:, None, :]).astype(x.dtype)
    y = jnp.zeros_like(t)
    for g in range(N_GROUPS):
        h = jax.nn.silu(jnp.einsum('td,edf->tef', t, w_gate[g])) * jnp.einsum('td,edf->tef', t, w_up[g])
        y = y + jnp.einsum('tef,efd->td', h * gate[:, g, :, None], w_down[g])
    return y.reshape(B, S, D)

def second_inputs(seed: int = 0) -> dict:
    key = jax.random.key(seed)
    ks = jax.random.split(key, 20)

    def nrm(k, shape, scale):
        return jax.random.normal(k, shape, jnp.float32) * scale

    x = nrm(ks[0], (BATCH, SEQ, D_MODEL), 1.0)
    positions = (jax.random.randint(ks[1], (BATCH, 1), 0, 4096, dtype=jnp.int32)
                 + jnp.arange(SEQ, dtype=jnp.int32)[None, :])
    G, E, F = N_GROUPS, EXPERTS_PER_GROUP, EXPERT_HIDDEN
    return {
        "x": x,
        "positions": positions,
        "w_in": nrm(ks[2], (DEPTH, D_MODEL, IN_COLS_2), D_MODEL ** -0.5),
        "mla_q_norm": 1.0 + nrm(ks[3], (DEPTH, MLA_Q_RANK), 0.02),
        "mla_kv_norm": 1.0 + nrm(ks[4], (DEPTH, MLA_KV_RANK), 0.02),
        "mla_w_uq": nrm(ks[5], (DEPTH, MLA_Q_RANK, MLA_HEADS * (MLA_NOPE + MLA_ROPE)), MLA_Q_RANK ** -0.5),
        "mla_w_ukv": nrm(ks[6], (DEPTH, MLA_KV_RANK, MLA_HEADS * (MLA_NOPE + MLA_V)), MLA_KV_RANK ** -0.5),
        "w_o": nrm(ks[7], (DEPTH, MIX_WIDTH, D_MODEL), MIX_WIDTH ** -0.5 * DEEPNORM_BETA),
        "ln1_g": 1.0 + nrm(ks[8], (DEPTH, D_MODEL), 0.02),
        "ln1_b": nrm(ks[9], (DEPTH, D_MODEL), 0.02),
        "router_group_w": nrm(ks[10], (DEPTH, D_MODEL, G), D_MODEL ** -0.5),
        "router_group_b": nrm(ks[11], (DEPTH, G), 0.01),
        "router_expert_w": nrm(ks[12], (DEPTH, G, D_MODEL, E), D_MODEL ** -0.5),
        "router_expert_b": nrm(ks[13], (DEPTH, G, E), 0.01),
        "expert_w_gate": nrm(ks[14], (DEPTH, G, E, D_MODEL, F), D_MODEL ** -0.5),
        "expert_w_up": nrm(ks[15], (DEPTH, G, E, D_MODEL, F), D_MODEL ** -0.5),
        "expert_w_down": nrm(ks[16], (DEPTH, G, E, F, D_MODEL), F ** -0.5 * DEEPNORM_BETA),
        "ln2_g": 1.0 + nrm(ks[17], (DEPTH, D_MODEL), 0.02),
        "ln2_b": nrm(ks[18], (DEPTH, D_MODEL), 0.02),
    }

def second_block(x, positions, w_in, mla_q_norm, mla_kv_norm, mla_w_uq, mla_w_ukv, w_o, ln1_g, ln1_b,
              router_group_w, router_group_b, router_expert_w, router_expert_b,
              expert_w_gate, expert_w_up, expert_w_down, ln2_g, ln2_b):
    tabs = (rope_table(positions, MLA_ROPE),
            rope_table(positions, ROT_HEAD_DIMS),
            rope_table(positions, ROT_IDX_DIMS))
    for l in range(DEPTH):
        mix = hybrid_mixer(x, tabs, w_in[l], mla_q_norm[l], mla_kv_norm[l], mla_w_uq[l], mla_w_ukv[l], w_o[l])
        x = layer_norm(DEEPNORM_ALPHA * x + mix, ln1_g[l], ln1_b[l])
        moe = hier_moe(x, router_group_w[l], router_group_b[l], router_expert_w[l], router_expert_b[l],
                       expert_w_gate[l], expert_w_up[l], expert_w_down[l])
        x = layer_norm(DEEPNORM_ALPHA * x + moe, ln2_g[l], ln2_b[l])
    return x


def setup_inputs(seed=0):
    out = dict(first_inputs(seed))
    for name, value in second_inputs(seed + 1).items():
        if name != "x":
            out[name + "_2"] = value
    return out


def reference(
    x, norm_mix, w_in, w_ret_o, w_sb_o, w_out, norm_ffn, w_gate_up, w_down, norm_final,
    positions_2, w_in_2, mla_q_norm_2, mla_kv_norm_2, mla_w_uq_2, mla_w_ukv_2, w_o_2, ln1_g_2,
    ln1_b_2, router_group_w_2, router_group_b_2, router_expert_w_2, router_expert_b_2,
    expert_w_gate_2, expert_w_up_2, expert_w_down_2, ln2_g_2, ln2_b_2,
):
    x = first_block(
        x, norm_mix, w_in, w_ret_o, w_sb_o, w_out, norm_ffn, w_gate_up, w_down, norm_final,
    )
    return second_block(
        x, positions_2, w_in_2, mla_q_norm_2, mla_kv_norm_2, mla_w_uq_2, mla_w_ukv_2, w_o_2,
        ln1_g_2, ln1_b_2, router_group_w_2, router_group_b_2, router_expert_w_2,
        router_expert_b_2, expert_w_gate_2, expert_w_up_2, expert_w_down_2, ln2_g_2, ln2_b_2,
    )


_drawn_inputs = setup_inputs


def setup_inputs(seed=0):
    import zlib

    import numpy as np

    out = dict(_drawn_inputs(seed))
    spreads = {}
    factors = {'mla_q_norm_2': 8.0,
     'mla_kv_norm_2': 7.293,
     'router_group_b_2': 7.055,
     'router_expert_b_2': 6.209}
    for name, (base, spread) in spreads.items():
        noise = np.random.default_rng([zlib.crc32(name.encode()), seed]).standard_normal(out[name].shape)
        drawn = base * np.exp(spread * noise) if base else spread * noise
        out[name] = __import__('jax').numpy.asarray(drawn.astype(out[name].dtype))
    for name, factor in factors.items():
        out[name] = (out[name] * factor).astype(out[name].dtype)
    return out
```

```python
from contextlib import ExitStack

import concourse.bass as bass
import numpy as np
from concourse import mybir

F32 = mybir.dt.float32
I32 = mybir.dt.int32
U32 = mybir.dt.uint32
ALU = mybir.AluOpType
ACT = mybir.ActivationFunctionType
AX_X = mybir.AxisListType.X

P = 128
LAYERS = 2
SEQ = 256
TT = SEQ // P
D = 1024
KT = D // P
BANKS = 8
RING = 6
UNIT = 2048
EPS = 1e-6
LN_EPS = 1e-5

HR, DK, DV = 4, 128, 256
HS, DS = 8, 64
FF = 2816
PAIRS = FF // (2 * P)
IN_COLS = 6656
CHUNK = 512
CHUNKS = [("rq", 0), ("rk", 512), ("sq", 3072), ("sk", 3584), ("rv0", 1024), ("rv1", 1536), ("sv", 4096),
          ("rg0", 2048), ("rg1", 2560), ("gr0", 4608), ("gr1", 5120), ("gs0", 5632), ("gs1", 6144)]
TRI = SEQ + P


HM, NOPE, ROPE, VM = 8, 64, 32, 64
QR, KVR = 256, 128
HD = 64
HI, DI = 8, 32
HX = 4
TOP_K = 64
DILATED = ((128, 1), (512, 4), (2048, 16))
GROUPS, EXPERTS, EH = 4, 8, 256
ALPHA = (2.0 * LAYERS) ** 0.25
FAR = -1e30
TAKEN = -3e38
UCOLS = 3400
CHUNKS2 = [("C", 800, 296), ("A", 0, 416), ("B", 416, 384), ("q0", 1096, 384), ("q1", 1480, 384),
           ("k0", 1864, 384), ("k1", 2248, 384), ("v0", 2632, 384), ("v1", 3016, 384)]
COL2 = {name: (at, width) for name, at, width in CHUNKS2}
BY_ACT = ("C", "B", "q1", "k1", "v1")
JOBS = HM + HX + HX
ROT = {"mla": (0, 16), "head": (32, 8), "idx": (48, 4)}
ROT_COLS = 56
MAGIC = 1.5 * 2.0 ** 23


class Turns:

    def __init__(self, seq, after=None):
        self.start = {} if after is None else {r: after.end(r) for r in set(after.start) | set(after.per)}
        self.per, self.place = {}, {}
        for key, r in seq:
            self.place[key] = (r, self.per.get(r, 0))
            self.per[r] = self.per.get(r, 0) + 1

    def end(self, r):
        return self.start.get(r, 0) + LAYERS * self.per.get(r, 0)

    def __getitem__(self, key):
        return self.place[key][0]

    def before(self, key, layer, more=0):
        r, n = self.place[key]
        return layer * self.per[r] + (self.start.get(r, 0) + n) + more

    def stride(self, key, later):
        assert self.place[key][0] == self.place[later][0]
        return self.place[later][1] - self.place[key][1]


class Signal:

    def __init__(self, sem, per, start=0):
        self.sem, self.per, self.start = sem, per, start

    def at(self, layer, k):
        return layer * self.per + (self.start + k)


def mixer_banks():
    seq = [("nT", kp) for kp in range(4)]
    for c in ("rq", "rk"):
        seq += [(c, t) for t in range(TT)]
    seq += [("sq", 0), ("sq", 1), ("sk", 0), ("sk", 1), ("rv0", 0), ("rv0", 1)]
    seq += [("qT", 0), ("qT", 1), ("kT", 0), ("kT", 1), ("rv1", 0), ("rv1", 1)]
    seq += [("rs", h) for h in range(HR)] + [("z", h) for h in range(HS)] + [("sv", 0), ("sv", 1)]
    seq += [("rg0", 0), ("rg0", 1)] + [("ro", h) for h in range(HR)] + [("rg1", 0), ("rg1", 1)]
    seq += [("c", h) for h in range(HS)] + [("gr0", 0), ("gr0", 1), ("gr1", 0), ("gr1", 1)]
    seq += [("so", h) for h in range(HS // 2)] + [("gs0", 0), ("gs0", 1), ("gs1", 0), ("gs1", 1)]
    seq += [("rT", kp) for kp in range(4)] + [("ret", i) for i in range(4)] + [("sb", i) for i in range(4)]
    seq += [("mT", kp) for kp in range(4)] + [("wo", i) for i in range(4)]
    out = [(key, n % BANKS) for n, key in enumerate(seq)]
    out += [(("nT2", kp), 4 + kp) for kp in range(4)]
    out += [(("ffn", i), i) for i in range(4)]
    out += [(("gu", i), 4 + i % 4) for i in range(2 * PAIRS)]
    return Turns(out)


def mixer_units():
    seq = [(c, half) for c, _ in CHUNKS for half in range(2)]
    seq += [("w_ret_o", u) for u in range(4)] + [("w_sb_o", u) for u in range(2)] + [("w_out", u) for u in range(4)]
    for p in range(PAIRS):
        seq += [("gate", p), ("up", p), ("down", p)]
    return Turns([(key, n % RING) for n, key in enumerate(seq)])


def attention_banks(after):
    seq = [("xT", kp) for kp in range(4)]
    for c in ("C", "A", "B", "q0"):
        seq += [(c, t) for t in range(TT)]
    seq += [("qiT", 0), ("kkT", 0), ("cT", 0), ("cT", 1), ("q1", 0), ("q1", 1)]
    seq += [("rel", h) for h in range(HI)]
    seq += [("uq", i) for i in range(4)] + [("ukv", i) for i in range(4)]
    seq += [("k0", 0), ("k0", 1), ("k1", 0), ("k1", 1), ("v0", 0), ("v0", 1)]
    seq += [("mqT", b) for b in range(4)] + [("mkT", b) for b in range(4)]
    seq += [("v1", 0), ("v1", 1), ("dsT", 0)] + [("dqT", b) for b in range(3)] + [("dkT", b) for b in range(3)]
    out = [(key, n % BANKS) for n, key in enumerate(seq)]
    out += [(("O", i), i) for i in range(4)]
    n = 0
    for j in range(JOBS + 1):
        for what, i in (("S", j), ("E", j - 1)):
            for part in range(parts(i)):
                out.append(((what, i, part), 4 + n % 4))
                n += 1
    out += [(("oT", kp), 4 + kp) for kp in range(4)] + [(("wo", i), i) for i in range(4)]
    out += [(("xT2", kp), 4 + kp) for kp in range(4)] + [(("router", 0), 0), (("ranks", 0), 1)]
    for pass_ in range(2):
        out += [(("pT", pass_, 0), 2), (("pT", pass_, 1), 3), (("slots", pass_), 1)]
        for g in range(GROUPS):
            out += [(("xg", pass_, g, b), 2 + b) for b in range(2)]
            for e in range(EXPERTS):
                out += [(("gu", pass_, g, e), 4 + e % 2), (("hT", pass_, g, e), 6 + e % 2)]
            out += [(("yg", pass_, g, half), half) for half in range(2)]
        out += [(("sc", pass_, i), i) for i in range(4)]
    return Turns(out, after)


def parts(j):
    return 0 if not 0 <= j < JOBS else 3 if j >= HM + HX else 1


def attention_units(after):
    order = ["C", "A", "B", "q0", "q1", "uq", "ukv", "k0", "k1", "v0", "v1"]
    seq = [(c, half) for c in order for half in range(1 if c in ("uq", "ukv") else 2)]
    seq += [("w_o_2", u) for u in range(4)]
    assert len(seq) % RING == 0
    for pass_ in range(2):
        for g in range(GROUPS):
            for e in range(EXPERTS):
                seq += [(w, pass_, g, e) for w in ("gate", "up", "down")]
    return Turns([(key, n % RING) for n, key in enumerate(seq)], after)


def constants():
    i = np.arange(P)
    pos = np.arange(SEQ, dtype=np.float32)
    half = DK // 2
    inv = (1.0 / (np.float32(10000.0) ** (np.arange(half, dtype=np.float32) / np.float32(half)))).astype(np.float32)
    ang = (pos[:, None] * inv[None, :]).astype(np.float32)
    cos, sin = np.cos(ang).astype(np.float32), np.sin(ang).astype(np.float32)
    rope = np.concatenate([cos, cos, -sin, sin], 1).reshape(TT, P, 4 * half).transpose(1, 0, 2)
    log_g = np.log1p(-np.exp2(-5.0 - np.arange(HR)))
    decay = np.zeros((P, HR, TRI))
    for h in range(HR):
        for j0, i0, n, at in ((0, 0, SEQ, 0), (P, P, P, SEQ)):
            diff = (i0 + np.arange(n))[None, :] - (j0 + i)[:, None]
            decay[:, h, at:at + n] = np.where(diff >= 0, np.exp(log_g[h] * np.maximum(diff, 0)), 0.0) * DK ** -0.5
    f = lambda a: np.ascontiguousarray(a, np.float32)
    freq, sign = [], []
    for _, half in ROT.values():
        f_ = 500000.0 ** (-np.arange(0, 2 * half, 2) / (2.0 * half))
        freq += [f_, f_]
        sign += [-np.ones(half), np.ones(half)]
    q, k = np.arange(SEQ)[:, None], np.arange(SEQ)[None, :]
    causal = np.where(k <= q, 0.0, FAR)
    near = [np.where((q >= k) & ((q - k) % d == 0) & (q - k <= w), 0.0, FAR) for w, d in DILATED]
    return {
        "c_freq": np.tile(np.concatenate(freq).astype(np.float32), (P, 1)),
        "c_sign": f(np.tile(np.concatenate(sign), (P, 1))),
        "c_causal": f(np.concatenate([causal[:P, :P], causal[P:, :]], 1)),
        "c_near": f(np.concatenate([m[P:, :] for m in near] + [m[:P, :P] for m in near], 1)),
        "c_before": f(i[:, None] < i[None, :]),
        "c_iota": f(np.tile(i, (P, 1))),
        "c_ident": f(np.eye(P)),
        "c_suffix": f(i[:, None] >= i[None, :]),
        "c_rope": f(rope),
        "c_decay": f(decay),
    }


def build(nc, src, out, debug=None):
    banks = mixer_banks()
    units = mixer_units()
    banks2 = attention_banks(banks)
    units2 = attention_units(units)
    ctx = ExitStack()
    with ctx:
        def sb(name, shape, dt=F32):
            return ctx.enter_context(nc.sbuf_tensor(name, shape, dt))

        def sem(name):
            return ctx.enter_context(nc.semaphore(name))

        def signal(name, per, start=0):
            return Signal(sem(name), per, start)

        ps = ctx.enter_context(nc.psum_tensor("ps", [P, BANKS, 512], F32))
        ring = sb("ring", [P, RING, UNIT])
        ident = sb("ident", [P, P])
        suffix = sb("suffix", [P, P])
        ones = sb("ones", [P, P])
        minus_half = sb("minus_half", [P, 4])
        lstat = sb("lstat", [P, 3, 4])
        H = sb("H", [P, TT, D])
        xn = sb("xn", [P, TT, D])
        T8 = sb("T8", [P, KT, SEQ])
        gains = sb("gains", [P, 2, KT])
        stat = sb("stat", [P, 8])
        freq = sb("freq", [P, 2, ROT_COLS])
        pos_i = sb("pos_i", [P, TT], I32)
        pos = sb("pos", [P, TT])
        rope2 = sb("rope2", [P, 2, TT, ROT_COLS])
        turns_ = sb("turns", [P, 3, TT, ROT_COLS])
        rotation = [rope2[:, i] for i in range(2)]
        arena = sb("arena", [P, ARENA])

        def carver():
            at = [0]

            def carve(*shape):
                n = int(np.prod(shape))
                view = arena[:, at[0]:at[0] + n]
                at[0] += n
                assert at[0] <= ARENA, at[0]
                names = "abc"[:len(shape)]
                if len(shape) == 1:
                    return view
                return view.rearrange(f"p ({' '.join(names)}) -> p {' '.join(names)}",
                                      **{names[i]: shape[i] for i in range(len(shape))})
            return carve, at

        carve, _ = carver()
        gfinal = carve(D)
        rope1 = carve(TT, 256)
        decay = carve(HR, TRI)
        qk_flat = carve(4 * 512)
        qk = qk_flat.rearrange("p (a t n) -> p a t n", a=2, t=TT)
        retn = qk_flat.rearrange("p (t n) -> p t n", t=TT)
        rot = carve(2, 512)
        qT = carve(HR, SEQ)
        kT = carve(HR, SEQ)
        rv = carve(TT, D)
        sqT = carve(HS // 2, SEQ)
        skT = carve(HS // 2, SEQ)
        sv = carve(TT, HS * DS)
        rg = carve(TT, D)
        gr = carve(TT, D)
        gs = carve(TT, D)
        ST = carve(HR, TRI)
        z = carve(HS, TRI)
        sp = carve(HS, TRI)
        lnt = carve(2, TRI)
        moments_flat = carve(HR * TT * 6)
        moments = moments_flat.rearrange("p (h t n) -> p h t n", h=HR, t=TT)
        mv_flat = carve(HR * TT * 2)
        mv = mv_flat.rearrange("p (h t n) -> p h t n", h=HR, t=TT)
        rstd = carve(HR, TT)
        retT = carve(KT, SEQ)
        sbT = carve(HS // 2, SEQ)
        silu_g = retT[:, 0:4, :]
        guT = retT[:, 4:8, :]

        carve, arena_at = carver()
        lng = carve(4, D)
        cgain = carve(4)
        rw = carve(KT, GROUPS + GROUPS * EXPERTS)
        rb = carve(GROUPS + GROUPS * EXPERTS)
        causal_m = carve(TRI)
        near_m = carve(3 * TRI)
        before = carve(P)
        iota = carve(P)
        moments2_flat = carve(TT * 2 * 6)
        moments2 = moments2_flat.rearrange("p (t a n) -> p t a n", t=TT, a=2)
        mv2 = carve(TT, 2)
        rstd2 = carve(TT)
        moe_at = arena_at[0]
        U = carve(TT, UCOLS)
        mqk = carve(2 * TT * HM * (NOPE + ROPE))
        mq, mk = (mqk[:, i * 1536:(i + 1) * 1536].rearrange("p (t n) -> p t n", t=TT) for i in range(2))
        mvv = carve(TT, HM * VM)
        cT = carve(3, SEQ)
        mqT = carve(HM, SEQ)
        mkT = carve(HM, SEQ)
        dqT = carve(6, SEQ)
        dkT = carve(6, SEQ)
        dsT = carve(2, SEQ)
        kkT = carve(2, SEQ)
        qiT = carve(2, SEQ)
        before_jobs = carve(2 * 256 + 2 * 768 + 2 * TRI)
        kk = before_jobs[:, 0:256].rearrange("p (t n) -> p t n", t=TT)
        ki4 = before_jobs[:, 256:512].rearrange("p (t n) -> p t n", t=TT)
        ra = before_jobs[:, 512:1280]
        rbuf = before_jobs[:, 1280:2048]
        relu = before_jobs[:, 2048:2816].rearrange("p (a n) -> p a n", a=2)
        score = carve(TRI)
        nm = carve(TRI)
        best = carve(TT, 8)
        S = mqk[:, 0:6 * TRI].rearrange("p (a n) -> p a n", a=2)
        ET = before_jobs[:, 0:6 * TRI].rearrange("p (a n) -> p a n", a=2)
        nmx = carve(JOBS, 4)
        lsum = carve(JOBS, TT)
        rinv = carve(JOBS, TT)

        arena_at[0] = moe_at
        logit = carve(TT, 36)
        hot_max = carve(TT)
        shifted = carve(TT, GROUPS)
        eq = carve(TT, GROUPS)
        prefix = carve(TT, GROUPS)
        hot = carve(TT, GROUPS)
        gexp = carve(TT, GROUPS)
        ptop = carve(4, TT)
        sel_flat = carve(TT * EXPERTS * GROUPS)
        sel4 = sel_flat.rearrange("p (t e g) -> p t e g", t=TT, e=EXPERTS)
        sel = carve(TT, EXPERTS)
        top = carve(TT, 8)
        topi = carve(TT, 8).bitcast(U32)
        topf = carve(TT, 8)
        diff = carve(3, TT)
        ge = carve(TT, EXPERTS)
        ge2 = carve(TT, EXPERTS)
        gate_flat = carve(TT * GROUPS * EXPERTS)
        gate = gate_flat.rearrange("p (t g e) -> p t g e", t=TT, g=GROUPS)
        crank = carve(TT, GROUPS)
        rank = carve(TT)
        npass_f = carve(2)
        npass = carve(1).bitcast(I32)
        pick_flat = carve(GROUPS * TT * P)
        pick = pick_flat.rearrange("p (g t n) -> p g t n", g=GROUPS, t=TT)
        pickT = carve(GROUPS, SEQ)
        gslot = carve(GROUPS * EXPERTS)
        XG = carve(KT, P)
        sg = carve(2, EH)
        hh = carve(2, EH)
        hT = carve(2, 2 * P)
        YG = carve(GROUPS, D)

        filled = [sem(f"filled{b}") for b in range(BANKS)]
        landed = [sem(f"landed{s}") for s in range(RING)]
        unit_read = signal("unit_read", 3 + 1 + 3 + PAIRS - 1)
        const_in = sem("const_in")
        x_in = sem("x_in")
        out_done = sem("out_done")
        const_set = sem("const_set")
        dve_step = sem("dve_step")
        act_step = sem("act_step")
        pool_step = sem("pool_step")
        h_added = signal("h_added", 8, 1)
        sumsq = signal("sumsq", 4)
        gains_in = signal("gains_in", 32)
        meansq = signal("meansq", 2)
        rms = signal("rms", 2)
        xn_done = signal("xn_done", 4)
        nT_act = signal("nT_act", 8)
        nT_dve = signal("nT_dve", 8)
        rotated = signal("rotated", 4)
        roped = signal("roped", 4)
        qT_in = signal("qT_in", 2)
        kT_in = signal("kT_in", 2)
        sqk_in = signal("sqk_in", 4)
        rv_in = signal("rv_in", 4)
        sv_in = signal("sv_in", 2)
        st_in = signal("st_in", HR)
        z_in = signal("z_in", HS)
        negabs = signal("negabs", HS)
        ln_done = signal("ln_done", HS)
        sp_done = signal("sp_done", HS)
        sp_masked = signal("sp_masked", HS)
        logw = signal("logw", HS)
        w_exp = signal("w_exp", HS)
        w_masked = signal("w_masked", HS)
        sbT_in = signal("sbT_in", HS // 2)
        rg_in = signal("rg_in", 4)
        gr_in = signal("gr_in", 4)
        gs_in = signal("gs_in", 4)
        rg_silu = signal("rg_silu", 2)
        gates = signal("gates", 4)
        head_var = signal("head_var", HR)
        head_rstd = signal("head_rstd", HR)
        ret_normed = signal("ret_normed", HR)
        ret_gated = signal("ret_gated", 2)
        rT_act = signal("rT_act", 2)
        rT_dve = signal("rT_dve", 2)
        ret_out = signal("ret_out", 4)
        sb_gated = signal("sb_gated", 4)
        merged = signal("merged", 4)
        mT_act = signal("mT_act", 2)
        mT_dve = signal("mT_dve", 2)
        g_silu = signal("g_silu", 2 * PAIRS)
        gu_done = signal("gu_done", 2 * PAIRS)

        unit_read2 = signal("unit_read2", 3 + 2 * GROUPS * (EXPERTS - 1))
        x_ready = signal("x_ready", 4, TT)
        table_step = sem("table_step")
        passed = sem("passed")
        ln_step = sem("ln_step")
        table_done = sem("table_done")
        params_in = signal("params_in", 16 * N_PARAMS)
        bT_act = signal("bT_act", 6)
        bT_dve = signal("bT_dve", 6)
        u_act = signal("u_act", 10)
        u_dve = signal("u_dve", 8)
        latent_sq = signal("latent_sq", 4)
        latent_ms = signal("latent_ms", 1)
        latent_rms = signal("latent_rms", 1)
        latent_done = signal("latent_done", 1)
        r_mul = signal("r_mul", 5)
        r_add = signal("r_add", 5)
        kcopy = signal("kcopy", 3)
        wi_done = signal("wi_done", 1)
        qiT_in = signal("qiT_in", 1)
        kkT_in = signal("kkT_in", 1)
        cT_in = signal("cT_in", 3)
        relu_in = signal("relu_in", HI)
        score_in = signal("score_in", HI)
        score_masked = signal("score_masked", 1)
        topk_done = signal("topk_done", 1)
        nm_masked = signal("nm_masked", 1)
        mq_in = signal("mq_in", 4)
        mk_in = signal("mk_in", 4)
        mqT_in = signal("mqT_in", 4)
        mkT_in = signal("mkT_in", 4)
        dsT_in = signal("dsT_in", 1)
        dqT_in = signal("dqT_in", 3)
        dkT_in = signal("dkT_in", 3)
        masked = signal("masked", JOBS * 3)
        weighed = signal("weighed", JOBS)
        ET_dve = signal("ET_dve", HM + HX + 2 * HX)
        ET_act = signal("ET_act", HX)
        mix_done = signal("mix_done", 4)
        stat_done = signal("stat_done", 2)
        rstd_done = signal("rstd_done", 2)
        gained = signal("gained", 4)
        wo_in = signal("wo_in", 4)
        logit_in = signal("logit_in", 1)
        hot_done = signal("hot_done", 1)
        shift_done = signal("shift_done", 1)
        gexp_done = signal("gexp_done", 1)
        diff_done = signal("diff_done", 1)
        eexp_done = signal("eexp_done", 1)
        rank_ready = signal("rank_ready", 3)
        npass_done = signal("npass_done", 1)
        resid_in = signal("resid_in", TT)
        pick_done = signal("pick_done", 1)
        pickT_in = signal("pickT_in", 2)
        gslot_in = signal("gslot_in", 1)
        xg_act = signal("xg_act", GROUPS)
        xg_dve = signal("xg_dve", GROUPS)
        g2_silu = signal("g2_silu", GROUPS * EXPERTS)
        h2_done = signal("h2_done", GROUPS * EXPERTS)
        hT_in = signal("hT_in", GROUPS * EXPERTS)
        yg_in = signal("yg_in", 2 * GROUPS, 1)
        sc_added = signal("sc_added", 4)

        def wait_apart(eng, semaphore, count):
            eng.wait_ge(semaphore, count)
            eng.sem_inc(passed, 1)

        def bank_of(key):
            return ps[:, banks[key], :]

        def bank2(key):
            return ps[:, banks2[key], :]


        bank_read = {}
        for kp in range(4):
            bank_read["nT", kp] = ((nT_act, nT_dve)[kp % 2], kp // 2 * 2 + 2)
            bank_read["nT2", kp] = ((nT_act, nT_dve)[kp % 2], 4 + kp // 2 * 2 + 2)
            bank_read["rT", kp] = ((rT_act, rT_dve)[kp % 2], kp // 2 + 1)
            bank_read["mT", kp] = ((mT_act, mT_dve)[kp % 2], kp // 2 + 1)
            bank_read["ret", kp] = (ret_out, kp + 1)
            bank_read["sb", kp] = (sb_gated, kp + 1)
            bank_read["wo", kp] = (h_added, kp + 1)
            bank_read["ffn", kp] = (h_added, 4 + kp + 1)
        for t in range(TT):
            for name, signal_, k in (("rq", rotated, 0), ("rk", rotated, 2), ("sq", sqk_in, 0), ("sk", sqk_in, 2),
                                     ("rv0", rv_in, 0), ("rv1", rv_in, 2), ("qT", qT_in, 0), ("kT", kT_in, 0),
                                     ("sv", sv_in, 0), ("rg0", rg_in, 0), ("rg1", rg_in, 2), ("gr0", gr_in, 0),
                                     ("gr1", gr_in, 2), ("gs0", gs_in, 0), ("gs1", gs_in, 2)):
                bank_read[name, t] = (signal_, k + t + 1)
        for h in range(HS):
            bank_read["z", h] = (z_in, h + 1)
            bank_read["c", h] = (logw, h + 1)
        for h in range(HR):
            bank_read["rs", h] = (st_in, h + 1)
            bank_read["ro", h] = (ret_normed, h + 1)
            bank_read["so", h] = (sbT_in, h + 1)
        for i in range(2 * PAIRS):
            bank_read["gu", i] = (gu_done, i + 1)

        read2 = {}
        for kp in range(4):
            for n, name in enumerate(("xT", "oT", "xT2")):
                read2[name, kp] = ((bT_act, bT_dve)[kp % 2], 2 * n + kp // 2 + 1)
            read2["uq", kp] = (mq_in, kp + 1)
            read2["ukv", kp] = (mk_in, kp + 1)
            read2["mqT", kp] = (mqT_in, kp + 1)
            read2["mkT", kp] = (mkT_in, kp + 1)
            read2["wo", kp] = (wo_in, kp + 1)
            read2["O", kp] = (mix_done, kp + 1)
        for by, signal_ in ((BY_ACT, u_act), ([c for c, _, _ in CHUNKS2 if c not in BY_ACT], u_dve)):
            for n, name in enumerate(by):
                for t in range(TT):
                    read2[name, t] = (signal_, 2 * n + t + 1)
        for b in range(3):
            read2["dqT", b] = (dqT_in, b + 1)
            read2["dkT", b] = (dkT_in, b + 1)
        read2["qiT", 0], read2["kkT", 0], read2["dsT", 0] = (qiT_in, 1), (kkT_in, 1), (dsT_in, 1)
        read2["cT", 0], read2["cT", 1] = (cT_in, 2), (cT_in, 3)
        for h in range(HI):
            read2["rel", h] = (relu_in, h + 1)
        for j in range(JOBS):
            for part in range(parts(j)):
                read2["S", j, part] = (masked, 3 * j + 3 if part == parts(j) - 1 else 3 * j + part + 1)
                if j < HM + HX:
                    read2["E", j, part] = (ET_dve, j + 1)
                elif part == 0:
                    read2["E", j, part] = (ET_act, j - HM - HX + 1)
                else:
                    read2["E", j, part] = (ET_dve, HM + HX + 2 * (j - HM - HX) + part)
        read2["router", 0], read2["ranks", 0] = (logit_in, 1), (npass_done, 1)

        def held_before(plan, key):
            bank, n = plan.place[key]
            return next((k for k, at in plan.place.items() if at == (bank, n - 1)), None)

        units_group = units2.stride(("gate", 0, 0, 0), ("gate", 0, 1, 0))
        units_pass = units2.stride(("gate", 0, 0, 0), ("gate", 1, 0, 0))

        def pass_turn(name, key, l, pass_, g):
            first = (name, 0) + key
            more = pass_ * banks2.stride(first, (name, 1) + key)
            if name in ("xg", "gu", "hT", "yg"):
                more = more + g * banks2.stride(first, (name, 0, 1) + key[1:])
            return banks2.before(first, l) + more

        block = ctx.enter_context(nc.Block())

        @block.sync
        def _(sp_):
            col = dict(CHUNKS)

            def source(key, l):
                name, u = key
                if name in col:
                    w = src["w_in"].rearrange("l (p k) n -> (l p) k n", k=KT)
                    return w[l * P:(l + 1) * P, 4 * u:4 * u + 4, col[name]:col[name] + CHUNK]
                if name in ("gate", "up"):
                    w = src["w_gate_up"].rearrange("l (p k) n -> (l p) k n", k=KT)
                    first = (name == "up") * FF
                    return w[l * P:(l + 1) * P, :, bass.ds(u * 256 + first, 256)]
                if name == "down":
                    w = src["w_down"].rearrange("l (k p) n -> (l k) p n", p=P)
                    return w[bass.ds(u * 2 + l * (FF // P), 2)].rearrange("k p n -> p k n")
                w = src[name].rearrange("l (k p) n -> (l k) p n", p=P)
                n = src[name].shape[1] // P
                return w[l * n + 2 * u:l * n + 2 * u + 2].rearrange("k p n -> p k n")

            def into(key):
                shape = {"gate": (8, 256), "up": (8, 256), "down": (2, 1024)}.get(
                    key[0], (4, 512) if key[0] in col else (2, 1024))
                return ring[:, units[key], :].rearrange("p (k n) -> p k n", k=shape[0])

            reads = {k: n for n, k in enumerate([("w_ret_o", 0), ("w_ret_o", 1), ("w_ret_o", 2), ("w_sb_o", 0),
                                                 ("w_out", 0), ("w_out", 1), ("w_out", 2)])}
            last_fill = {"sq": ("sq", 1), "sk": ("sk", 1)}

            def wait_released(key, l, more=0, step=0):
                name, u = key
                if key in reads:
                    sp_.wait_ge(unit_read.sem, unit_read.at(l, reads[key] + 1))
                elif name == "down" and u < PAIRS - 1:
                    sp_.wait_ge(unit_read.sem, unit_read.at(l, len(reads) + u + 1) + more)
                else:
                    if name in ("gate", "up"):
                        fill = ("gu", 2 * u + 1)
                    elif name == "down":
                        fill = ("ffn", 3)
                    elif name in ("w_ret_o", "w_sb_o", "w_out"):
                        fill = ({"w_ret_o": "ret", "w_sb_o": "sb", "w_out": "wo"}[name], 3)
                    else:
                        fill = (name, 1)
                    sp_.wait_ge(filled[banks[fill]], banks.before(fill, l) + 1 + step)

            def on_all(row):
                return row.rearrange("(a d) -> a d", a=1).to_broadcast([P, row.shape[0]])

            sp_.dma_start(H[:], src["x"].rearrange("b (t p) d -> (b p) t d", p=P)).then_inc(x_in, 16)
            small = [(ident[:], src["c_ident"]), (suffix[:], src["c_suffix"]), (rope1, src["c_rope"]),
                     (decay, src["c_decay"])]
            small += [(freq[:, 0, :], src["c_freq"]), (freq[:, 1, :], src["c_sign"]),
                      (pos_i[:], src["positions_2"].rearrange("b (t p) -> p (b t)", p=P))]
            small += [(gfinal, on_all(src["norm_final"]))]
            order = list(units.place)
            for key in order[:2]:
                sp_.dma_start(into(key), source(key, 0)).then_inc(landed[units[key]], 16)
            for to, of in small:
                sp_.dma_start(to, of, allow_slow_non_contiguous=True).then_inc(const_in, 16)

            for l in range(LAYERS):
                if l > 0:
                    sp_.wait_ge(nT_act.sem, nT_act.at(l, 0))
                    sp_.wait_ge(nT_dve.sem, nT_dve.at(l, 0))
                for w, g in enumerate(("norm_mix", "norm_ffn")):
                    sp_.dma_start(gains[:, w, :], src[g][l].rearrange("(p k) -> p k", k=KT)).then_inc(gains_in.sem, 16)
                for n, key in enumerate(order):
                    if l == 0 and n < 2:
                        continue
                    slot = units[key]
                    if n >= RING:
                        wait_released(order[n - RING], l)
                    elif l > 0:
                        prev = [k for k in order if units[k] == slot][-1]
                        wait_released(prev, l - 1)
                    sp_.dma_start(into(key), source(key, l)).then_inc(landed[slot], 16)

            def params(l):
                yield cgain[:, 0:2], src["mla_q_norm_2"][l].rearrange("(k p) -> p k", p=P)
                yield cgain[:, 2:3], src["mla_kv_norm_2"][l].rearrange("(k p) -> p k", p=P)
                for n, name in enumerate(("ln1_g_2", "ln1_b_2", "ln2_g_2", "ln2_b_2")):
                    yield lng[:, n, :], on_all(src[name][l])
                yield rw[:, :, 0:GROUPS], src["router_group_w_2"][l].rearrange("(p k) g -> p k g", k=KT)
                yield rb[:, 0:GROUPS], on_all(src["router_group_b_2"][l])
                for g in range(GROUPS):
                    at = GROUPS + g * EXPERTS
                    yield rw[:, :, at:at + EXPERTS], src["router_expert_w_2"][l, g].rearrange("(p k) e -> p k e", k=KT)
                yield rb[:, GROUPS:36], on_all(src["router_expert_b_2"][l].rearrange("g e -> (g e)"))
                yield causal_m, src["c_causal"]
                yield near_m, src["c_near"]
                yield before, src["c_before"]
                yield iota, src["c_iota"]

            def source2(key, l, g=None):
                name = key[0]
                if name in COL2:
                    at, width = COL2[name]
                    w = src["w_in_2"].rearrange("l (p k) n -> (l p) k n", k=KT)
                    return w[l * P:(l + 1) * P, 4 * key[1]:4 * key[1] + 4, at:at + width]
                if name in ("uq", "ukv"):
                    w = src[f"mla_w_{name}_2"]
                    return w[l].rearrange("(k p) n -> p k n", p=P)
                if name == "w_o_2":
                    return src[name][l, 256 * key[1]:256 * (key[1] + 1), :].rearrange("(k p) n -> p k n", p=P)
                w = src[f"expert_w_{name}_2"]
                rows = 8 if name != "down" else 2
                e = key[3]
                w = w.rearrange("l g e (p k) n -> (l g e p) k n", k=rows)
                return w[bass.ds((l * GROUPS * EXPERTS + e) * P + g * (EXPERTS * P), P)]

            def into2(key, width=None):
                name = key[0]
                slot = ring[:, units2[key], :]
                if name in COL2:
                    return slot[:, 0:4 * COL2[name][1]].rearrange("p (k n) -> p k n", k=4)
                if name in ("uq", "ukv"):
                    k = 2 if name == "uq" else 1
                    return slot[:, 0:k * (768 if name == "uq" else 1024)].rearrange("p (k n) -> p k n", k=k)
                return slot.rearrange("p (k n) -> p k n", k=8 if name in ("gate", "up") else 2)

            def wait_released2(key, l, g=0):
                name = key[0]
                if name == "w_o_2" and key[1] < 3:
                    sp_.wait_ge(unit_read2.sem, unit_read2.at(l, key[1] + 1))
                elif name == "down" and key[3] < EXPERTS - 1:
                    pass_, e = key[1], key[3]
                    sp_.wait_ge(unit_read2.sem,
                                unit_read2.at(l, 3 + pass_ * GROUPS * (EXPERTS - 1) + e + 1) + g * (EXPERTS - 1))
                else:
                    if name in ("gate", "up"):
                        fill = ("gu", key[1], 0, key[3])
                        step = banks2.stride(fill, ("gu", key[1], 1, key[3]))
                    elif name == "down":
                        fill = ("yg", key[1], 0, 1)
                        step = banks2.stride(fill, ("yg", key[1], 1, 1))
                    else:
                        fill, step = {"uq": ("uq", 3), "ukv": ("ukv", 3), "w_o_2": ("wo", 3)}.get(name, (name, 1)), 0
                    sp_.wait_ge(filled[banks2[fill]], banks2.before(fill, l) + 1 + g * step)

            dense = [k for k in units2.place if len(k) == 2]
            last_of_first = {units[k]: k for k in order}
            for l in range(LAYERS):
                for n, key in enumerate(dense):
                    slot = units2[key]
                    if n >= RING:
                        wait_released2(dense[n - RING], l)
                    elif l == 0:
                        wait_released(last_of_first[slot], LAYERS - 1)
                    else:
                        e, w = divmod(3 * EXPERTS - RING + slot, 3)
                        wait_released2((("gate", "up", "down")[w], 1, 0, e), l - 1, GROUPS - 1)
                    sp_.dma_start(into2(key), source2(key, l)).then_inc(landed[slot], 16)
                    if n == RING - 1:
                        sp_.wait_ge(x_ready.sem, x_ready.at(l, 0))
                        for to, of in params(l):
                            sp_.dma_start(to, of, allow_slow_non_contiguous=True).then_inc(params_in.sem, 16)
                for pass_ in range(2):
                    kinds = ("gate", "up", "down")
                    held = dense[-RING:] if pass_ == 0 else [
                        (kinds[n % 3], 0, 0, n // 3) for n in range(3 * EXPERTS - RING, 3 * EXPERTS)]

                    def load(n, g):
                        key = (kinds[n % 3], pass_, 0, n // 3)
                        sp_.dma_start(into2(key), source2(key, l, g)).then_inc(landed[units2[key]], 16)

                    def load_rest(g):
                        for n in range(RING, 3 * EXPERTS):
                            wait_released2((kinds[(n - RING) % 3], pass_, 0, (n - RING) // 3), l, g)
                            load(n, g)

                    def expert_loads():
                        for n in range(RING):
                            wait_released2(held[n], l, 0 if pass_ == 0 else GROUPS - 1)
                            load(n, 0)
                        with sp_.Fori(0, GROUPS - 1) as g:
                            load_rest(g)
                            for n in range(RING):
                                m = 3 * EXPERTS - RING + n
                                wait_released2((kinds[m % 3], pass_, 0, m // 3), l, g)
                                load(n, g + 1)
                        load_rest(GROUPS - 1)

                    if pass_ == 0:
                        expert_loads()
                    else:
                        wait_apart(sp_, npass_done.sem, npass_done.at(l, 1))
                        passes = sp_.value_load(npass[0:1, 0:1], min_val=1, max_val=2)
                        with sp_.If(passes > 1):
                            expert_loads()
                        with sp_.Else():
                            for s_ in range(RING):
                                key = dense[s_]
                                sp_.wait_ge(landed[s_], 16 * (units2.before(key, l + 1) - GROUPS * 3 * EXPERTS // RING))
                                sp_.sem_inc(landed[s_], 16 * GROUPS * 3 * EXPERTS // RING)
            sp_.wait_ge(x_ready.sem, x_ready.at(LAYERS, 0))
            sp_.dma_start(out.rearrange("b (t p) d -> (b p) t d", p=P), H[:]).then_inc(out_done, 16)
            sp_.wait_ge(out_done, 16)

        @block.tensor
        def _(pe):
            def claim(key, l, more=0):
                old = held_before(banks, key)
                if old is not None:
                    signal_, k = bank_read[old]
                    pe.wait_ge(signal_.sem, signal_.at(l, k) + more)
                return bank_of(key)

            def weights(key, l, more=0):
                pe.wait_ge(landed[units[key]], (units.before(key, l, more) + 1) * 16)
                shape = {"gate": 8, "up": 8, "down": 2}.get(key[0], 4 if key in chunk_units else 2)
                return ring[:, units[key], :].rearrange("p (k n) -> p k n", k=shape)

            chunk_units = {(c, u) for c, _ in CHUNKS for u in range(2)}

            def project(c, l):
                w = [weights((c, 0), l), weights((c, 1), l)]
                for t in range(TT):
                    acc = claim((c, t), l)
                    for k in range(KT):
                        mm = nc.tensor.matmul(acc, T8[:, k, t * P:(t + 1) * P], w[k // 4][:, k % 4, :],
                                              start=(k == 0), stop=(k == KT - 1))
                    mm.then_inc(filled[banks[(c, t)]], 1)

            def project_turned(c, l):
                w = [weights((c, 0), l), weights((c, 1), l)]
                for b in range(2):
                    acc = claim((c, b), l)
                    for j in range(2):
                        cols = slice((2 * b + j) * P, (2 * b + j + 1) * P)
                        for k in range(KT):
                            mm = nc.tensor.matmul(acc[:, j * SEQ:(j + 1) * SEQ], w[k // 4][:, k % 4, cols],
                                                  T8[:, k, :], start=(k == 0), stop=(k == KT - 1))
                    mm.then_inc(filled[banks[(c, b)]], 1)

            def turn(key, a, b, l):
                acc = claim(key, l)
                for j, block_ in enumerate((a, b)):
                    for t in range(TT):
                        mm = nc.tensor.transpose(acc[:, j * SEQ + t * P:j * SEQ + (t + 1) * P], block_(t), ident[:])
                mm.then_inc(filled[banks[key]], 1)

            def turn_norm(name, l, k0):
                pe.wait_ge(xn_done.sem, xn_done.at(l, k0 + 2))
                for kp in range(4):
                    turn((name, kp), lambda t: xn[:, t, 2 * kp::8], lambda t: xn[:, t, 2 * kp + 1::8], l)
                pe.wait_ge(nT_act.sem, nT_act.at(l, 2 * k0 + 4))
                pe.wait_ge(nT_dve.sem, nT_dve.at(l, 2 * k0 + 4))

            def turn_heads(name, which, l):
                pe.wait_ge(roped.sem, roped.at(l, 2 * which + 2))
                for b in range(2):
                    turn((name, b), lambda t: qk[:, which, t, 2 * b * P:(2 * b + 1) * P],
                         lambda t: qk[:, which, t, (2 * b + 1) * P:(2 * b + 2) * P], l)

            def triangle(key, kt_, qt_, l):
                acc = claim(key, l)
                nc.tensor.matmul(acc[:, 0:SEQ], kt_[:, 0:P], qt_, start=True, stop=True)
                nc.tensor.matmul(acc[:, SEQ:TRI], kt_[:, P:SEQ], qt_[:, P:SEQ], start=True,
                                 stop=True).then_inc(filled[banks[key]], 1)

            def suffix_sums(h, l):
                pe.wait_ge(sp_masked.sem, sp_masked.at(l, h + 1))
                acc = claim(("c", h), l)
                nc.tensor.matmul(acc[:, 0:SEQ], suffix[:], sp[:, h, 0:SEQ], start=True, stop=False)
                nc.tensor.matmul(acc[:, P:SEQ], ones[:], sp[:, h, SEQ:TRI], start=False, stop=True)
                nc.tensor.matmul(acc[:, SEQ:TRI], suffix[:], sp[:, h, SEQ:TRI], start=True,
                                 stop=True).then_inc(filled[banks[("c", h)]], 1)

            def stick_out(hp, l):
                pe.wait_ge(w_masked.sem, w_masked.at(l, 2 * hp + 2))
                acc = claim(("so", hp), l)
                for e in range(2):
                    h = 2 * hp + e
                    o = acc[e * DS:(e + 1) * DS, :]
                    nc.tensor.matmul(o[:, 0:SEQ], sv[:, 0, h * DS:(h + 1) * DS], sp[:, h, 0:SEQ],
                                     start=True, stop=False)
                    mm = nc.tensor.matmul(o[:, P:SEQ], sv[:, 1, h * DS:(h + 1) * DS], sp[:, h, SEQ:TRI],
                                          start=False, stop=True)
                mm.then_inc(filled[banks[("so", hp)]], 1)

            def retention_out(h, l):
                pe.wait_ge(st_in.sem, st_in.at(l, h + 1))
                acc = claim(("ro", h), l)
                v = [rv[:, t, h * DV:(h + 1) * DV] for t in range(TT)]
                nc.tensor.matmul(acc[:, 0:DV], ST[:, h, 0:P], v[0], start=True, stop=True)
                nc.tensor.matmul(acc[:, DV:2 * DV], ST[:, h, P:SEQ], v[0], start=True, stop=False)
                nc.tensor.matmul(acc[:, DV:2 * DV], ST[:, h, SEQ:TRI], v[1], start=False,
                                 stop=True).then_inc(filled[banks[("ro", h)]], 1)

            def output_product(name, w_name, aT, n_units, l):
                for u in range(n_units):
                    w = weights((w_name, u), l)
                    for j in range(2):
                        for i in range(4):
                            t, half = divmod(i, 2)
                            if u == 0 and j == 0:
                                claim((name, i), l)
                            last = u == n_units - 1 and j == 1
                            mm = nc.tensor.matmul(bank_of((name, i)), aT[:, 2 * u + j, t * P:(t + 1) * P],
                                                  w[:, j, half * 512:(half + 1) * 512],
                                                  start=(u == 0 and j == 0), stop=last)
                            if last:
                                mm.then_inc(filled[banks[(name, i)]], 1)
                    if u < n_units - 1:
                        mm.then_inc(unit_read.sem, 1)

            def gate_up(p, l, step):
                wg = weights(("gate", p), l, step)
                wu = weights(("up", p), l, step)
                for j in range(2):
                    key = ("gu", 2 * p + j)
                    acc = claim(key, l, step * 4)
                    for w, at in ((wg, 0), (wu, SEQ)):
                        for k in range(KT):
                            mm = nc.tensor.matmul(acc[:, at:at + SEQ], w[:, k, j * P:(j + 1) * P], T8[:, k, :],
                                                  start=(k == 0), stop=(k == KT - 1))
                    mm.then_inc(filled[banks[key]], 1)

            def down(p, l, step, begin=False, end=False):
                w = weights(("down", p), l, step)
                for j in range(2):
                    tile = 2 * p + j
                    pe.wait_ge(gu_done.sem, gu_done.at(l, tile + 1) + step * 4)
                    for i in range(4):
                        t, half = divmod(i, 2)
                        if begin and j == 0:
                            claim(("ffn", i), l)
                        mm = nc.tensor.matmul(bank_of(("ffn", i)), guT[:, tile % 4, t * P:(t + 1) * P],
                                              w[:, j, half * 512:(half + 1) * 512],
                                              start=(begin and j == 0), stop=(end and j == 1))
                        if end and j == 1:
                            mm.then_inc(filled[banks[("ffn", i)]], 1)
                if not end:
                    mm.then_inc(unit_read.sem, 1)

            pe.wait_ge(const_in, N_CONST * 16)
            pe.wait_ge(const_set, 1)
            with pe.Fori(0, LAYERS) as l:
                turn_norm("nT", l, 0)
                project("rq", l)
                project("rk", l)
                project_turned("sq", l)
                project_turned("sk", l)
                project("rv0", l)
                turn_heads("qT", 0, l)
                turn_heads("kT", 1, l)
                project("rv1", l)
                pe.wait_ge(qT_in.sem, qT_in.at(l, 2))
                pe.wait_ge(kT_in.sem, kT_in.at(l, 2))
                for h in range(HR):
                    triangle(("rs", h), kT[:, h, :], qT[:, h, :], l)
                pe.wait_ge(sqk_in.sem, sqk_in.at(l, 4))
                for h in range(HS):
                    rows = slice((h % 2) * DS, (h % 2 + 1) * DS)
                    triangle(("z", h), skT[rows, h // 2, :], sqT[rows, h // 2, :], l)
                project("sv", l)
                project("rg0", l)
                pe.wait_ge(rv_in.sem, rv_in.at(l, 4))
                for h in range(HR):
                    retention_out(h, l)
                project("rg1", l)
                for h in range(HS):
                    suffix_sums(h, l)
                project("gr0", l)
                project("gr1", l)
                pe.wait_ge(sv_in.sem, sv_in.at(l, 2))
                for hp in range(HS // 2):
                    stick_out(hp, l)
                project("gs0", l)
                project("gs1", l)
                pe.wait_ge(ret_gated.sem, ret_gated.at(l, 2))
                for kp in range(4):
                    turn(("rT", kp), lambda t: retn[:, t, 2 * kp * P:(2 * kp + 1) * P],
                         lambda t: retn[:, t, (2 * kp + 1) * P:(2 * kp + 2) * P], l)
                pe.wait_ge(rT_act.sem, rT_act.at(l, 2))
                pe.wait_ge(rT_dve.sem, rT_dve.at(l, 2))
                output_product("ret", "w_ret_o", retT, 4, l)
                pe.wait_ge(sbT_in.sem, sbT_in.at(l, 4))
                output_product("sb", "w_sb_o", sbT, 2, l)
                pe.wait_ge(merged.sem, merged.at(l, 4))
                for kp in range(4):
                    turn(("mT", kp), lambda t: xn[:, t, 2 * kp * P:(2 * kp + 1) * P],
                         lambda t: xn[:, t, (2 * kp + 1) * P:(2 * kp + 2) * P], l)
                pe.wait_ge(mT_act.sem, mT_act.at(l, 2))
                pe.wait_ge(mT_dve.sem, mT_dve.at(l, 2))
                output_product("wo", "w_out", T8, 4, l)
                turn_norm("nT2", l, 2)
                gate_up(0, l, 0)
                gate_up(1, l, 0)
                down(0, l, 0, begin=True)
                with pe.Fori(0, (PAIRS - 3) // 2) as it:
                    for p in (1, 2):
                        gate_up(p + 1, l, it)
                        down(p, l, it)
                gate_up(PAIRS - 1, l, 0)
                down(PAIRS - 2, l, 0)
                down(PAIRS - 1, l, 0, end=True)


            def claim2(key, l):
                old = held_before(banks2, key)
                if old is not None and old in read2:
                    signal_, k = read2[old]
                    pe.wait_ge(signal_.sem, signal_.at(l, k))
                return bank2(key)

            def unit(key, l, more=0):
                pe.wait_ge(landed[units2[key]], (units2.before(key, l) + 1 + more) * 16)
                return ring[:, units2[key], :]

            def fill(mm, key):
                mm.then_inc(filled[banks2[key]], 1)

            def project2(c, l):
                width = COL2[c][1]
                w = [unit((c, u), l)[:, 0:4 * width].rearrange("p (k n) -> p k n", k=4) for u in range(2)]
                for t in range(TT):
                    acc = claim2((c, t), l)
                    for k in range(KT):
                        mm = nc.tensor.matmul(acc[:, 0:width], T8[:, k, t * P:(t + 1) * P], w[k // 4][:, k % 4, :],
                                              start=(k == 0), stop=(k == KT - 1))
                    fill(mm, (c, t))

            def turn2(key, blocks, l):
                acc = claim2(key, l)
                for j, block_ in enumerate(blocks):
                    for t in range(TT):
                        a = block_(t)
                        mm = nc.tensor.transpose(acc[0:a.shape[1], j * SEQ + t * P:j * SEQ + (t + 1) * P], a, ident[:])
                fill(mm, key)

            def turn_stream(name, l, buf, n, split):
                for kp in range(4):
                    if split:
                        blocks = [lambda t, k=k: buf[:, t, k::8] for k in (2 * kp, 2 * kp + 1)]
                    else:
                        blocks = [lambda t, k=k: buf[:, t, k * P:(k + 1) * P] for k in (2 * kp, 2 * kp + 1)]
                    turn2((name, kp), blocks, l)
                pe.wait_ge(bT_act.sem, bT_act.at(l, 2 * n + 2))
                pe.wait_ge(bT_dve.sem, bT_dve.at(l, 2 * n + 2))

            def index_scores(h, l):
                rows = slice(h % 4 * DI, h % 4 * DI + DI)
                acc = claim2(("rel", h), l)
                nc.tensor.matmul(acc[:, 0:P], qiT[rows, h // 4, 0:P], kkT[rows, 1, 0:P], start=True, stop=True)
                fill(nc.tensor.matmul(acc[:, P:TRI], qiT[rows, h // 4, P:SEQ], kkT[rows, 1, :],
                                      start=True, stop=True), ("rel", h))

            def head_operands(j):
                if j < HM:
                    return [(mqT[0:96, j, :], mkT[0:96, j, :])]
                if j < HM + HX:
                    n = j - HM
                    rows = slice(n % 2 * HD, (n % 2 + 1) * HD)
                    return [(dsT[rows, n // 2, :], kkT[rows, 0, :])]
                out_ = []
                for c in range(len(DILATED)):
                    n = c * HX + j - HM - HX
                    rows = slice(n % 2 * HD, (n % 2 + 1) * HD)
                    out_.append((dqT[rows, n // 2, :], dkT[rows, n // 2, :]))
                return out_

            def head_scores(j, l):
                ops = head_operands(j)
                if len(ops) == 1:
                    q, k = ops[0]
                    acc = claim2(("S", j, 0), l)
                    nc.tensor.matmul(acc[:, 0:P], q[:, 0:P], k[:, 0:P], start=True, stop=True)
                    fill(nc.tensor.matmul(acc[:, P:TRI], q[:, P:SEQ], k, start=True, stop=True), ("S", j, 0))
                    return
                for part, which in enumerate(((0, 1), (2,))):
                    acc = claim2(("S", j, part), l)
                    for n, c in enumerate(which):
                        q, k = ops[c]
                        mm = nc.tensor.matmul(acc[:, n * SEQ:(n + 1) * SEQ], q[:, P:SEQ], k, start=True, stop=True)
                    fill(mm, ("S", j, part))
                acc = claim2(("S", j, 2), l)
                for c, (q, k) in enumerate(ops):
                    mm = nc.tensor.matmul(acc[:, c * P:(c + 1) * P], q[:, 0:P], k[:, 0:P], start=True, stop=True)
                fill(mm, ("S", j, 2))

            def head_turn(j, l):
                pe.wait_ge(weighed.sem, weighed.at(l, j + 1))
                n = 3 if j < HM + HX else 9
                for part in range(parts(j)):
                    acc = claim2(("E", j, part), l)
                    lo = 0 if n == 3 else (0, 4, 6)[part]
                    hi = 3 if n == 3 else (4, 6, 9)[part]
                    for i in range(lo, hi):
                        mm = nc.tensor.transpose(acc[:, (i - lo) * P:(i - lo + 1) * P],
                                                 S[:, j % 2, i * P:(i + 1) * P], ident[:])
                    fill(mm, ("E", j, part))

            def head_out(j, l):
                signal_, k = read2["E", j, parts(j) - 1]
                pe.wait_ge(signal_.sem, signal_.at(l, k))
                if j >= HM + HX:
                    pe.wait_ge(ET_act.sem, ET_act.at(l, j - HM - HX + 1))
                E = ET[:, j % 2, :]
                second = [] if j < HM + HX else [(i, c, kt_) for i, (c, kt_) in
                                                enumerate([(c, kt_) for c in range(3) for kt_ in range(2)])]
                if j < HM:
                    v = lambda c, kt_: mvv[:, kt_, j * VM:(j + 1) * VM]
                elif j < HM + HX:
                    v = lambda c, kt_: U[:, kt_, 736:800]
                else:
                    n = j - HM - HX
                    v = lambda c, kt_: U[:, kt_, 2632 + (c * HX + n) * HD:2632 + (c * HX + n + 1) * HD]
                cols = slice(j % 8 * HD, (j % 8 + 1) * HD)
                o = [bank2(("O", 2 * (j // 8) + t))[:, cols] for t in range(TT)]
                if j < HM + HX:
                    todo = [(0, [(0, 0, 0)]), (1, [(1, 0, 0), (2, 0, 1)])]
                else:
                    todo = [(0, [(6 + c, c, 0) for c in range(3)]),
                            (1, [(2 * c + kt_, c, kt_) for c in range(3) for kt_ in range(2)])]
                for t, terms in todo:
                    for n_, (blk, c, kt_) in enumerate(terms):
                        mm = nc.tensor.matmul(o[t], E[:, blk * P:(blk + 1) * P], v(c, kt_),
                                              start=(n_ == 0), stop=(n_ == len(terms) - 1))
                    if j % 8 == 7:
                        fill(mm, ("O", 2 * (j // 8) + t))

            with pe.Fori(0, LAYERS) as l:
                pe.wait_ge(x_ready.sem, x_ready.at(l, 0))
                turn_stream("xT", l, H, 0, True)
                project2("C", l)
                project2("A", l)
                project2("B", l)
                project2("q0", l)
                pe.wait_ge(r_add.sem, r_add.at(l, 1))
                turn2(("qiT", 0), [lambda t: U[:, t, 800:928], lambda t: U[:, t, 928:1056]], l)
                pe.wait_ge(kcopy.sem, kcopy.at(l, 3))
                turn2(("kkT", 0), [lambda t: kk[:, t, :], lambda t: ki4[:, t, :]], l)
                pe.wait_ge(latent_done.sem, latent_done.at(l, 1))
                turn2(("cT", 0), [lambda t: U[:, t, 0:128], lambda t: U[:, t, 128:256]], l)
                turn2(("cT", 1), [lambda t: U[:, t, 256:384]], l)
                project2("q1", l)
                pe.wait_ge(qiT_in.sem, qiT_in.at(l, 1))
                pe.wait_ge(kkT_in.sem, kkT_in.at(l, 1))
                for h in range(HI):
                    index_scores(h, l)
                pe.wait_ge(cT_in.sem, cT_in.at(l, 3))
                w = unit(("uq", 0), l)[:, 0:1536].rearrange("p (k n) -> p k n", k=2)
                for i in range(4):
                    t, half = divmod(i, 2)
                    acc = claim2(("uq", i), l)
                    for k in range(2):
                        mm = nc.tensor.matmul(acc[:, 0:384], cT[:, k, t * P:(t + 1) * P],
                                              w[:, k, half * 384:(half + 1) * 384], start=(k == 0), stop=(k == 1))
                    fill(mm, ("uq", i))
                w = unit(("ukv", 0), l)
                for i in range(4):
                    t, half = divmod(i, 2)
                    fill(nc.tensor.matmul(claim2(("ukv", i), l), cT[:, 2, t * P:(t + 1) * P],
                                          w[:, half * 512:(half + 1) * 512], start=True, stop=True), ("ukv", i))
                project2("k0", l)
                project2("k1", l)
                project2("v0", l)
                pe.wait_ge(r_add.sem, r_add.at(l, 4))
                for b in range(4):
                    turn2(("mqT", b), [lambda t, h=h: mq[:, t, h * 96:(h + 1) * 96] for h in (2 * b, 2 * b + 1)], l)
                pe.wait_ge(mk_in.sem, mk_in.at(l, 4))
                for b in range(4):
                    turn2(("mkT", b), [lambda t, h=h: mk[:, t, h * 96:(h + 1) * 96] for h in (2 * b, 2 * b + 1)], l)
                project2("v1", l)
                turn2(("dsT", 0), [lambda t: U[:, t, 416:544], lambda t: U[:, t, 544:672]], l)
                pe.wait_ge(r_add.sem, r_add.at(l, 5))
                for name, at in (("dqT", 1096), ("dkT", 1864)):
                    for b in range(3):
                        turn2((name, b), [lambda t, c=at + (2 * b + i) * P: U[:, t, c:c + P] for i in range(2)], l)
                pe.wait_ge(mqT_in.sem, mqT_in.at(l, 4))
                pe.wait_ge(mkT_in.sem, mkT_in.at(l, 4))
                pe.wait_ge(dsT_in.sem, dsT_in.at(l, 1))
                pe.wait_ge(dqT_in.sem, dqT_in.at(l, 3))
                pe.wait_ge(dkT_in.sem, dkT_in.at(l, 3))
                for i in range(4):
                    claim2(("O", i), l)
                for j in range(JOBS + 2):
                    if j < JOBS:
                        head_scores(j, l)
                    if 1 <= j <= JOBS:
                        head_turn(j - 1, l)
                    if j >= 2:
                        head_out(j - 2, l)
                pe.wait_ge(mix_done.sem, mix_done.at(l, 4))
                turn_stream("oT", l, xn, 1, False)
                for u in range(4):
                    w = unit(("w_o_2", u), l).rearrange("p (k n) -> p k n", k=2)
                    for j in range(2):
                        for i in range(4):
                            t, half = divmod(i, 2)
                            last = u == 3 and j == 1
                            mm = nc.tensor.matmul(bank2(("wo", i)), T8[:, 2 * u + j, t * P:(t + 1) * P],
                                                  w[:, j, half * 512:(half + 1) * 512],
                                                  start=(u == 0 and j == 0), stop=last)
                            if last:
                                fill(mm, ("wo", i))
                    if u < 3:
                        mm.then_inc(unit_read2.sem, 1)
                pe.wait_ge(x_ready.sem, x_ready.at(l, 2))
                turn_stream("xT2", l, H, 2, True)
                acc = bank2(("router", 0))
                for t in range(TT):
                    for k in range(KT):
                        mm = nc.tensor.matmul(acc[:, t * 64:t * 64 + 36], T8[:, k, t * P:(t + 1) * P], rw[:, k, :],
                                              start=(k == 0), stop=(k == KT - 1))
                fill(mm, ("router", 0))
                pe.wait_ge(hot_done.sem, hot_done.at(l, 1))
                acc = bank2(("ranks", 0))
                nc.tensor.matmul(acc[:, 0:4], before, hot[:, 0, :], start=True, stop=True)
                nc.tensor.matmul(acc[:, 4:8], before, hot[:, 1, :], start=True, stop=False)
                nc.tensor.matmul(acc[:, 4:8], ones[:], hot[:, 0, :], start=False, stop=True)
                nc.tensor.matmul(acc[:, 8:12], ones[:], hot[:, 0, :], start=True, stop=False)
                fill(nc.tensor.matmul(acc[:, 8:12], ones[:], hot[:, 1, :], start=False, stop=True), ("ranks", 0))
                wait_apart(pe, npass_done.sem, npass_done.at(l, 1))
                passes = pe.value_load(npass[0:1, 0:1], min_val=1, max_val=2)
                with pe.Fori(0, 2) as ps_:
                    lp = l * 2 + ps_

                    def fill_p(mm, name, *key):
                        mm.then_inc(filled[banks2[(name, 0) + key]], 1)

                    with pe.If(passes > ps_):
                        pe.wait_ge(pick_done.sem, pick_done.at(lp, 1))
                        for b in range(2):
                            acc = bank2(("pT", 0, b))
                            for i in range(2):
                                for t in range(TT):
                                    mm = nc.tensor.transpose(acc[:, (2 * i + t) * P:(2 * i + t + 1) * P],
                                                             pick[:, 2 * b + i, t, :], ident[:])
                            fill_p(mm, "pT", b)
                        acc = bank2(("slots", 0))
                        for g in range(GROUPS):
                            for t in range(TT):
                                mm = nc.tensor.matmul(acc[:, g * EXPERTS:(g + 1) * EXPERTS], pick[:, g, t, :],
                                                      gate[:, t, g, :], start=(t == 0), stop=(t == 1))
                        fill_p(mm, "slots")
                        pe.wait_ge(pickT_in.sem, pickT_in.at(lp, 2))
                        wait_apart(pe, gslot_in.sem, gslot_in.at(lp, 1))

                        def gate_up2(e, g):
                            more = units_pass * ps_ + g * units_group
                            unit(("gate", 0, 0, e), l, more)
                            unit(("up", 0, 0, e), l, more)
                            s_ = units2[("gate", 0, 0, e)]
                            w_ = ring[:, s_:s_ + 2, :].rearrange("p s (k n) -> p s k n", k=KT)
                            acc = bank2(("gu", 0, 0, e))
                            for k in range(KT):
                                mm = nc.tensor.matmul(acc.rearrange("p (s n) -> p s n", s=2), XG[:, k, :], w_[:, :, k, :],
                                                      start=(k == 0), stop=(k == KT - 1))
                            fill_p(mm, "gu", 0, e)

                        def down2(e, g):
                            count = g * EXPERTS + e
                            pe.wait_ge(h2_done.sem, h2_done.at(lp, 1) + count)
                            acc = bank2(("hT", 0, 0, e))
                            for j in range(2):
                                mm = nc.tensor.transpose(acc[:, j * P:(j + 1) * P], hh[:, e % 2, j::2], ident[:])
                            fill_p(mm, "hT", 0, e)
                            w_ = unit(("down", 0, 0, e), l, units_pass * ps_ + g * units_group)
                            pe.wait_ge(hT_in.sem, hT_in.at(lp, 1) + count)
                            for j in range(2):
                                for half in range(2):
                                    mm = nc.tensor.matmul(bank2(("yg", 0, 0, half)), hT[:, e % 2, j * P:(j + 1) * P],
                                                          w_[:, j * D + half * 512:j * D + (half + 1) * 512],
                                                          start=(e == 0 and j == 0),
                                                          stop=(e == EXPERTS - 1 and j == 1))
                                    if e == EXPERTS - 1 and j == 1:
                                        fill_p(mm, "yg", 0, half)
                            if e < EXPERTS - 1:
                                mm.then_inc(unit_read2.sem, 1)

                        with pe.Fori(0, GROUPS) as g:
                            for b in range(2):
                                acc = bank2(("xg", 0, 0, b))
                                for k in range(4):
                                    for t in range(TT):
                                        mm = nc.tensor.matmul(acc[:, k * P:(k + 1) * P], H[:, t, 4 * b + k::8],
                                                              pick[:, bass.ds(g, 1), t, :].rearrange("p a n -> p (a n)"),
                                                              start=(t == 0), stop=(t == 1))
                                fill_p(mm, "xg", 0, b)
                            pe.wait_ge(xg_act.sem, xg_act.at(lp, 1) + g)
                            pe.wait_ge(xg_dve.sem, xg_dve.at(lp, 1) + g)
                            gate_up2(0, g)
                            pe.wait_ge(yg_in.sem, yg_in.at(lp, 0) + g * 2)
                            for e in range(1, EXPERTS):
                                gate_up2(e, g)
                                down2(e - 1, g)
                            down2(EXPERTS - 1, g)
                        pe.wait_ge(yg_in.sem, yg_in.at(lp, 2 * GROUPS))
                        for i in range(4):
                            t, half = divmod(i, 2)
                            for g in range(GROUPS):
                                mm = nc.tensor.matmul(bank2(("sc", 0, i)), pickT[:, g, t * P:(t + 1) * P],
                                                      YG[:, g, half * 512:(half + 1) * 512],
                                                      start=(g == 0), stop=(g == GROUPS - 1))
                            fill_p(mm, "sc", i)
                    with pe.Else():
                        pe.drain()
                        for b in range(BANKS):
                            n = sum(k[0] in PASS_KEYS and k[1] == 0 and r == b for k, (r, _) in banks2.place.items())
                            pe.sem_inc(filled[b], n)
                        pe.sem_inc(unit_read2.sem, GROUPS * (EXPERTS - 1))

        @block.scalar
        def _(act):
            def content(key, l, more=0):
                act.wait_ge(filled[banks[key]], banks.before(key, l, more) + 1)
                return bank_of(key)

            def square_sums(l, k0):
                act.wait_ge(h_added.sem, h_added.at(l, 2 * k0))
                for t in range(TT):
                    nc.scalar.activation(xn[:, t, :], H[:, t, :], ACT.Square,
                                         accum_out=stat[:, t:t + 1]).then_inc(sumsq.sem, 1)

            def norm_turned(name, l, w):
                for kp in (0, 2):
                    acc = content((name, kp), l)
                    for j in range(2):
                        nc.scalar.activation(T8[:, 2 * kp + j, :], acc[:, j * SEQ:(j + 1) * SEQ], ACT.Copy,
                                             scale=gains[:, w, 2 * kp + j:2 * kp + j + 1]).then_inc(nT_act.sem, 1)

            def leave(key, l, to, signal_, scale=1.0):
                nc.scalar.activation(to, content(key, l), ACT.Copy, scale=scale).then_inc(signal_.sem, 1)

            def flat(a):
                return a.rearrange("p a n -> p (a n)")

            act.wait_ge(table_done, 1)
            nc.scalar.activation(rotation[1], turns_[:, 0], ACT.Sin).then_inc(table_done, 1)
            nc.scalar.activation(rotation[0], turns_[:, 1], ACT.Sin).then_inc(table_done, 1)
            with act.Fori(0, LAYERS) as l:
                act.sem_clear(act_step)
                square_sums(l, 0)
                act.wait_ge(gains_in.sem, gains_in.at(l, 32))
                norm_turned("nT", l, 0)
                for name, to, scale in (("sq", sqT, DS ** -0.5), ("sk", skT, 1.0)):
                    for b in range(2):
                        leave((name, b), l, flat(to[:, 2 * b:2 * b + 2, :]), sqk_in, scale)
                for t in range(TT):
                    leave(("rv0", t), l, rv[:, t, 0:512], rv_in)
                for b in range(2):
                    leave(("qT", b), l, flat(qT[:, 2 * b:2 * b + 2, :]), qT_in)
                for t in range(TT):
                    leave(("rv1", t), l, rv[:, t, 512:D], rv_in)
                nc.scalar.preload_act_table_set("natural_log_exp_and_others")
                for h in range(HS + 1):
                    if h < HS:
                        nc.scalar.activation(z[:, h, :], content(("z", h), l)[:, 0:TRI],
                                             ACT.Copy).then_inc(z_in.sem, 1)
                    if h >= 1:
                        g = h - 1
                        act.wait_ge(negabs.sem, negabs.at(l, g + 1))
                        if g >= 2:
                            act.wait_ge(sp_done.sem, sp_done.at(l, g - 1))
                        nc.scalar.activation(lnt[:, g % 2, :], sp[:, g, :], ACT.Exp).then_inc(act_step, 1)
                        act.wait_ge(act_step, g + 1)
                        nc.scalar.activation(lnt[:, g % 2, :], lnt[:, g % 2, :], ACT.Ln,
                                             bias=ones[:, 0:1]).then_inc(ln_done.sem, 1)
                for t in range(TT):
                    leave(("sv", t), l, sv[:, t, :], sv_in)
                for h in range(HS):
                    act.wait_ge(logw.sem, logw.at(l, h + 1))
                    nc.scalar.activation(sp[:, h, :], z[:, h, :], ACT.Exp).then_inc(w_exp.sem, 1)
                for half in range(2):
                    for t in range(TT):
                        leave((f"gr{half}", t), l, gr[:, t, half * 512:(half + 1) * 512], gr_in)
                act.wait_ge(rg_in.sem, rg_in.at(l, 4))
                for t in range(TT):
                    nc.scalar.activation(rg[:, t, :], rg[:, t, :], ACT.Silu).then_inc(rg_silu.sem, 1)
                act.wait_ge(gr_in.sem, gr_in.at(l, 4))
                for t in range(TT):
                    nc.scalar.activation(gr[:, t, :], gr[:, t, :], ACT.Sigmoid).then_inc(gates.sem, 1)
                act.wait_ge(gs_in.sem, gs_in.at(l, 4))
                for t in range(TT):
                    nc.scalar.activation(gs[:, t, :], gs[:, t, :], ACT.Sigmoid).then_inc(gates.sem, 1)
                for kp in (0, 2):
                    leave(("rT", kp), l, flat(retT[:, 2 * kp:2 * kp + 2, :]), rT_act)
                for kp in (0, 2):
                    leave(("mT", kp), l, flat(T8[:, 2 * kp:2 * kp + 2, :]), mT_act)
                square_sums(l, 2)
                norm_turned("nT2", l, 1)

                def gate(i, step):
                    acc = content(("gu", i), l, step)
                    if i >= 4:
                        act.wait_ge(gu_done.sem, gu_done.at(l, i - 3) + step * 4)
                    nc.scalar.activation(silu_g[:, i % 4, :], acc[:, 0:SEQ], ACT.Silu).then_inc(g_silu.sem, 1)

                for i in range(4):
                    gate(i, 0)
                with act.Fori(0, (PAIRS - 3) // 2) as it:
                    for i in range(4, 8):
                        gate(i, it)
                for i in range(2 * PAIRS - 2, 2 * PAIRS):
                    gate(i, 0)
            square_sums(LAYERS, 0)

            def content2(key, l):
                act.wait_ge(filled[banks2[key]], banks2.before(key, l) + 1)
                return bank2(key)

            def leave2(key, l, to, signal_, rows=P, width=512, scale=1.0, at=0):
                acc = content2(key, l)[0:rows, at:at + width]
                nc.scalar.activation(to, acc, ACT.Copy, scale=scale).then_inc(signal_.sem, 1)

            act.sem_inc(yg_in.sem, 1)
            with act.Fori(0, LAYERS) as l:
                for kp in (0, 2):
                    leave2(("xT", kp), l, flat(T8[:, 2 * kp:2 * kp + 2, :]), bT_act)

                def chunk(name):
                    at, width = COL2[name]
                    for t in range(TT):
                        leave2((name, t), l, U[:, t, at:at + width], u_act, width=width)

                chunk("C")
                act.wait_ge(u_dve.sem, u_dve.at(l, 2))
                for n, (lo, hi) in enumerate(((0, 256), (256, 384))):
                    for t in range(TT):
                        nc.scalar.activation(relu[:, t, lo:hi], U[:, t, lo:hi], ACT.Square,
                                             accum_out=lstat[:, 0, 2 * n + t:2 * n + t + 1]).then_inc(latent_sq.sem, 1)
                chunk("B")
                leave2(("qiT", 0), l, flat(qiT), qiT_in)
                act.wait_ge(params_in.sem, params_in.at(l, 16 * N_PARAMS))
                for k in range(2):
                    leave2(("cT", 0), l, cT[:, k, :], cT_in, width=SEQ, scale=cgain[:, k:k + 1], at=k * SEQ)
                leave2(("cT", 1), l, cT[:, 2, :], cT_in, width=SEQ, scale=cgain[:, 2:3])
                chunk("q1")
                for h in range(HI):
                    acc = content2(("rel", h), l)[:, 0:TRI]
                    if h >= 2:
                        act.wait_ge(score_in.sem, score_in.at(l, h - 1))
                    nc.scalar.activation(relu[:, h % 2, :], acc, ACT.Relu).then_inc(relu_in.sem, 1)
                for i in range(4):
                    t, half = divmod(i, 2)
                    leave2(("uq", i), l, mq[:, t, half * 384:(half + 1) * 384], mq_in, width=384)
                chunk("k1")
                for b in range(4):
                    leave2(("mqT", b), l, flat(mqT[0:96, 2 * b:2 * b + 2, :]), mqT_in, rows=96)
                chunk("v1")
                leave2(("dsT", 0), l, flat(dsT), dsT_in)
                for b in range(3):
                    leave2(("dqT", b), l, flat(dqT[:, 2 * b:2 * b + 2, :]), dqT_in)
                for j in range(JOBS + 1):
                    if j < JOBS:
                        act.wait_ge(masked.sem, masked.at(l, 3 * j + 3))
                        first = (0, P, TRI) if j < HM + HX else (2 * TRI, 3 * TRI, 2 * TRI)
                        second = (P, TRI) if j < HM + HX else (0, 2 * TRI)
                        for t, (lo, hi) in enumerate((first[0:2], second)):
                            last = nc.scalar.activation(S[:, j % 2, lo:hi], S[:, j % 2, lo:hi], ACT.Exp, scale=-1.0,
                                                        bias=nmx[:, j, t:t + 1], accum_out=lsum[:, j, t:t + 1])
                        last.then_inc(weighed.sem, 1)
                    if j > HM + HX:
                        leave2(("E", j - 1, 0), l, ET[:, (j - 1) % 2, 0:512], ET_act)
                for kp in (0, 2):
                    leave2(("oT", kp), l, flat(T8[:, 2 * kp:2 * kp + 2, :]), bT_act)
                act.wait_ge(x_ready.sem, x_ready.at(l, 2))
                for t in range(TT):
                    nc.scalar.activation(xn[:, t, :], H[:, t, :], ACT.Copy, scale=ALPHA).then_inc(resid_in.sem, 1)
                for kp in (0, 2):
                    leave2(("xT2", kp), l, flat(T8[:, 2 * kp:2 * kp + 2, :]), bT_act)
                act.wait_ge(shift_done.sem, shift_done.at(l, 1))
                nc.scalar.activation(gexp, shifted, ACT.Exp).then_inc(gexp_done.sem, 1)
                act.wait_ge(diff_done.sem, diff_done.at(l, 1))
                nc.scalar.activation(diff[:, 1, :], diff[:, 0, :], ACT.Exp).then_inc(eexp_done.sem, 1)
                wait_apart(act, npass_done.sem, npass_done.at(l, 1))
                passes = act.value_load(npass[0:1, 0:1], min_val=1, max_val=2)
                with act.Fori(0, 2) as ps_:
                    lp = l * 2 + ps_

                    def content_p(g, name, *key):
                        act.wait_ge(filled[banks2[(name, 0) + key]],
                                    pass_turn(name, key, l, ps_, g) + 1)
                        return bank2((name, 0) + key)

                    with act.If(passes > ps_):
                        nc.scalar.activation(flat(pickT[:, 0:2, :]), content_p(0, "pT", 0),
                                             ACT.Copy).then_inc(pickT_in.sem, 1)
                        with act.Fori(0, GROUPS) as g:
                            nc.scalar.activation(flat(XG[:, 0:4, :]), content_p(g, "xg", 0, 0),
                                                 ACT.Copy).then_inc(xg_act.sem, 1)
                            for e in range(EXPERTS + 1):
                                if e < EXPERTS:
                                    acc = content_p(g, "gu", 0, e)
                                    if e >= 2:
                                        act.wait_ge(h2_done.sem, h2_done.at(lp, e - 1) + g * EXPERTS)
                                    nc.scalar.activation(sg[:, e % 2, :], acc[:, 0:EH],
                                                         ACT.Silu).then_inc(g2_silu.sem, 1)
                                if e >= 1:
                                    acc = content_p(g, "hT", 0, e - 1)
                                    nc.scalar.activation(hT[:, (e - 1) % 2, :], acc[:, 0:2 * P],
                                                         ACT.Copy).then_inc(hT_in.sem, 1)
                            for half in range(2):
                                nc.scalar.activation(
                                    YG[:, bass.ds(g, 1), half * 512:(half + 1) * 512].rearrange("p a n -> p (a n)"),
                                    content_p(g, "yg", 0, half), ACT.Copy).then_inc(yg_in.sem, 1)
                    with act.Else():
                        act.drain()
                        for signal_, n in ((pickT_in, 1), (xg_act, GROUPS), (g2_silu, GROUPS * EXPERTS),
                                           (hT_in, GROUPS * EXPERTS), (yg_in, 2 * GROUPS)):
                            act.sem_inc(signal_.sem, n)

        @block.vector
        def _(dve):
            def content(key, l, more=0):
                dve.wait_ge(filled[banks[key]], banks.before(key, l, more) + 1)
                return bank_of(key)

            def normalise(l, k0):
                dve.wait_ge(sumsq.sem, sumsq.at(l, k0 + 2))
                nc.vector.tensor_scalar(stat[:, 2:4], stat[:, 0:2], 1.0 / D, EPS, ALU.mult,
                                        ALU.add).then_inc(meansq.sem, 1)
                dve.wait_ge(rms.sem, rms.at(l, k0 // 2 + 1))
                for t in range(TT):
                    nc.vector.tensor_scalar(xn[:, t, :], H[:, t, :], stat[:, 4 + t:5 + t], None,
                                            ALU.mult).then_inc(xn_done.sem, 1)

            def norm_turned(name, l, w):
                for kp in (1, 3):
                    acc = content((name, kp), l)
                    for j in range(2):
                        nc.vector.tensor_scalar(T8[:, 2 * kp + j, :], acc[:, j * SEQ:(j + 1) * SEQ],
                                                gains[:, w, 2 * kp + j:2 * kp + j + 1], None,
                                                ALU.mult).then_inc(nT_dve.sem, 1)

            def leave(key, l, to, signal_):
                nc.vector.tensor_copy(to, content(key, l)).then_inc(signal_.sem, 1)

            def rotate(name, which, t, l):
                n = 2 * which + t
                acc = content((name, t), l).rearrange("p (h d) -> p h d", h=HR)
                half = DK // 2
                if n >= 2:
                    dve.wait_ge(roped.sem, roped.at(l, n - 1))
                o = rot[:, t, :].rearrange("p (h d) -> p h d", h=HR)
                nc.vector.tensor_tensor(qk[:, which, t, :].rearrange("p (h d) -> p h d", h=HR), acc,
                                        rope1[:, t, 0:DK].unsqueeze(1).to_broadcast([P, HR, DK]), ALU.mult)
                nc.vector.tensor_tensor(o[:, :, 0:half], acc[:, :, half:DK],
                                        rope1[:, t, DK:DK + half].unsqueeze(1).to_broadcast([P, HR, half]), ALU.mult)
                nc.vector.tensor_tensor(o[:, :, half:DK], acc[:, :, 0:half],
                                        rope1[:, t, DK + half:2 * DK].unsqueeze(1).to_broadcast([P, HR, half]),
                                        ALU.mult).then_inc(rotated.sem, 1)

            def flat(a):
                return a.rearrange("p a n -> p (a n)")

            nc.vector.memset(ones[:], 1.0)
            nc.vector.memset(minus_half[:], -0.5).then_inc(const_set, 1)
            dve.wait_ge(x_in, 16)
            dve.sem_inc(h_added.sem, 1)
            dve.wait_ge(const_in, N_CONST * 16)
            two_pi = 2 * np.pi
            c1 = 6.28125
            c2 = float(np.float32(np.round((two_pi - c1) * 2 ** 20) / 2 ** 20))
            c3 = float(np.float32(two_pi - c1 - c2))
            n_steps = [0]

            def table(ins):
                n_steps[0] += 1
                ins.then_inc(table_step, 1)
                dve.wait_ge(table_step, n_steps[0])

            ang, whole, over = turns_[:, 0], turns_[:, 1], turns_[:, 2]
            edge = 3.1415925
            table(nc.vector.tensor_copy(pos[:], pos_i[:]))
            for t in range(TT):
                table(nc.vector.tensor_scalar(ang[:, t, :], freq[:, 0, :], pos[:, t:t + 1], None, ALU.mult))
            table(nc.vector.tensor_scalar(whole, ang, 1.0 / two_pi, MAGIC, ALU.mult, ALU.add))
            table(nc.vector.tensor_scalar(whole, whole, -MAGIC, None, ALU.add))
            for c in (c1, c2, c3):
                table(nc.vector.scalar_tensor_tensor(out=ang, in0=whole, scalar=-c, in1=ang, op0=ALU.mult, op1=ALU.add))
            table(nc.vector.tensor_scalar(ang, ang, -edge, edge, ALU.max, ALU.min))
            table(nc.vector.tensor_scalar(whole, ang, np.pi / 2, None, ALU.add))
            table(nc.vector.tensor_scalar(over, whole, np.pi, -two_pi, ALU.is_gt, ALU.mult))
            table(nc.vector.tensor_tensor(whole, whole, over, ALU.add))
            nc.vector.tensor_scalar(whole, whole, -edge, edge, ALU.max, ALU.min).then_inc(table_done, 1)
            dve.wait_ge(table_done, 3)
            for t in range(TT):
                table(nc.vector.tensor_tensor(rotation[1][:, t, :], rotation[1][:, t, :], freq[:, 1, :], ALU.mult))
            with dve.Fori(0, LAYERS) as l:
                dve.sem_clear(dve_step)
                normalise(l, 0)
                dve.wait_ge(gains_in.sem, gains_in.at(l, 32))
                norm_turned("nT", l, 0)
                for which, name in enumerate(("rq", "rk")):
                    for t in range(TT):
                        rotate(name, which, t, l)
                for b in range(2):
                    leave(("kT", b), l, flat(kT[:, 2 * b:2 * b + 2, :]), kT_in)
                for h in range(HR):
                    nc.vector.tensor_tensor(ST[:, h, :], content(("rs", h), l)[:, 0:TRI], decay[:, h, :],
                                            ALU.mult).then_inc(st_in.sem, 1)
                for h in range(HS + 1):
                    if h < HS:
                        dve.wait_ge(z_in.sem, z_in.at(l, h + 1))
                        nc.vector.scalar_tensor_tensor(out=sp[:, h, :], in0=z[:, h, :], scalar=-1.0,
                                                       in1=z[:, h, :], op0=ALU.mult,
                                                       op1=ALU.min).then_inc(negabs.sem, 1)
                    if h >= 1:
                        g = h - 1
                        dve.wait_ge(ln_done.sem, ln_done.at(l, g + 1))
                        nc.vector.scalar_tensor_tensor(out=sp[:, g, :], in0=z[:, g, :], scalar=0.0,
                                                       in1=lnt[:, g % 2, :], op0=ALU.max,
                                                       op1=ALU.add).then_inc(sp_done.sem, 1)
                for t in range(TT):
                    leave(("rg0", t), l, rg[:, t, 0:512], rg_in)
                steps = 0
                for h in range(HR + 1):
                    if h < HR:
                        acc = content(("ro", h), l)
                        for t in range(TT):
                            nc.vector.bn_stats(moments[:, h, t, :], acc[:, t * DV:(t + 1) * DV]).then_inc(dve_step, 1)
                            steps += 1
                        dve.wait_ge(dve_step, steps)
                        for t in range(TT):
                            last = nc.vector.bn_aggr(mv[:, h, t, :], moments[:, h, t, :])
                        last.then_inc(head_var.sem, 1)
                    if h >= 1:
                        g = h - 1
                        dve.wait_ge(head_rstd.sem, head_rstd.at(l, g + 1))
                        acc = bank_of(("ro", g))
                        for t in range(TT):
                            last = nc.vector.tensor_scalar(retn[:, t, g * DV:(g + 1) * DV],
                                                           acc[:, t * DV:(t + 1) * DV], mv[:, g, t, 0:1],
                                                           rstd[:, g, t:t + 1], ALU.subtract, ALU.mult)
                        last.then_inc(ret_normed.sem, 1)
                for t in range(TT):
                    leave(("rg1", t), l, rg[:, t, 512:D], rg_in)
                for h in range(HS):
                    nc.vector.tensor_tensor(z[:, h, :], z[:, h, :], content(("c", h), l)[:, 0:TRI],
                                            ALU.subtract).then_inc(logw.sem, 1)
                for hp in range(HS // 2):
                    nc.vector.tensor_copy(sbT[:, hp, :], content(("so", hp), l)[:, 0:SEQ]).then_inc(sbT_in.sem, 1)
                for half in range(2):
                    for t in range(TT):
                        leave((f"gs{half}", t), l, gs[:, t, half * 512:(half + 1) * 512], gs_in)
                dve.wait_ge(ret_normed.sem, ret_normed.at(l, HR))
                for t in range(TT):
                    dve.wait_ge(rg_silu.sem, rg_silu.at(l, t + 1))
                    nc.vector.tensor_tensor(retn[:, t, :], retn[:, t, :], rg[:, t, :],
                                            ALU.mult).then_inc(ret_gated.sem, 1)
                for kp in (1, 3):
                    leave(("rT", kp), l, flat(retT[:, 2 * kp:2 * kp + 2, :]), rT_dve)
                dve.wait_ge(gates.sem, gates.at(l, 4))
                for i in range(4):
                    t, cols = i // 2, slice(i % 2 * 512, (i % 2 + 1) * 512)
                    nc.vector.tensor_tensor(xn[:, t, cols], content(("ret", i), l), gr[:, t, cols],
                                            ALU.mult).then_inc(ret_out.sem, 1)
                for i in range(4):
                    t, cols = i // 2, slice(i % 2 * 512, (i % 2 + 1) * 512)
                    nc.vector.tensor_tensor(gs[:, t, cols], content(("sb", i), l), gs[:, t, cols],
                                            ALU.mult).then_inc(sb_gated.sem, 1)
                for kp in (1, 3):
                    leave(("mT", kp), l, flat(T8[:, 2 * kp:2 * kp + 2, :]), mT_dve)

                def add_to_h(name):
                    for i in range(4):
                        t, cols = i // 2, slice(i % 2 * 512, (i % 2 + 1) * 512)
                        nc.vector.tensor_tensor(H[:, t, cols], content((name, i), l), H[:, t, cols],
                                                ALU.add).then_inc(h_added.sem, 1)

                add_to_h("wo")
                normalise(l, 2)
                norm_turned("nT2", l, 1)

                def gate_times_up(i, step):
                    if i >= 4:
                        dve.wait_ge(unit_read.sem, unit_read.at(l, 7 + (i - 4) // 2 + 1) + step * 2)
                    dve.wait_ge(g_silu.sem, g_silu.at(l, i + 1) + step * 4)
                    nc.vector.tensor_tensor(guT[:, i % 4, :], bank_of(("gu", i))[:, SEQ:2 * SEQ],
                                            silu_g[:, i % 4, :], ALU.mult).then_inc(gu_done.sem, 1)

                for i in range(4):
                    gate_times_up(i, 0)
                with dve.Fori(0, (PAIRS - 3) // 2) as it:
                    for i in range(4, 8):
                        gate_times_up(i, it)
                for i in range(2 * PAIRS - 2, 2 * PAIRS):
                    gate_times_up(i, 0)
                add_to_h("ffn")
            dve.wait_ge(h_added.sem, h_added.at(LAYERS, 0))
            normalise(LAYERS, 0)
            dve.wait_ge(xn_done.sem, xn_done.at(LAYERS, 2))
            for t in range(TT):
                nc.vector.tensor_tensor(H[:, t, :], xn[:, t, :], gfinal, ALU.mult).then_inc(x_ready.sem, 1)

            def content2(key, l):
                dve.wait_ge(filled[banks2[key]], banks2.before(key, l) + 1)
                return bank2(key)

            def leave2(key, l, to, signal_, rows=P, width=512):
                nc.vector.tensor_copy(to, content2(key, l)[0:rows, 0:width]).then_inc(signal_.sem, 1)

            def rotate2(x, table, n, l):
                at, half = ROT[table]
                heads = x.shape[2]
                if n > 1:
                    dve.wait_ge(r_add.sem, r_add.at(l, n - 1))
                a, b = (buf[:, 0:TT * heads * 2 * half].rearrange("p (t h d) -> p t h d", t=TT, h=heads)
                        for buf in (ra, rbuf))

                def tab(which, lo, hi):
                    return rotation[which][:, :, at + lo:at + hi].unsqueeze(2).to_broadcast([P, TT, heads, hi - lo])

                nc.vector.tensor_tensor(a, x[:, :, :, 0:2 * half], tab(0, 0, 2 * half), ALU.mult)
                nc.vector.tensor_tensor(b[:, :, :, 0:half], x[:, :, :, half:2 * half], tab(1, 0, half), ALU.mult)
                nc.vector.tensor_tensor(b[:, :, :, half:2 * half], x[:, :, :, 0:half], tab(1, half, 2 * half),
                                        ALU.mult).then_inc(r_mul.sem, 1)

            with dve.Fori(0, LAYERS) as l:
                dve.sem_clear(dve_step)
                steps = [0]

                def step(ins):
                    steps[0] += 1
                    ins.then_inc(dve_step, 1)
                    dve.wait_ge(dve_step, steps[0])

                for kp in (1, 3):
                    leave2(("xT", kp), l, flat(T8[:, 2 * kp:2 * kp + 2, :]), bT_dve)

                def chunk(name):
                    at, width = COL2[name]
                    for t in range(TT):
                        leave2((name, t), l, U[:, t, at:at + width], u_dve, width=width)

                dve.wait_ge(u_act.sem, u_act.at(l, 2))
                rotate2(U[:, :, 800:1088].rearrange("p t (h d) -> p t h d", h=9), "idx", 1, l)
                chunk("A")
                dve.wait_ge(latent_sq.sem, latent_sq.at(l, 4))
                for n, width in enumerate((QR, KVR)):
                    last = nc.vector.tensor_scalar(lstat[:, 1, 2 * n:2 * n + 2], lstat[:, 0, 2 * n:2 * n + 2],
                                                   1.0 / width, EPS, ALU.mult, ALU.add)
                last.then_inc(latent_ms.sem, 1)
                rotate2(U[:, :, 384:416].unsqueeze(2), "mla", 2, l)
                dve.wait_ge(latent_rms.sem, latent_rms.at(l, 1))
                for n, (lo, hi) in enumerate(((0, 256), (256, 384))):
                    for t in range(TT):
                        last = nc.vector.tensor_scalar(U[:, t, lo:hi], U[:, t, lo:hi],
                                                       lstat[:, 2, 2 * n + t:2 * n + t + 1], None, ALU.mult)
                last.then_inc(latent_done.sem, 1)
                dve.wait_ge(u_act.sem, u_act.at(l, 4))
                rotate2(U[:, :, 416:736].rearrange("p t (h d) -> p t h d", h=5), "head", 3, l)
                chunk("q0")
                leave2(("kkT", 0), l, flat(kkT), kkT_in)
                dve.wait_ge(wi_done.sem, wi_done.at(l, 1))
                for h in range(HI):
                    if h >= 1:
                        dve.wait_ge(score_in.sem, score_in.at(l, h))
                    dve.wait_ge(relu_in.sem, relu_in.at(l, h + 1))
                    for t, (lo, hi) in enumerate(((0, P), (P, TRI))):
                        w = U[:, t, 1088 + h:1089 + h]
                        if h == 0:
                            last = nc.vector.tensor_scalar(score[:, lo:hi], relu[:, 0, lo:hi], w, None, ALU.mult)
                        else:
                            last = nc.vector.scalar_tensor_tensor(out=score[:, lo:hi], in0=relu[:, h % 2, lo:hi],
                                                                  scalar=w, in1=score[:, lo:hi], op0=ALU.mult,
                                                                  op1=ALU.add)
                    last.then_inc(score_in.sem, 1)
                for i in range(4):
                    t, half = divmod(i, 2)
                    acc = content2(("ukv", i), l).rearrange("p (h d) -> p h d", h=4)
                    nc.vector.tensor_copy(mk[:, t, half * 384:(half + 1) * 384].rearrange(
                        "p (h d) -> p h d", h=4)[:, :, 0:NOPE], acc[:, :, 0:NOPE])
                    nc.vector.tensor_copy(mvv[:, t, half * 256:(half + 1) * 256].rearrange(
                        "p (h d) -> p h d", h=4), acc[:, :, NOPE:NOPE + VM]).then_inc(mk_in.sem, 1)
                dve.wait_ge(mq_in.sem, mq_in.at(l, 4))
                rotate2(mq.rearrange("p t (h d) -> p t h d", h=HM)[:, :, :, NOPE:NOPE + ROPE], "mla", 4, l)
                chunk("k0")
                wait_apart(dve, score_masked.sem, score_masked.at(l, 1))
                tiles = ((0, P), (P, TRI))
                for _ in range(TOP_K // 8):
                    for t, (lo, hi) in enumerate(tiles):
                        last = nc.vector.max(best[:, t, :], score[:, lo:hi])
                    step(last)
                    for t, (lo, hi) in enumerate(tiles):
                        last = nc.vector.match_replace(score[:, lo:hi], best[:, t, :], score[:, lo:hi], TAKEN)
                    step(last)
                nc.vector.tensor_scalar(nm, score, TAKEN / 2, FAR, ALU.is_gt, ALU.mult).then_inc(topk_done.sem, 1)
                chunk("v0")
                dve.wait_ge(u_act.sem, u_act.at(l, 8))
                dve.wait_ge(u_dve.sem, u_dve.at(l, 6))
                rotate2(U[:, :, 1096:2632].rearrange("p t (h d) -> p t h d", h=24), "head", 5, l)
                for b in range(4):
                    leave2(("mkT", b), l, flat(mkT[0:96, 2 * b:2 * b + 2, :]), mkT_in, rows=96)
                for b in range(3):
                    leave2(("dkT", b), l, flat(dkT[:, 2 * b:2 * b + 2, :]), dkT_in)
                dve.wait_ge(nm_masked.sem, nm_masked.at(l, 1))
                for j in range(JOBS + 1):
                    if j < JOBS:
                        if j >= 2:
                            key = ("E", j - 2, parts(j - 2) - 1)
                            dve.wait_ge(filled[banks2[key]], banks2.before(key, l) + 1)
                        scale = -((NOPE + ROPE) ** -0.5) if j < HM else -(HD ** -0.5)
                        if j < HM + HX:
                            m = causal_m if j < HM else nm
                            acc = content2(("S", j, 0), l)
                            dve.sem_inc(passed, 1)
                            for t, (lo, hi) in enumerate(tiles):
                                last = nc.vector.tensor_tensor_reduce(S[:, j % 2, lo:hi], acc[:, lo:hi], m[:, lo:hi],
                                                                      scale, 3e38, ALU.add, ALU.min,
                                                                      nmx[:, j, t:t + 1])
                            last.then_inc(masked.sem, 3)
                        else:
                            for part, lo, hi, least, start in ((0, 0, 512, 2, None), (1, 512, 768, 1, 2),
                                                               (2, 768, 1152, 0, None)):
                                acc = content2(("S", j, part), l)
                                if start is not None:
                                    dve.wait_ge(masked.sem, masked.at(l, 3 * j + 1))
                                dve.sem_inc(passed, 1)
                                nc.vector.tensor_tensor_reduce(
                                    S[:, j % 2, lo:hi], acc[:, 0:hi - lo], near_m[:, lo:hi], scale,
                                    3e38 if start is None else nmx[:, j, start:start + 1], ALU.add, ALU.min,
                                    nmx[:, j, least:least + 1]).then_inc(masked.sem, 1)
                    if j >= 1:
                        i = j - 1
                        if i < HM + HX:
                            leave2(("E", i, 0), l, ET[:, i % 2, 0:TRI], ET_dve, width=TRI)
                        else:
                            leave2(("E", i, 1), l, ET[:, i % 2, 512:768], ET_dve, width=256)
                            leave2(("E", i, 2), l, ET[:, i % 2, 768:1152], ET_dve, width=TRI)
                dve.wait_ge(weighed.sem, weighed.at(l, JOBS))
                step(nc.vector.reciprocal(rinv, lsum))
                for i in range(4):
                    g8, t = divmod(i, 2)
                    nc.vector.tensor_tensor(
                        xn[:, t, g8 * 512:(g8 + 1) * 512].rearrange("p (h d) -> p h d", h=8),
                        content2(("O", i), l).rearrange("p (h d) -> p h d", h=8),
                        rinv[:, 8 * g8:8 * g8 + 8, t:t + 1].to_broadcast([P, 8, HD]), ALU.mult).then_inc(mix_done.sem, 1)
                for kp in (1, 3):
                    leave2(("oT", kp), l, flat(T8[:, 2 * kp:2 * kp + 2, :]), bT_dve)
                for i in range(4):
                    t, cols = i // 2, slice(i % 2 * 512, (i % 2 + 1) * 512)
                    nc.vector.scalar_tensor_tensor(out=H[:, t, cols], in0=H[:, t, cols], scalar=ALPHA,
                                                   in1=content2(("wo", i), l), op0=ALU.mult,
                                                   op1=ALU.add).then_inc(wo_in.sem, 1)

                def layer_norm(buf, n):
                    for t in range(TT):
                        for a in range(2):
                            last = nc.vector.bn_stats(moments2[:, t, a, :], buf[:, t, a * 512:(a + 1) * 512])
                    step(last)
                    for t in range(TT):
                        last = nc.vector.bn_aggr(mv2[:, t, :], moments2[:, t, :, :])
                    last.then_inc(stat_done.sem, 1)
                    dve.wait_ge(rstd_done.sem, rstd_done.at(l, n + 1))
                    for t in range(TT):
                        step(nc.vector.tensor_scalar(H[:, t, :], buf[:, t, :], mv2[:, t, 0:1], rstd2[:, t:t + 1],
                                                     ALU.subtract, ALU.mult))
                        nc.vector.tensor_tensor(H[:, t, :], H[:, t, :], lng[:, 2 * n, :],
                                                ALU.mult).then_inc(gained.sem, 1)

                dve.wait_ge(wo_in.sem, wo_in.at(l, 4))
                layer_norm(H, 0)
                for kp in (1, 3):
                    leave2(("xT2", kp), l, flat(T8[:, 2 * kp:2 * kp + 2, :]), bT_dve)

                acc = content2(("router", 0), l)[:, 0:128].rearrange("p (t n) -> p t n", t=TT)
                nc.vector.tensor_tensor(logit, acc[:, :, 0:36], rb.unsqueeze(1).to_broadcast([P, TT, 36]),
                                        ALU.add).then_inc(logit_in.sem, 1)
                dve.wait_ge(logit_in.sem, logit_in.at(l, 1))
                step(nc.vector.tensor_reduce(hot_max, logit[:, :, 0:GROUPS], AX_X, ALU.max))
                nc.vector.tensor_tensor(shifted, logit[:, :, 0:GROUPS],
                                        hot_max.unsqueeze(2).to_broadcast([P, TT, GROUPS]),
                                        ALU.subtract).then_inc(shift_done.sem, 1)
                dve.wait_ge(shift_done.sem, shift_done.at(l, 1))
                step(nc.vector.tensor_scalar(eq, shifted, 0.0, None, ALU.is_ge))
                for t in range(TT):
                    last = nc.vector.tensor_tensor_scan(prefix[:, t, :], ones[:, 0:GROUPS], eq[:, t, :], 0.0,
                                                        ALU.mult, ALU.add)
                step(last)
                nc.vector.scalar_tensor_tensor(out=hot, in0=prefix, scalar=1.0, in1=eq, op0=ALU.is_equal,
                                               op1=ALU.mult).then_inc(hot_done.sem, 1)
                dve.wait_ge(hot_done.sem, hot_done.at(l, 1))
                step(nc.vector.tensor_tensor(sel4, logit[:, :, GROUPS:36].rearrange("p t (g e) -> p t e g", g=GROUPS),
                                             hot.unsqueeze(2).to_broadcast([P, TT, EXPERTS, GROUPS]), ALU.mult))
                step(nc.vector.tensor_reduce(sel, sel4, AX_X, ALU.add))
                for t in range(TT):
                    last = nc.vector.max(top[:, t, :], sel[:, t, :])
                step(last)
                nc.vector.tensor_tensor(diff[:, 0, :], top[:, :, 1], top[:, :, 0],
                                        ALU.subtract).then_inc(diff_done.sem, 1)
                acc = content2(("ranks", 0), l)
                step(nc.vector.tensor_tensor(crank, acc[:, 0:8].rearrange("p (t g) -> p t g", t=TT), hot, ALU.mult))
                nc.vector.tensor_reduce(rank, crank, AX_X, ALU.add).then_inc(rank_ready.sem, 1)
                step(nc.vector.tensor_reduce(npass_f[:, 0:1], acc[:, 8:12], AX_X, ALU.max))
                step(nc.vector.tensor_scalar(npass_f[:, 1:2], npass_f[:, 0:1], SLOTS + 0.5, 1.0, ALU.is_gt, ALU.add))
                nc.vector.tensor_copy(npass, npass_f[:, 1:2]).then_inc(npass_done.sem, 1)
                for t in range(TT):
                    last = nc.vector.max_index(topi[:, t, :], top[:, t, :], sel[:, t, :])
                step(last)
                step(nc.vector.tensor_copy(topf, topi))
                dve.wait_ge(gexp_done.sem, gexp_done.at(l, 1))
                dve.wait_ge(eexp_done.sem, eexp_done.at(l, 1))
                step(nc.vector.tensor_reduce(ptop[:, 0, :], gexp, AX_X, ALU.add))
                step(nc.vector.tensor_scalar(diff[:, 2, :], diff[:, 1, :], 1.0, None, ALU.add))
                step(nc.vector.reciprocal(ptop[:, 1, :], ptop[:, 0, :]))
                step(nc.vector.reciprocal(ptop[:, 0, :], diff[:, 2, :]))
                step(nc.vector.tensor_tensor(ptop[:, 2, :], ptop[:, 0, :], ptop[:, 1, :], ALU.mult))
                step(nc.vector.tensor_tensor(ptop[:, 3, :], ptop[:, 2, :], diff[:, 1, :], ALU.mult))
                for t in range(TT):
                    nc.vector.tensor_scalar(ge[:, t, :], iota[:, 0:EXPERTS], topf[:, t, 0:1], ptop[:, 2, t:t + 1],
                                            ALU.is_equal, ALU.mult)
                    last = nc.vector.tensor_scalar(ge2[:, t, :], iota[:, 0:EXPERTS], topf[:, t, 1:2],
                                                   ptop[:, 3, t:t + 1], ALU.is_equal, ALU.mult)
                step(last)
                step(nc.vector.tensor_tensor(ge, ge, ge2, ALU.add))
                step(nc.vector.tensor_tensor(gate, ge.unsqueeze(2).to_broadcast([P, TT, GROUPS, EXPERTS]),
                                             hot.unsqueeze(3).to_broadcast([P, TT, GROUPS, EXPERTS]), ALU.mult))
                dve.wait_ge(npass_done.sem, npass_done.at(l, 1))
                passes = dve.value_load(npass[0:1, 0:1], min_val=1, max_val=2)
                with dve.Fori(0, 2) as ps_:
                    lp = l * 2 + ps_

                    def content_p(g, name, *key):
                        dve.wait_ge(filled[banks2[(name, 0) + key]], pass_turn(name, key, l, ps_, g) + 1)
                        return bank2((name, 0) + key)

                    with dve.If(passes > ps_):
                        dve.wait_ge(rank_ready.sem, rank_ready.at(l, 1) + ps_)
                        for g in range(GROUPS):
                            for t in range(TT):
                                last = nc.vector.tensor_scalar(pick[:, g, t, :], iota, rank[:, t:t + 1],
                                                               hot[:, t, g:g + 1], ALU.is_equal, ALU.mult)
                        last.then_inc(pick_done.sem, 1)
                        nc.vector.tensor_copy(flat(pickT[:, 2:4, :]), content_p(0, "pT", 1)).then_inc(pickT_in.sem, 1)
                        nc.vector.tensor_copy(gslot, content_p(0, "slots")[:, 0:GROUPS * EXPERTS]).then_inc(
                            gslot_in.sem, 1)
                        with dve.Fori(0, GROUPS) as g:
                            nc.vector.tensor_copy(flat(XG[:, 4:8, :]), content_p(g, "xg", 0, 1)).then_inc(xg_dve.sem, 1)
                            if True:
                                dve.wait_ge(gslot_in.sem, gslot_in.at(lp, 1))
                            for e in range(EXPERTS):
                                acc = content_p(g, "gu", 0, e)
                                dve.wait_ge(g2_silu.sem, g2_silu.at(lp, e + 1) + g * EXPERTS)
                                nc.vector.scalar_tensor_tensor(out=hh[:, e % 2, :], in0=sg[:, e % 2, :],
                                                               scalar=gslot[:, bass.ds(g * EXPERTS + e, 1)],
                                                               in1=acc[:, EH:2 * EH], op0=ALU.mult,
                                                               op1=ALU.mult).then_inc(h2_done.sem, 1)
                        dve.wait_ge(resid_in.sem, resid_in.at(l, TT))
                        for i in range(4):
                            t, cols = i // 2, slice(i % 2 * 512, (i % 2 + 1) * 512)
                            nc.vector.tensor_tensor(xn[:, t, cols], content_p(0, "sc", i), xn[:, t, cols],
                                                    ALU.add).then_inc(sc_added.sem, 1)
                        nc.vector.tensor_scalar(rank, rank, -float(SLOTS), None, ALU.add).then_inc(rank_ready.sem, 1)
                    with dve.Else():
                        dve.drain()
                        for signal_, n in ((pick_done, 1), (pickT_in, 1), (gslot_in, 1), (xg_dve, GROUPS),
                                           (h2_done, GROUPS * EXPERTS), (sc_added, 4), (rank_ready, 1)):
                            dve.sem_inc(signal_.sem, n)
                dve.wait_ge(sc_added.sem, sc_added.at(2 * l + 1, 4))
                layer_norm(xn, 1)

        @block.gpsimd
        def _(pool):
            def inverse_rms(l, n):
                pool.wait_ge(meansq.sem, meansq.at(l, n + 1))
                nc.gpsimd.tensor_tensor(stat[:, 4:6], stat[:, 2:4], minus_half[:, 0:2], ALU.pow).then_inc(rms.sem, 1)

            def causal(h, wait, signal_, l):
                wait_apart(pool, wait.sem, wait.at(l, h + 1))
                blocks = sp[:, h, :].rearrange("p (a n) -> p a n", n=P)[:, 0:3:2, :]
                nc.gpsimd.affine_select(out=blocks, in_=blocks, pattern=[[0, 2], [1, P]], compare_op=ALU.is_gt,
                                        fill=0.0, base=0, channel_multiplier=-1).then_inc(signal_.sem, 1)

            pool.wait_ge(const_set, 1)
            with pool.Fori(0, LAYERS) as l:
                pool.sem_clear(pool_step)
                inverse_rms(l, 0)
                for which in range(2):
                    for t in range(TT):
                        pool.wait_ge(rotated.sem, rotated.at(l, 2 * which + t + 1))
                        nc.gpsimd.tensor_tensor(qk[:, which, t, :], qk[:, which, t, :], rot[:, t, :],
                                                ALU.add).then_inc(roped.sem, 1)
                for h in range(HS):
                    causal(h, sp_done, sp_masked, l)
                for h in range(HR):
                    wait_apart(pool, head_var.sem, head_var.at(l, h + 1))
                    nc.gpsimd.tensor_scalar(rstd[:, h, :], mv[:, h, :, 1], EPS, None, ALU.add).then_inc(pool_step, 1)
                    pool.wait_ge(pool_step, h + 1)
                    nc.gpsimd.tensor_tensor(rstd[:, h, :], rstd[:, h, :], minus_half[:, 0:2],
                                            ALU.pow).then_inc(head_rstd.sem, 1)
                for h in range(HS):
                    causal(h, w_exp, w_masked, l)
                for i in range(4):
                    t, cols = i // 2, slice(i % 2 * 512, (i % 2 + 1) * 512)
                    pool.wait_ge(ret_out.sem, ret_out.at(l, i + 1))
                    pool.wait_ge(sb_gated.sem, sb_gated.at(l, i + 1))
                    nc.gpsimd.tensor_tensor(xn[:, t, cols], xn[:, t, cols], gs[:, t, cols],
                                            ALU.add).then_inc(merged.sem, 1)
                inverse_rms(l, 1)
            inverse_rms(LAYERS, 0)

            def add_rotation(x, n, half, l):
                heads = x.shape[2]
                a, b = (buf[:, 0:TT * heads * 2 * half].rearrange("p (t h d) -> p t h d", t=TT, h=heads)
                        for buf in (ra, rbuf))
                pool.wait_ge(r_mul.sem, r_mul.at(l, n))
                nc.gpsimd.tensor_tensor(x[:, :, :, 0:2 * half], a, b, ALU.add).then_inc(r_add.sem, 1)
                wait_apart(pool, r_add.sem, r_add.at(l, n))

            def diagonal(buf, signal_):
                blocks = buf.rearrange("p (a n) -> p a n", n=P)[:, 0:3:2, :]
                nc.gpsimd.affine_select(out=blocks, in_=blocks, pattern=[[0, 2], [-1, P]], compare_op=ALU.is_ge,
                                        fill=FAR, base=0, channel_multiplier=1).then_inc(signal_.sem, 1)

            def both(a, b):
                return U[:, :, a:b]

            with pool.Fori(0, LAYERS) as l:
                add_rotation(both(800, 1088).rearrange("p t (h d) -> p t h d", h=9), 1, 4, l)
                nc.gpsimd.tensor_copy(ki4.rearrange("p t (a d) -> p t a d", a=4),
                                      both(1056, 1088).unsqueeze(2).to_broadcast([P, TT, 4, DI])).then_inc(kcopy.sem, 1)
                nc.gpsimd.tensor_scalar(both(1088, 1096), both(1088, 1096), DI ** -0.5 * HI ** -0.5, None,
                                        ALU.mult).then_inc(wi_done.sem, 1)
                pool.wait_ge(latent_ms.sem, latent_ms.at(l, 1))
                nc.gpsimd.tensor_tensor(lstat[:, 2, :], lstat[:, 1, :], minus_half[:], ALU.pow).then_inc(
                    latent_rms.sem, 1)
                add_rotation(both(384, 416).unsqueeze(2), 2, 16, l)
                nc.gpsimd.tensor_copy(mk.rearrange("p t (h d) -> p t h d", h=HM)[:, :, :, NOPE:NOPE + ROPE],
                                      both(384, 416).unsqueeze(2).to_broadcast([P, TT, HM, ROPE])).then_inc(
                                          kcopy.sem, 1)
                add_rotation(both(416, 736).rearrange("p t (h d) -> p t h d", h=5), 3, 8, l)
                nc.gpsimd.tensor_copy(kk.rearrange("p t (a d) -> p t a d", a=2),
                                      both(672, 736).unsqueeze(2).to_broadcast([P, TT, 2, HD])).then_inc(kcopy.sem, 1)
                wait_apart(pool, score_in.sem, score_in.at(l, HI))
                diagonal(score, score_masked)
                add_rotation(mq.rearrange("p t (h d) -> p t h d", h=HM)[:, :, :, NOPE:NOPE + ROPE], 4, 16, l)
                wait_apart(pool, topk_done.sem, topk_done.at(l, 1))
                diagonal(nm, nm_masked)
                add_rotation(both(1096, 2632).rearrange("p t (h d) -> p t h d", h=24), 5, 8, l)
                for n in range(2):
                    wait_apart(pool, stat_done.sem, stat_done.at(l, n + 1))
                    nc.gpsimd.tensor_scalar(rstd2, mv2[:, :, 1], LN_EPS, None, ALU.add).then_inc(ln_step, 1)
                    pool.wait_ge(ln_step, n + 1)
                    nc.gpsimd.tensor_tensor(rstd2, rstd2, minus_half[:, 0:2], ALU.pow).then_inc(rstd_done.sem, 1)
                    for t in range(TT):
                        pool.wait_ge(gained.sem, gained.at(l, 2 * n + t + 1))
                        nc.gpsimd.tensor_tensor(H[:, t, :], H[:, t, :], lng[:, 2 * n + 1, :],
                                                ALU.add).then_inc(x_ready.sem, 1)
                pool.sem_clear(ln_step)


N_CONST = 8
N_PARAMS = 17
SLOTS = P
PASS_KEYS = ("pT", "slots", "xg", "gu", "hT", "yg", "sc")
ARENA = 32900


def kernel(**inputs):
    from concourse import bacc
    from concourse.bass_utils import run_bass_kernel_spmd

    nc = bacc.Bacc("TRN2", target_bir_lowering=False, num_devices=1)
    arrays = {name: np.ascontiguousarray(a) for name, a in inputs.items()}
    arrays.update(constants())
    src = {name: nc.dram_tensor(f"in_{name}", a.shape, mybir.dt.from_np(a.dtype), kind="ExternalInput").ap()
           for name, a in arrays.items()}
    out = nc.dram_tensor("out", (1, SEQ, D), F32, kind="ExternalOutput").ap()
    build(nc, src, out)
    r = run_bass_kernel_spmd(nc, [{f"in_{name}": a for name, a in arrays.items()}], core_ids=[0])
    return r.results[0]["out"]
```

```python
from contextlib import ExitStack

import concourse.bass as bass
import numpy as np
from concourse import mybir

F32 = mybir.dt.float32
F32R = mybir.dt.float32r
I32 = mybir.dt.int32
U32 = mybir.dt.uint32
ALU = mybir.AluOpType
ACT = mybir.ActivationFunctionType
AX_X = mybir.AxisListType.X

P = 128
LAYERS = 2
SEQ = 256
TT = SEQ // P
D = 1024
KT = D // P
BANKS = 8
RING = 6
HIGH = 3
TRIPLES = 3
EXPERT_SLOTS = 3 * TRIPLES
KINDS = ("gate", "up", "down")
UNIT = 2048
EPS = 1e-6
LN_EPS = 1e-5

HR, DK, DV = 4, 128, 256
HS, DS = 8, 64
FF = 2816
PAIRS = FF // (2 * P)
IN_COLS = 6656
CHUNK = 512
CHUNKS = [("rq", 0), ("rk", 512), ("sq", 3072), ("sk", 3584), ("rv0", 1024), ("rv1", 1536), ("sv", 4096),
          ("rg0", 2048), ("rg1", 2560), ("gr0", 4608), ("gr1", 5120), ("gs0", 5632), ("gs1", 6144)]
TRI = SEQ + P


HM, NOPE, ROPE, VM = 8, 64, 32, 64
QR, KVR = 256, 128
HD = 64
HI, DI = 8, 32
HX = 4
TOP_K = 64
DILATED = ((128, 1), (512, 4), (2048, 16))
GROUPS, EXPERTS, EH = 4, 8, 256
ALPHA = (2.0 * LAYERS) ** 0.25
FAR = -1e30
TAKEN = -3e38
UCOLS = 3400
CHUNKS2 = [("C", 800, 296), ("A", 0, 416), ("B", 416, 384), ("q0", 1096, 384), ("q1", 1480, 384),
           ("k0", 1864, 384), ("k1", 2248, 384), ("v0", 2632, 384), ("v1", 3016, 384)]
COL2 = {name: (at, width) for name, at, width in CHUNKS2}
BY_ACT = ("C", "B", "q1", "k1", "v1")
JOBS = HM + HX + HX
ROT = {"mla": (0, 16), "head": (32, 8), "idx": (48, 4)}
ROT_COLS = 56
MAGIC = 1.5 * 2.0 ** 23


class Turns:

    def __init__(self, seq, after=None):
        self.start = {} if after is None else {r: after.end(r) for r in set(after.start) | set(after.per)}
        self.per, self.place = {}, {}
        for key, r in seq:
            self.place[key] = (r, self.per.get(r, 0))
            self.per[r] = self.per.get(r, 0) + 1

    def end(self, r):
        return self.start.get(r, 0) + LAYERS * self.per.get(r, 0)

    def __getitem__(self, key):
        return self.place[key][0]

    def before(self, key, layer, more=0):
        r, n = self.place[key]
        return layer * self.per[r] + (self.start.get(r, 0) + n) + more

    def stride(self, key, later):
        assert self.place[key][0] == self.place[later][0]
        return self.place[later][1] - self.place[key][1]


class Signal:

    def __init__(self, sem, per, start=0):
        self.sem, self.per, self.start = sem, per, start

    def at(self, layer, k):
        return layer * self.per + (self.start + k)


def mixer_banks():
    seq = [("nT", kp) for kp in range(4)]
    for c in ("rq", "rk"):
        seq += [(c, t) for t in range(TT)]
    seq += [("sq", 0), ("sq", 1), ("sk", 0), ("sk", 1), ("rv0", 0), ("rv0", 1)]
    seq += [("qT", 0), ("qT", 1), ("kT", 0), ("kT", 1), ("rv1", 0), ("rv1", 1)]
    seq += [("rs", h) for h in range(HR)] + [("z", h) for h in range(HS)] + [("sv", 0), ("sv", 1)]
    seq += [("rg0", 0), ("rg0", 1)] + [("ro", h) for h in range(HR)] + [("rg1", 0), ("rg1", 1)]
    seq += [("c", h) for h in range(HS)] + [("gr0", 0), ("gr0", 1), ("gr1", 0), ("gr1", 1)]
    seq += [("so", h) for h in range(HS // 2)] + [("gs0", 0), ("gs0", 1), ("gs1", 0), ("gs1", 1)]
    seq += [("rT", kp) for kp in range(4)] + [("ret", i) for i in range(4)] + [("sb", i) for i in range(4)]
    seq += [("mT", kp) for kp in range(4)] + [("wo", i) for i in range(4)]
    out = [(key, n % BANKS) for n, key in enumerate(seq)]
    out += [(("nT2", kp), 4 + kp) for kp in range(4)]
    out += [(("ffn", i), i) for i in range(4)]
    out += [(("gu", i), 4 + i % 4) for i in range(2 * PAIRS)]
    return Turns(out)


def mixer_units():
    seq = [(c, half) for c, _ in CHUNKS for half in range(2)]
    seq += [("w_ret_o", u) for u in range(4)] + [("w_sb_o", u) for u in range(2)] + [("w_out", u) for u in range(4)]
    for p in range(PAIRS):
        seq += [("gate", p), ("up", p)] + ([("down", p - 1)] if p > 0 else [])
    seq += [("down", PAIRS - 1)]
    return Turns([(key, n % RING) for n, key in enumerate(seq)])


def attention_banks(after):
    seq = [("xT", kp) for kp in range(4)]
    for c in ("C", "A", "B", "q0"):
        seq += [(c, t) for t in range(TT)]
    seq += [("qiT", 0), ("kkT", 0), ("cT", 0), ("cT", 1), ("q1", 0), ("q1", 1)]
    seq += [("rel", h) for h in range(HI)]
    seq += [("uq", i) for i in range(4)] + [("ukv", i) for i in range(4)]
    seq += [("k0", 0), ("k0", 1), ("k1", 0), ("k1", 1), ("v0", 0), ("v0", 1)]
    seq += [("mqT", b) for b in range(4)] + [("mkT", b) for b in range(4)]
    seq += [("v1", 0), ("v1", 1), ("dsT", 0)] + [("dqT", b) for b in range(3)] + [("dkT", b) for b in range(3)]
    out = [(key, n % BANKS) for n, key in enumerate(seq)]
    out += [(("O", i), i) for i in range(4)]
    n = 0
    for j in range(JOBS + 1):
        for what, i in (("S", j), ("E", j - 1)):
            for part in range(parts(i)):
                out.append(((what, i, part), 4 + n % 4))
                n += 1
    out += [(("oT", kp), 4 + kp) for kp in range(4)] + [(("wo", i), i) for i in range(4)]
    out += [(("xT2", kp), 4 + kp) for kp in range(4)] + [(("router", 0), 0), (("ranks", 0), 1)]
    for pass_ in range(2):
        out += [(("pT", pass_, 0), 2), (("pT", pass_, 1), 3), (("slots", pass_), 1)]
        for g in range(GROUPS):
            out += [(("xg", pass_, g, b), 2 + b) for b in range(2)]
            for e in range(EXPERTS):
                out += [(("gu", pass_, g, e), 4 + e % 2), (("hT", pass_, g, e), 6 + e % 2)]
            out += [(("yg", pass_, g, half), half) for half in range(2)]
        out += [(("sc", pass_, i), i) for i in range(4)]
    return Turns(out, after)


def parts(j):
    return 0 if not 0 <= j < JOBS else 3 if j >= HM + HX else 1


def attention_units(after):
    order = ["C", "A", "B", "q0", "q1", "uq", "ukv", "k0", "k1", "v0", "v1"]
    seq = [(c, half) for c in order for half in range(1 if c in ("uq", "ukv") else 2)]
    seq += [("w_o_2", u) for u in range(4)]
    assert len(seq) % RING == 0
    out = [(key, n % RING) for n, key in enumerate(seq)]
    for pass_ in range(2):
        for g in range(GROUPS):
            for e in range(EXPERTS):
                out += [((w, pass_, g, e), 3 * (e % TRIPLES) + n) for n, w in enumerate(KINDS)]
    return Turns(out, after)


def constants():
    i = np.arange(P)
    pos = np.arange(SEQ, dtype=np.float32)
    half = DK // 2
    inv = (1.0 / (np.float32(10000.0) ** (np.arange(half, dtype=np.float32) / np.float32(half)))).astype(np.float32)
    ang = (pos[:, None] * inv[None, :]).astype(np.float32)
    cos, sin = np.cos(ang).astype(np.float32), np.sin(ang).astype(np.float32)
    rope = np.concatenate([cos, cos, -sin, sin], 1).reshape(TT, P, 4 * half).transpose(1, 0, 2)
    log_g = np.log1p(-np.exp2(-5.0 - np.arange(HR)))
    decay = np.zeros((P, HR, TRI))
    for h in range(HR):
        for j0, i0, n, at in ((0, 0, SEQ, 0), (P, P, P, SEQ)):
            diff = (i0 + np.arange(n))[None, :] - (j0 + i)[:, None]
            decay[:, h, at:at + n] = np.where(diff >= 0, np.exp(log_g[h] * np.maximum(diff, 0)), 0.0) * DK ** -0.5
    f = lambda a: np.ascontiguousarray(a, np.float32)
    freq, sign = [], []
    for _, half in ROT.values():
        f_ = 500000.0 ** (-np.arange(0, 2 * half, 2) / (2.0 * half))
        freq += [f_, f_]
        sign += [-np.ones(half), np.ones(half)]
    q, k = np.arange(SEQ)[:, None], np.arange(SEQ)[None, :]
    causal = np.where(k <= q, 0.0, FAR)
    near = [np.where((q >= k) & ((q - k) % d == 0) & (q - k <= w), 0.0, FAR) for w, d in DILATED]
    return {
        "c_freq": np.tile(np.concatenate(freq).astype(np.float32), (P, 1)),
        "c_sign": f(np.tile(np.concatenate(sign), (P, 1))),
        "c_causal": f(np.concatenate([causal[:P, :P], causal[P:, :]], 1)),
        "c_near": f(np.concatenate([m[P:, :] for m in near] + [m[:P, :P] for m in near], 1)),
        "c_before": f(i[:, None] < i[None, :]),
        "c_iota": f(np.tile(i, (P, 1))),
        "c_ident": f(np.eye(P)),
        "c_suffix": f(i[:, None] >= i[None, :]),
        "c_rope": f(rope),
        "c_decay": f(decay),
    }


def build(nc, src, out, debug=None):
    banks = mixer_banks()
    units = mixer_units()
    banks2 = attention_banks(banks)
    units2 = attention_units(units)
    ctx = ExitStack()
    with ctx:
        def sb(name, shape, dt=F32):
            return ctx.enter_context(nc.sbuf_tensor(name, shape, dt))

        def sem(name):
            return ctx.enter_context(nc.semaphore(name))

        def signal(name, per, start=0):
            return Signal(sem(name), per, start)

        ps = ctx.enter_context(nc.psum_tensor("ps", [P, BANKS, 512], F32))
        twins = []

        def sb_split(name, shape):
            at = -(-nc.sbuf_base // 32) * 32
            return sb(name, shape), at

        def twin(tensor, at, first, n):
            name = f"split{len(twins)}"
            twins.append((tensor.name, first, n,
                          nc.alloc_sbuf_tensor_at(name, [P, n], F32R, offset=at + 4 * first)))

        def split(view):
            for name, first, n, of in twins:
                if name == view.tensor.name and first <= view.offset < first + n:
                    return bass.AP(of, view.offset - first, [[n, P]] + [list(d) for d in view.ap][1:])
            assert view.tensor.dtype == F32R
            return view

        ring, at = sb_split("ring", [P, RING, UNIT])
        twin(ring, at, 0, RING * UNIT)
        ident = sb("ident", [P, P])
        suffix = sb("suffix", [P, P])
        ones = sb("ones", [P, P])
        minus_half = sb("minus_half", [P, 4])
        lstat = sb("lstat", [P, 3, 4])
        H = sb("H", [P, TT, D])
        xn, at = sb_split("xn", [P, TT, D])
        twin(xn, at, 0, TT * D)
        T8, at = sb_split("T8", [P, KT, SEQ])
        twin(T8, at, 0, KT * SEQ)
        T8low = xn.rearrange("p t (k n) -> p (t k) n", n=SEQ)
        high = sb("high", [P, HIGH, UNIT], F32R)
        gains = sb("gains", [P, 2, KT])
        stat = sb("stat", [P, 8])
        freq = sb("freq", [P, 2, ROT_COLS])
        pos_i = sb("pos_i", [P, TT], I32)
        pos = sb("pos", [P, TT])
        rope2 = sb("rope2", [P, 2, TT, ROT_COLS])
        turns_ = sb("turns", [P, 3, TT, ROT_COLS])
        rotation = [rope2[:, i] for i in range(2)]
        arena, arena_base = sb_split("arena", [P, ARENA])

        def twin_of(*buffers):
            first = buffers[0].offset
            end = buffers[-1].offset + int(np.prod(buffers[-1].shape[1:]))
            twin(arena, arena_base, first, end - first)


        def carver():
            at = [0]

            def carve(*shape):
                n = int(np.prod(shape))
                at[0] = -(-at[0] // 8) * 8
                view = arena[:, at[0]:at[0] + n]
                at[0] += n
                assert at[0] <= ARENA, at[0]
                names = "abc"[:len(shape)]
                if len(shape) == 1:
                    return view
                return view.rearrange(f"p ({' '.join(names)}) -> p {' '.join(names)}",
                                      **{names[i]: shape[i] for i in range(len(shape))})
            return carve, at

        carve, _ = carver()
        rot_flat = carve(1024)
        qkT_flat = carve(2 * HR * SEQ)
        ST_flat = carve(HR * TRI)
        z_flat = carve(HS * TRI)
        for buf in (rot_flat, qkT_flat, ST_flat, z_flat):
            twin_of(buf)
        gfinal = carve(D)
        rope1 = carve(TT, 256)
        decay = carve(HR, TRI)
        qk_flat = carve(4 * 512)
        qk = qk_flat.rearrange("p (a t n) -> p a t n", a=2, t=TT)
        retn = qk_flat.rearrange("p (t n) -> p t n", t=TT)
        rot = rot_flat.rearrange("p (a n) -> p a n", a=2)
        lnt = rot_flat[:, 0:2 * TRI].rearrange("p (a n) -> p a n", a=2)
        sbTlow = rot_flat.rearrange("p (a n) -> p a n", n=SEQ)
        qT, kT = (qkT_flat[:, i * 1024:(i + 1) * 1024].rearrange("p (a n) -> p a n", n=SEQ) for i in range(2))
        retT = qkT_flat.rearrange("p (a n) -> p a n", n=SEQ)
        rv = carve(TT, D)
        sqT = carve(HS // 2, SEQ)
        skT = carve(HS // 2, SEQ)
        sv = carve(TT, HS * DS)
        rg = carve(TT, D)
        gr = carve(TT, D)
        gs = carve(TT, D)
        ST = ST_flat.rearrange("p (a n) -> p a n", n=TRI)
        sbT = ST_flat[:, 0:1024].rearrange("p (a n) -> p a n", n=SEQ)
        z = z_flat.rearrange("p (a n) -> p a n", n=TRI)
        retTlow = z_flat[:, 0:2048].rearrange("p (a n) -> p a n", n=SEQ)
        sp = carve(HS, TRI)
        moments_flat = carve(HR * TT * 6)
        moments = moments_flat.rearrange("p (h t n) -> p h t n", h=HR, t=TT)
        mv_flat = carve(HR * TT * 2)
        mv = mv_flat.rearrange("p (h t n) -> p h t n", h=HR, t=TT)
        rstd = carve(HR, TT)
        silu_g = retT[:, 0:4, :]
        guT = retT[:, 4:8, :]
        guTlow = retTlow[:, 0:4, :]
        gu_full = retTlow[:, 4:8, :]

        carve, arena_at = carver()
        lng = carve(2, D)
        cgain = carve(4)
        rw = carve(KT, GROUPS + GROUPS * EXPERTS)
        rb = carve(GROUPS + GROUPS * EXPERTS)
        causal_m = carve(TRI)
        near_m = carve(3 * TRI)
        before = carve(P)
        iota = carve(P)
        moments2_flat = carve(TT * 2 * 6)
        moments2 = moments2_flat.rearrange("p (t a n) -> p t a n", t=TT, a=2)
        mv2 = carve(TT, 2)
        rstd2 = carve(TT)
        moe_at = arena_at[0]
        U = carve(TT, UCOLS)
        mqk = carve(2 * TT * HM * (NOPE + ROPE))
        mq, mk = (mqk[:, i * 1536:(i + 1) * 1536].rearrange("p (t n) -> p t n", t=TT) for i in range(2))
        mvv = carve(TT, HM * VM)
        mqT = carve(HM, SEQ)
        mkT = carve(HM, SEQ)
        dqT = carve(6, SEQ)
        dkT_flat = carve(6 * SEQ)
        dkT = dkT_flat.rearrange("p (a n) -> p a n", n=SEQ)
        cT = dkT_flat[:, 0:3 * SEQ].rearrange("p (a n) -> p a n", n=SEQ)
        dsT = carve(2, SEQ)
        kkT = carve(2, SEQ)
        qiT = carve(2, SEQ)
        before_jobs = carve(2 * 256 + 2 * 768 + 2 * TRI)
        kk = before_jobs[:, 0:256].rearrange("p (t n) -> p t n", t=TT)
        ki4 = before_jobs[:, 256:512].rearrange("p (t n) -> p t n", t=TT)
        ra = before_jobs[:, 512:1280]
        rbuf = before_jobs[:, 1280:2048]
        relu = before_jobs[:, 2048:2816].rearrange("p (a n) -> p a n", a=2)
        score = carve(TRI)
        nm = carve(TRI)
        best = carve(TT, 8)
        S = mqk[:, 0:6 * TRI].rearrange("p (a n) -> p a n", a=2)
        ET = before_jobs[:, 0:6 * TRI].rearrange("p (a n) -> p a n", a=2)
        rows_ = before_jobs[:, 6 * TRI:6 * TRI + 8 * JOBS]
        nmx = rows_[:, 0:4 * JOBS].rearrange("p (j n) -> p j n", n=4)
        lsum = rows_[:, 4 * JOBS:6 * JOBS].rearrange("p (j t) -> p j t", t=TT)
        rinv = rows_[:, 6 * JOBS:8 * JOBS].rearrange("p (j t) -> p j t", t=TT)

        arena_at[0] = moe_at
        logit = carve(TT, 36)
        hot_max = carve(TT)
        shifted = carve(TT, GROUPS)
        eq = carve(TT, GROUPS)
        prefix = carve(TT, GROUPS)
        hot = carve(TT, GROUPS)
        gexp = carve(TT, GROUPS)
        ptop = carve(4, TT)
        sel_flat = carve(TT * EXPERTS * GROUPS)
        sel4 = sel_flat.rearrange("p (t e g) -> p t e g", t=TT, e=EXPERTS)
        sel = carve(TT, EXPERTS)
        top = carve(TT, 8)
        topi = carve(TT, 8).bitcast(U32)
        topf = carve(TT, 8)
        diff = carve(3, TT)
        ge = carve(TT, EXPERTS)
        ge2 = carve(TT, EXPERTS)
        gate_flat = carve(TT * GROUPS * EXPERTS)
        gate = gate_flat.rearrange("p (t g e) -> p t g e", t=TT, g=GROUPS)
        crank = carve(TT, GROUPS)
        rank = carve(TT)
        npass_f = carve(2)
        npass = carve(1).bitcast(I32)
        pick_flat = carve(GROUPS * TT * P)
        pick = pick_flat.rearrange("p (g t n) -> p g t n", g=GROUPS, t=TT)
        pickT = carve(GROUPS, SEQ)
        gslot = carve(GROUPS * EXPERTS)
        YG = carve(GROUPS, D)
        XG = carve(KT, P)
        XGlow = carve(KT, P)
        more_slots = carve(EXPERT_SLOTS - RING, UNIT)
        ehigh = [high[:, 0:2, :], carve(2, UNIT)]
        assert XG.offset >= z_flat.offset + HS * TRI
        twin_of(XG, XGlow, more_slots, ehigh[1])
        sg = carve(2, EH)
        hh = carve(2, EH)
        hT = carve(2, 2 * P)

        filled = [sem(f"filled{b}") for b in range(BANKS)]
        landed = [sem(f"landed{s}") for s in range(EXPERT_SLOTS)]
        unit_read = signal("unit_read", len(CHUNKS) + 3 + 1 + 3 + 2 * PAIRS - 1)
        high_done = signal("high_done", len(units.place))
        low_done = signal("low_done", len(units.place))
        first_in = sem("first_in")
        const_in = sem("const_in")
        x_in = sem("x_in")
        out_done = sem("out_done")
        const_set = sem("const_set")
        dve_step = sem("dve_step")
        act_step = sem("act_step")
        pool_step = sem("pool_step")
        h_added = signal("h_added", 8, 3)
        sumsq = signal("sumsq", 4)
        gains_in = signal("gains_in", 32)
        meansq = signal("meansq", 2)
        rms = signal("rms", 2)
        xn_done = signal("xn_done", 4)
        nT_act = signal("nT_act", 16)
        nT_dve = signal("nT_dve", 16)
        rotated = signal("rotated", 4)
        roped = signal("roped", 4)
        qT_in = signal("qT_in", 2)
        kT_in = signal("kT_in", 2)
        sqk_in = signal("sqk_in", 4)
        rv_in = signal("rv_in", 4)
        sv_in = signal("sv_in", 2)
        st_in = signal("st_in", HR)
        z_in = signal("z_in", HS)
        negabs = signal("negabs", HS)
        ln_done = signal("ln_done", HS)
        sp_done = signal("sp_done", HS)
        sp_masked = signal("sp_masked", HS)
        logw = signal("logw", HS)
        w_exp = signal("w_exp", HS)
        w_masked = signal("w_masked", HS)
        sbT_high = signal("sbT_high", HS // 2)
        sbT_in = signal("sbT_in", HS // 2)
        rg_in = signal("rg_in", 4)
        gr_in = signal("gr_in", 4)
        gs_in = signal("gs_in", 4)
        rg_silu = signal("rg_silu", 2)
        gates = signal("gates", 4)
        head_var = signal("head_var", HR)
        head_rstd = signal("head_rstd", HR)
        ret_normed = signal("ret_normed", HR)
        ret_gated = signal("ret_gated", 2)
        rT_act = signal("rT_act", 4)
        rT_dve = signal("rT_dve", 4)
        ret_out = signal("ret_out", 4)
        sb_gated = signal("sb_gated", 4)
        merged = signal("merged", 4)
        mT_act = signal("mT_act", 4)
        mT_dve = signal("mT_dve", 4)
        g_silu = signal("g_silu", 2 * PAIRS)
        gu_mul = signal("gu_mul", 2 * PAIRS)
        gu_high = signal("gu_high", 2 * PAIRS)
        gu_done = signal("gu_done", 2 * PAIRS)

        unit_read2 = signal("unit_read2", len(CHUNKS2) + 3 + 2 * GROUPS * (EXPERTS - 1))
        split2 = [k for k in units2.place if k[0] in COL2 or k[0] == "w_o_2"]
        high2_done = signal("high2_done", len(split2))
        low2_done = signal("low2_done", len(split2))
        ln2_in = signal("ln2_in", 32)
        x_ready = signal("x_ready", 4, TT)
        table_step = sem("table_step")
        passed = sem("passed")
        ln_step = sem("ln_step")
        table_done = sem("table_done")
        params_in = signal("params_in", 16 * N_PARAMS)
        bT_high = signal("bT_high", 8)
        bT_low = signal("bT_low", 8)
        xT2_act = signal("xT2_act", 2)
        xT2_dve = signal("xT2_dve", 2)
        u_act = signal("u_act", 10)
        u_dve = signal("u_dve", 8)
        latent_sq = signal("latent_sq", 4)
        latent_ms = signal("latent_ms", 1)
        latent_rms = signal("latent_rms", 1)
        latent_done = signal("latent_done", 1)
        r_mul = signal("r_mul", 5)
        r_add = signal("r_add", 5)
        kcopy = signal("kcopy", 3)
        wi_done = signal("wi_done", 1)
        qiT_in = signal("qiT_in", 1)
        kkT_in = signal("kkT_in", 1)
        cT_in = signal("cT_in", 3)
        relu_in = signal("relu_in", HI)
        score_in = signal("score_in", HI)
        score_masked = signal("score_masked", 1)
        topk_done = signal("topk_done", 1)
        nm_masked = signal("nm_masked", 1)
        mq_in = signal("mq_in", 4)
        mk_in = signal("mk_in", 4)
        mqT_in = signal("mqT_in", 4)
        mkT_in = signal("mkT_in", 4)
        dsT_in = signal("dsT_in", 1)
        dqT_in = signal("dqT_in", 3)
        dkT_in = signal("dkT_in", 3)
        masked = signal("masked", JOBS * 3)
        weighed = signal("weighed", JOBS)
        ET_dve = signal("ET_dve", HM + HX + 2 * HX)
        ET_act = signal("ET_act", HX)
        mix_done = signal("mix_done", 4)
        stat_done = signal("stat_done", 2)
        rstd_done = signal("rstd_done", 2)
        gained = signal("gained", 4)
        wo_in = signal("wo_in", 4)
        logit_in = signal("logit_in", 1)
        hot_done = signal("hot_done", 1)
        shift_done = signal("shift_done", 1)
        gexp_done = signal("gexp_done", 1)
        diff_done = signal("diff_done", 1)
        eexp_done = signal("eexp_done", 1)
        gate_done = signal("gate_done", 1)
        rank_ready = signal("rank_ready", 3)
        npass_done = signal("npass_done", 1)
        pick_done = signal("pick_done", 3)
        resid_in = signal("resid_in", TT)
        pickT_in = signal("pickT_in", 2)
        gslot_in = signal("gslot_in", 1)
        xg_high = signal("xg_high", 2 * GROUPS)
        xg_low = signal("xg_low", 2 * GROUPS)
        ehigh_done = signal("ehigh_done", 2 * GROUPS * EXPERTS)
        elow_done = signal("elow_done", 2 * GROUPS * EXPERTS)
        g2_silu = signal("g2_silu", GROUPS * EXPERTS)
        h2_done = signal("h2_done", GROUPS * EXPERTS)
        hT_in = signal("hT_in", GROUPS * EXPERTS)
        yg_in = signal("yg_in", 2 * GROUPS, 1)
        sc_added = signal("sc_added", 4)
        moe_moments = signal("moe_moments", 4)

        def wait_apart(eng, semaphore, count):
            eng.wait_ge(semaphore, count)
            eng.sem_inc(passed, 1)

        def bank_of(key):
            return ps[:, banks[key], :]

        def bank2(key):
            return ps[:, banks2[key], :]


        bank_read = {}
        for kp in range(4):
            bank_read["nT", kp] = (nT_dve, 2 * kp + 2)
            bank_read["nT2", kp] = (nT_dve, 8 + 2 * kp + 2)
            bank_read["rT", kp] = (rT_dve, kp + 1)
            bank_read["mT", kp] = (mT_dve, kp + 1)
            bank_read["ret", kp] = (ret_out, kp + 1)
            bank_read["sb", kp] = (sb_gated, kp + 1)
            bank_read["wo", kp] = (h_added, kp + 1)
            bank_read["ffn", kp] = (h_added, 4 + kp + 1)
        for t in range(TT):
            for name, signal_, k in (("rq", rotated, 0), ("rk", rotated, 2), ("sq", sqk_in, 0), ("sk", sqk_in, 2),
                                     ("rv0", rv_in, 0), ("rv1", rv_in, 2), ("qT", qT_in, 0), ("kT", kT_in, 0),
                                     ("sv", sv_in, 0), ("rg0", rg_in, 0), ("rg1", rg_in, 2), ("gr0", gr_in, 0),
                                     ("gr1", gr_in, 2), ("gs0", gs_in, 0), ("gs1", gs_in, 2)):
                bank_read[name, t] = (signal_, k + t + 1)
        for h in range(HS):
            bank_read["z", h] = (z_in, h + 1)
            bank_read["c", h] = (logw, h + 1)
        for h in range(HR):
            bank_read["rs", h] = (st_in, h + 1)
            bank_read["ro", h] = (ret_normed, h + 1)
            bank_read["so", h] = (sbT_in, h + 1)
        for i in range(2 * PAIRS):
            bank_read["gu", i] = (gu_mul, i + 1)

        read2 = {}
        for kp in range(4):
            for n, name in enumerate(("xT", "oT")):
                read2[name, kp] = (bT_low, 4 * n + kp + 1)
            read2["xT2", kp] = ((xT2_act, xT2_dve)[kp % 2], kp // 2 + 1)
            read2["uq", kp] = (mq_in, kp + 1)
            read2["ukv", kp] = (mk_in, kp + 1)
            read2["mqT", kp] = (mqT_in, kp + 1)
            read2["mkT", kp] = (mkT_in, kp + 1)
            read2["wo", kp] = (wo_in, kp + 1)
            read2["O", kp] = (mix_done, kp + 1)
        for by, signal_ in ((BY_ACT, u_act), ([c for c, _, _ in CHUNKS2 if c not in BY_ACT], u_dve)):
            for n, name in enumerate(by):
                for t in range(TT):
                    read2[name, t] = (signal_, 2 * n + t + 1)
        for b in range(3):
            read2["dqT", b] = (dqT_in, b + 1)
            read2["dkT", b] = (dkT_in, b + 1)
        read2["qiT", 0], read2["kkT", 0], read2["dsT", 0] = (qiT_in, 1), (kkT_in, 1), (dsT_in, 1)
        read2["cT", 0], read2["cT", 1] = (cT_in, 2), (cT_in, 3)
        for h in range(HI):
            read2["rel", h] = (relu_in, h + 1)
        for j in range(JOBS):
            for part in range(parts(j)):
                read2["S", j, part] = (masked, 3 * j + 3 if part == parts(j) - 1 else 3 * j + part + 1)
                if j < HM + HX:
                    read2["E", j, part] = (ET_dve, j + 1)
                elif part == 0:
                    read2["E", j, part] = (ET_act, j - HM - HX + 1)
                else:
                    read2["E", j, part] = (ET_dve, HM + HX + 2 * (j - HM - HX) + part)
        read2["router", 0], read2["ranks", 0] = (logit_in, 1), (npass_done, 1)

        def held_before(plan, key):
            bank, n = plan.place[key]
            return next((k for k, at in plan.place.items() if at == (bank, n - 1)), None)

        order = list(units.place)
        said = [(c, 0) for c, _ in CHUNKS] + [("w_ret_o", 0), ("w_ret_o", 1), ("w_ret_o", 2), ("w_sb_o", 0),
                                              ("w_out", 0), ("w_out", 1), ("w_out", 2), ("gate", 0), ("gate", 1)]
        for p in range(2, PAIRS + 1):
            said += [("down", p - 2)] + ([("gate", p)] if p < PAIRS else [])
        said_at = {key: n + 1 for n, key in enumerate(said)}
        said_per_step = said_at["gate", 3] - said_at["gate", 1]
        units_per_step = order.index(("gate", 4)) - order.index(("gate", 2))

        def released(key, l, step=0):
            if key in said_at:
                return unit_read.sem, unit_read.at(l, said_at[key]) + step * said_per_step
            name, u = key
            fill = {"up": ("gu", 2 * u + 1), "down": ("ffn", 3), "w_ret_o": ("ret", 3), "w_sb_o": ("sb", 3),
                    "w_out": ("wo", 3)}.get(name, (name, 1))
            return filled[banks[fill]], banks.before(fill, l) + 1 + step

        said2_at = {key: n + 1 for n, key in enumerate([(c, 0) for c, _, _ in CHUNKS2] +
                                                       [("w_o_2", u) for u in range(3)])}
        DENSE_READS = len(said2_at)

        def released2(key, l, g=0):
            name = key[0]
            if key in said2_at:
                return unit_read2.sem, unit_read2.at(l, said2_at[key])
            if name == "down" and key[3] < EXPERTS - 1:
                pass_, e = key[1], key[3]
                return unit_read2.sem, (unit_read2.at(l, DENSE_READS + pass_ * GROUPS * (EXPERTS - 1) + e + 1)
                                        + g * (EXPERTS - 1))
            if name in ("gate", "up"):
                fill = ("gu", key[1], 0, key[3])
                step = banks2.stride(fill, ("gu", key[1], 1, key[3]))
            elif name == "down":
                fill = ("yg", key[1], 0, 1)
                step = banks2.stride(fill, ("yg", key[1], 1, 1))
            else:
                fill, step = {"uq": ("uq", 3), "ukv": ("ukv", 3), "w_o_2": ("wo", 3)}.get(name, (name, 1)), 0
            return filled[banks2[fill]], banks2.before(fill, l) + 1 + g * step

        def used(key):
            return 4 * COL2[key[0]][1] if key[0] in COL2 else UNIT

        def high_part(n, l, step=0):
            key = order[n]
            nc.scalar.wait_ge(landed[units[key]], (units.before(key, l) + 1 + step) * 16)
            if n >= HIGH:
                nc.scalar.wait_ge(*released(order[n - HIGH], l, step))
            nc.scalar.activation(split(high[:, n % HIGH, :]), ring[:, units[key], :],
                                 ACT.Copy).then_inc(high_done.sem, 1)

        def low_part(n, l, step=0):
            nc.vector.wait_ge(high_done.sem, high_done.at(l, n + 1) + step * units_per_step)
            slot = ring[:, units[order[n]], :]
            nc.vector.tensor_tensor(split(slot), slot, split(high[:, n % HIGH, :]),
                                    ALU.subtract).then_inc(low_done.sem, 1)

        def high_part2(n, l):
            key = split2[n]
            nc.scalar.wait_ge(landed[units2[key]], (units2.before(key, l) + 1) * 16)
            if n >= HIGH:
                nc.scalar.wait_ge(*released2(split2[n - HIGH], l))
            nc.scalar.activation(split(high[:, n % HIGH, 0:used(key)]), ring[:, units2[key], 0:used(key)],
                                 ACT.Copy).then_inc(high2_done.sem, 1)

        def low_part2(n, l):
            nc.vector.wait_ge(high2_done.sem, high2_done.at(l, n + 1))
            slot = ring[:, units2[split2[n]], 0:used(split2[n])]
            nc.vector.tensor_tensor(split(slot), slot, split(high[:, n % HIGH, 0:used(split2[n])]),
                                    ALU.subtract).then_inc(low2_done.sem, 1)

        def product3(acc, stationary, moving, start, stop):
            (sh, sl), (mh, ml) = [tuple(split(a) for a in pair) for pair in (stationary, moving)]
            nc.tensor.matmul(acc, sh, mh, start=start, stop=False)
            nc.tensor.matmul(acc, sh, ml, start=False, stop=False)
            return nc.tensor.matmul(acc, sl, mh, start=False, stop=stop)

        def slots_at(s, n):
            return ring[:, s:s + n, :] if s < RING else more_slots[:, s - RING:s - RING + n, :]

        def expert_landed(name, e, l, pass_, g):
            key = (name, 0, 0, e)
            turn_ = (units2.before(key, l) + 1 + pass_ * units2.stride(key, (name, 1, 0, e))
                     + g * units2.stride(key, (name, 0, 1, e)))
            return landed[units2[key]], turn_ * 16

        def pass_turn(name, key, l, pass_, g):
            first = (name, 0) + key
            more = pass_ * banks2.stride(first, (name, 1) + key)
            if name in ("xg", "gu", "hT", "yg"):
                more = more + g * banks2.stride(first, (name, 0, 1) + key[1:])
            return banks2.before(first, l) + more

        block = ctx.enter_context(nc.Block())

        @block.sync
        def _(sp_):
            col = dict(CHUNKS)

            def source(key, l):
                name, u = key
                if name in col:
                    w = src["w_in"].rearrange("l (p k) n -> (l p) k n", k=KT)
                    return w[l * P:(l + 1) * P, 4 * u:4 * u + 4, col[name]:col[name] + CHUNK]
                if name in ("gate", "up"):
                    w = src["w_gate_up"].rearrange("l (p k) n -> (l p) k n", k=KT)
                    first = (name == "up") * FF
                    return w[l * P:(l + 1) * P, :, bass.ds(u * 256 + first, 256)]
                if name == "down":
                    w = src["w_down"].rearrange("l (k p) n -> (l k) p n", p=P)
                    return w[bass.ds(u * 2 + l * (FF // P), 2)].rearrange("k p n -> p k n")
                w = src[name].rearrange("l (k p) n -> (l k) p n", p=P)
                n = src[name].shape[1] // P
                return w[l * n + 2 * u:l * n + 2 * u + 2].rearrange("k p n -> p k n")

            def into(key):
                shape = {"gate": (8, 256), "up": (8, 256), "down": (2, 1024)}.get(
                    key[0], (4, 512) if key[0] in col else (2, 1024))
                return ring[:, units[key], :].rearrange("p (k n) -> p k n", k=shape[0])

            def wait_released(key, l):
                sp_.wait_ge(*released(key, l))

            def on_all(row):
                return row.rearrange("(a d) -> a d", a=1).to_broadcast([P, row.shape[0]])

            table_small = [(freq[:, 0, :], src["c_freq"]), (freq[:, 1, :], src["c_sign"]),
                           (pos_i[:], src["positions_2"].rearrange("b (t p) -> p (b t)", p=P)),
                           (ident[:], src["c_ident"])]
            for to, of in table_small:
                sp_.dma_start(to, of, allow_slow_non_contiguous=True).then_inc(first_in, 16)
            sp_.dma_start(H[:], src["x"].rearrange("b (t p) d -> (b p) t d", p=P)).then_inc(x_in, 16)
            small = [(suffix[:], src["c_suffix"]), (rope1, src["c_rope"]),
                     (decay, src["c_decay"])]
            small += [(gfinal, on_all(src["norm_final"]))]
            for key in order[:2]:
                sp_.dma_start(into(key), source(key, 0)).then_inc(landed[units[key]], 16)
            for to, of in small:
                sp_.dma_start(to, of, allow_slow_non_contiguous=True).then_inc(const_in, 16)

            for l in range(LAYERS):
                if l > 0:
                    sp_.wait_ge(nT_act.sem, nT_act.at(l, 0))
                    sp_.wait_ge(nT_dve.sem, nT_dve.at(l, 0))
                for w, g in enumerate(("norm_mix", "norm_ffn")):
                    sp_.dma_start(gains[:, w, :], src[g][l].rearrange("(p k) -> p k", k=KT)).then_inc(gains_in.sem, 16)
                for n, key in enumerate(order):
                    if l == 0 and n < 2:
                        continue
                    slot = units[key]
                    if n >= RING:
                        wait_released(order[n - RING], l)
                    elif l > 0:
                        prev = [k for k in order if units[k] == slot][-1]
                        wait_released(prev, l - 1)
                    sp_.dma_start(into(key), source(key, l)).then_inc(landed[slot], 16)

            def params(l):
                yield cgain[:, 0:2], src["mla_q_norm_2"][l].rearrange("(k p) -> p k", p=P)
                yield cgain[:, 2:3], src["mla_kv_norm_2"][l].rearrange("(k p) -> p k", p=P)
                for n, name in enumerate(("ln1_g_2", "ln1_b_2")):
                    yield lng[:, n, :], on_all(src[name][l])
                yield rw[:, :, 0:GROUPS], src["router_group_w_2"][l].rearrange("(p k) g -> p k g", k=KT)
                yield rb[:, 0:GROUPS], on_all(src["router_group_b_2"][l])
                for g in range(GROUPS):
                    at = GROUPS + g * EXPERTS
                    yield rw[:, :, at:at + EXPERTS], src["router_expert_w_2"][l, g].rearrange("(p k) e -> p k e", k=KT)
                yield rb[:, GROUPS:36], on_all(src["router_expert_b_2"][l].rearrange("g e -> (g e)"))
                yield causal_m, src["c_causal"]
                yield near_m, src["c_near"]
                yield before, src["c_before"]
                yield iota, src["c_iota"]

            def source2(key, l, g=None):
                name = key[0]
                if name in COL2:
                    at, width = COL2[name]
                    w = src["w_in_2"].rearrange("l (p k) n -> (l p) k n", k=KT)
                    return w[l * P:(l + 1) * P, 4 * key[1]:4 * key[1] + 4, at:at + width]
                if name in ("uq", "ukv"):
                    w = src[f"mla_w_{name}_2"]
                    return w[l].rearrange("(k p) n -> p k n", p=P)
                if name == "w_o_2":
                    return src[name][l, 256 * key[1]:256 * (key[1] + 1), :].rearrange("(k p) n -> p k n", p=P)
                w = src[f"expert_w_{name}_2"]
                rows = 8 if name != "down" else 2
                e = key[3]
                w = w.rearrange("l g e (p k) n -> (l g e p) k n", k=rows)
                return w[bass.ds((l * GROUPS * EXPERTS + e) * P + g * (EXPERTS * P), P)]

            def into2(key, width=None):
                name = key[0]
                slot = slots_at(units2[key], 1)[:, 0, :]
                if name in COL2:
                    return slot[:, 0:4 * COL2[name][1]].rearrange("p (k n) -> p k n", k=4)
                if name in ("uq", "ukv"):
                    k = 2 if name == "uq" else 1
                    return slot[:, 0:k * (768 if name == "uq" else 1024)].rearrange("p (k n) -> p k n", k=k)
                return slot.rearrange("p (k n) -> p k n", k=8 if name in ("gate", "up") else 2)

            def wait_released2(key, l, g=0):
                sp_.wait_ge(*released2(key, l, g))

            dense = [k for k in units2.place if len(k) == 2]
            last_of_first = {units[k]: k for k in order}
            for l in range(LAYERS):
                for n, key in enumerate(dense):
                    slot = units2[key]
                    if n >= RING:
                        wait_released2(dense[n - RING], l)
                    elif l == 0:
                        wait_released(last_of_first[slot], LAYERS - 1)
                    else:
                        e = max(i for i in range(EXPERTS) if i % TRIPLES == slot // 3)
                        wait_released2((KINDS[slot % 3], 1, 0, e), l - 1, GROUPS - 1)
                    sp_.dma_start(into2(key), source2(key, l)).then_inc(landed[slot], 16)
                    if n == RING - 1:
                        sp_.wait_ge(x_ready.sem, x_ready.at(l, 0))
                        for to, of in params(l):
                            sp_.dma_start(to, of, allow_slow_non_contiguous=True).then_inc(params_in.sem, 16)
                for pass_ in range(2):
                    def load(e, g, held, held_g):
                        for n, name in enumerate(KINDS):
                            if held is not None:
                                wait_released2(held[n] if isinstance(held, list) else (name, pass_, 0, held),
                                               l, held_g)
                            key = (name, pass_, 0, e)
                            sp_.dma_start(into2(key), source2(key, l, g)).then_inc(landed[units2[key]], 16)

                    def last_of(e):
                        return max(i for i in range(EXPERTS) if i % TRIPLES == e % TRIPLES)

                    def load_rest(g):
                        for e in range(TRIPLES, EXPERTS):
                            load(e, g, e - TRIPLES, g)

                    def expert_loads():
                        for e in range(TRIPLES):
                            if pass_ == 1:
                                load(e, 0, [(name, 0, 0, last_of(e)) for name in KINDS], GROUPS - 1)
                            elif 3 * e < RING:
                                load(e, 0, dense[len(dense) - RING + 3 * e:][:3], 0)
                            else:
                                sp_.wait_ge(x_ready.sem, x_ready.at(l, 2))
                                load(e, 0, None, 0)
                                for n, name in enumerate(("ln2_g_2", "ln2_b_2")):
                                    sp_.dma_start(lng[:, n, :], on_all(src[name][l])).then_inc(ln2_in.sem, 16)
                        with sp_.Fori(0, GROUPS - 1) as g:
                            load_rest(g)
                            for e in range(TRIPLES):
                                load(e, g + 1, last_of(e), g)
                        load_rest(GROUPS - 1)

                    if pass_ == 0:
                        expert_loads()
                    else:
                        wait_apart(sp_, npass_done.sem, npass_done.at(l, 1))
                        passes = sp_.value_load(npass[0:1, 0:1], min_val=1, max_val=2)
                        with sp_.If(passes > 1):
                            expert_loads()
                        with sp_.Else():
                            for s_ in range(EXPERT_SLOTS):
                                n = GROUPS * sum(e % TRIPLES == s_ // 3 for e in range(EXPERTS))
                                sp_.wait_ge(landed[s_], 16 * ((l + 1) * units2.per[s_] + units2.start.get(s_, 0) - n))
                                sp_.sem_inc(landed[s_], 16 * n)
            sp_.wait_ge(x_ready.sem, x_ready.at(LAYERS, 0))
            sp_.dma_start(out.rearrange("b (t p) d -> (b p) t d", p=P), H[:]).then_inc(out_done, 16)
            sp_.wait_ge(out_done, 16)

        @block.tensor
        def _(pe):
            def claim(key, l, more=0):
                old = held_before(banks, key)
                if old is not None:
                    signal_, k = bank_read[old]
                    pe.wait_ge(signal_.sem, signal_.at(l, k) + more)
                return bank_of(key)

            def weights(key, l, step=0):
                n = order.index(key)
                pe.wait_ge(low_done.sem, low_done.at(l, n + 1) + step * units_per_step)
                k = 8 if key[0] in ("gate", "up") else 4 if key[0] in dict(CHUNKS) else 2
                return [a.rearrange("p (k n) -> p k n", k=k) for a in (high[:, n % HIGH, :], ring[:, units[key], :])]

            def X(k, cols=slice(None)):
                return T8[:, k, cols], T8low[:, k, cols]

            def project(c, l):
                for u in range(2):
                    w = weights((c, u), l)
                    for t in range(TT):
                        acc = claim((c, t), l) if u == 0 else bank_of((c, t))
                        for k in range(4):
                            mm = product3(acc, X(4 * u + k, slice(t * P, (t + 1) * P)), [a[:, k, :] for a in w],
                                          start=(u == 0 and k == 0), stop=(u == 1 and k == 3))
                        if u == 1:
                            mm.then_inc(filled[banks[(c, t)]], 1)
                    if u == 0:
                        mm.then_inc(unit_read.sem, 1)

            def project_turned(c, l):
                for u in range(2):
                    w = weights((c, u), l)
                    for b in range(2):
                        acc = claim((c, b), l) if u == 0 else bank_of((c, b))
                        for j in range(2):
                            cols = slice((2 * b + j) * P, (2 * b + j + 1) * P)
                            for k in range(4):
                                mm = product3(acc[:, j * SEQ:(j + 1) * SEQ], [a[:, k, cols] for a in w], X(4 * u + k),
                                              start=(u == 0 and j == 0 and k == 0), stop=(u == 1 and j == 1 and k == 3))
                        if u == 1:
                            mm.then_inc(filled[banks[(c, b)]], 1)
                    if u == 0:
                        mm.then_inc(unit_read.sem, 1)

            def turn(key, a, b, l):
                acc = claim(key, l)
                for j, block_ in enumerate((a, b)):
                    for t in range(TT):
                        mm = nc.tensor.transpose(acc[:, j * SEQ + t * P:j * SEQ + (t + 1) * P], block_(t), ident[:])
                mm.then_inc(filled[banks[key]], 1)

            def turn_norm(name, l, k0):
                pe.wait_ge(xn_done.sem, xn_done.at(l, k0 + 2))
                for kp in range(4):
                    turn((name, kp), lambda t: xn[:, t, 2 * kp::8], lambda t: xn[:, t, 2 * kp + 1::8], l)
                pe.wait_ge(nT_dve.sem, nT_dve.at(l, 4 * k0 + 8))

            def turn_heads(name, which, l):
                pe.wait_ge(roped.sem, roped.at(l, 2 * which + 2))
                for b in range(2):
                    turn((name, b), lambda t: qk[:, which, t, 2 * b * P:(2 * b + 1) * P],
                         lambda t: qk[:, which, t, (2 * b + 1) * P:(2 * b + 2) * P], l)

            def triangle(key, kt_, qt_, l):
                acc = claim(key, l)
                nc.tensor.matmul(acc[:, 0:SEQ], kt_[:, 0:P], qt_, start=True, stop=True)
                nc.tensor.matmul(acc[:, SEQ:TRI], kt_[:, P:SEQ], qt_[:, P:SEQ], start=True,
                                 stop=True).then_inc(filled[banks[key]], 1)

            def suffix_sums(h, l):
                pe.wait_ge(sp_masked.sem, sp_masked.at(l, h + 1))
                acc = claim(("c", h), l)
                nc.tensor.matmul(acc[:, 0:SEQ], suffix[:], sp[:, h, 0:SEQ], start=True, stop=False)
                nc.tensor.matmul(acc[:, P:SEQ], ones[:], sp[:, h, SEQ:TRI], start=False, stop=True)
                nc.tensor.matmul(acc[:, SEQ:TRI], suffix[:], sp[:, h, SEQ:TRI], start=True,
                                 stop=True).then_inc(filled[banks[("c", h)]], 1)

            def stick_out(hp, l):
                pe.wait_ge(w_masked.sem, w_masked.at(l, 2 * hp + 2))
                acc = claim(("so", hp), l)
                for e in range(2):
                    h = 2 * hp + e
                    o = acc[e * DS:(e + 1) * DS, :]
                    nc.tensor.matmul(o[:, 0:SEQ], sv[:, 0, h * DS:(h + 1) * DS], sp[:, h, 0:SEQ],
                                     start=True, stop=False)
                    mm = nc.tensor.matmul(o[:, P:SEQ], sv[:, 1, h * DS:(h + 1) * DS], sp[:, h, SEQ:TRI],
                                          start=False, stop=True)
                mm.then_inc(filled[banks[("so", hp)]], 1)

            def retention_out(h, l):
                pe.wait_ge(st_in.sem, st_in.at(l, h + 1))
                acc = claim(("ro", h), l)
                v = [rv[:, t, h * DV:(h + 1) * DV] for t in range(TT)]
                nc.tensor.matmul(acc[:, 0:DV], ST[:, h, 0:P], v[0], start=True, stop=True)
                nc.tensor.matmul(acc[:, DV:2 * DV], ST[:, h, P:SEQ], v[0], start=True, stop=False)
                nc.tensor.matmul(acc[:, DV:2 * DV], ST[:, h, SEQ:TRI], v[1], start=False,
                                 stop=True).then_inc(filled[banks[("ro", h)]], 1)

            def output_product(name, w_name, aT, n_units, l):
                for u in range(n_units):
                    w = weights((w_name, u), l)
                    for j in range(2):
                        for i in range(4):
                            t, half = divmod(i, 2)
                            if u == 0 and j == 0:
                                claim((name, i), l)
                            last = u == n_units - 1 and j == 1
                            mm = product3(bank_of((name, i)), [a[:, 2 * u + j, t * P:(t + 1) * P] for a in aT],
                                          [a[:, j, half * 512:(half + 1) * 512] for a in w],
                                          start=(u == 0 and j == 0), stop=last)
                            if last:
                                mm.then_inc(filled[banks[(name, i)]], 1)
                    if u < n_units - 1:
                        mm.then_inc(unit_read.sem, 1)

            def gate_up(p, l, step):
                for name, at in (("gate", 0), ("up", SEQ)):
                    w = weights((name, p), l, step)
                    for j in range(2):
                        key = ("gu", 2 * p + j)
                        acc = claim(key, l, step * 4) if name == "gate" else bank_of(key)
                        for k in range(KT):
                            mm = product3(acc[:, at:at + SEQ], [a[:, k, j * P:(j + 1) * P] for a in w], X(k),
                                          start=(k == 0), stop=(k == KT - 1))
                        if name == "up":
                            mm.then_inc(filled[banks[key]], 1)
                    if name == "gate":
                        mm.then_inc(unit_read.sem, 1)

            def down(p, l, step, begin=False, end=False):
                w = weights(("down", p), l, step)
                for j in range(2):
                    tile = 2 * p + j
                    pe.wait_ge(gu_done.sem, gu_done.at(l, tile + 1) + step * 4)
                    for i in range(4):
                        t, half = divmod(i, 2)
                        if begin and j == 0:
                            claim(("ffn", i), l)
                        mm = product3(bank_of(("ffn", i)),
                                      [a[:, tile % 4, t * P:(t + 1) * P] for a in (guT, guTlow)],
                                      [a[:, j, half * 512:(half + 1) * 512] for a in w],
                                      start=(begin and j == 0), stop=(end and j == 1))
                        if end and j == 1:
                            mm.then_inc(filled[banks[("ffn", i)]], 1)
                if not end:
                    mm.then_inc(unit_read.sem, 1)

            pe.wait_ge(first_in, N_FIRST * 16)
            pe.wait_ge(const_set, 1)
            with pe.Fori(0, LAYERS) as l:
                turn_norm("nT", l, 0)
                project("rq", l)
                project("rk", l)
                project_turned("sq", l)
                project_turned("sk", l)
                project("rv0", l)
                turn_heads("qT", 0, l)
                turn_heads("kT", 1, l)
                project("rv1", l)
                pe.wait_ge(qT_in.sem, qT_in.at(l, 2))
                pe.wait_ge(kT_in.sem, kT_in.at(l, 2))
                for h in range(HR):
                    triangle(("rs", h), kT[:, h, :], qT[:, h, :], l)
                pe.wait_ge(sqk_in.sem, sqk_in.at(l, 4))
                for h in range(HS):
                    rows = slice((h % 2) * DS, (h % 2 + 1) * DS)
                    triangle(("z", h), skT[rows, h // 2, :], sqT[rows, h // 2, :], l)
                project("sv", l)
                project("rg0", l)
                pe.wait_ge(rv_in.sem, rv_in.at(l, 4))
                for h in range(HR):
                    retention_out(h, l)
                project("rg1", l)
                pe.wait_ge(const_in, N_CONST * 16)
                for h in range(HS):
                    suffix_sums(h, l)
                project("gr0", l)
                project("gr1", l)
                pe.wait_ge(sv_in.sem, sv_in.at(l, 2))
                for hp in range(HS // 2):
                    stick_out(hp, l)
                project("gs0", l)
                project("gs1", l)
                pe.wait_ge(ret_gated.sem, ret_gated.at(l, 2))
                for kp in range(4):
                    turn(("rT", kp), lambda t: retn[:, t, 2 * kp * P:(2 * kp + 1) * P],
                         lambda t: retn[:, t, (2 * kp + 1) * P:(2 * kp + 2) * P], l)
                pe.wait_ge(rT_dve.sem, rT_dve.at(l, 4))
                output_product("ret", "w_ret_o", (retT, retTlow), 4, l)
                pe.wait_ge(sbT_in.sem, sbT_in.at(l, 4))
                output_product("sb", "w_sb_o", (sbT, sbTlow), 2, l)
                pe.wait_ge(merged.sem, merged.at(l, 4))
                for kp in range(4):
                    turn(("mT", kp), lambda t: xn[:, t, 2 * kp * P:(2 * kp + 1) * P],
                         lambda t: xn[:, t, (2 * kp + 1) * P:(2 * kp + 2) * P], l)
                pe.wait_ge(mT_dve.sem, mT_dve.at(l, 4))
                output_product("wo", "w_out", (T8, T8low), 4, l)
                turn_norm("nT2", l, 2)
                gate_up(0, l, 0)
                gate_up(1, l, 0)
                down(0, l, 0, begin=True)
                with pe.Fori(0, (PAIRS - 3) // 2) as it:
                    for p in (1, 2):
                        gate_up(p + 1, l, it)
                        down(p, l, it)
                gate_up(PAIRS - 1, l, 0)
                down(PAIRS - 2, l, 0)
                down(PAIRS - 1, l, 0, end=True)


            def claim2(key, l):
                old = held_before(banks2, key)
                if old is not None and old in read2:
                    signal_, k = read2[old]
                    pe.wait_ge(signal_.sem, signal_.at(l, k))
                return bank2(key)

            def unit(key, l, more=0):
                pe.wait_ge(landed[units2[key]], (units2.before(key, l) + 1 + more) * 16)
                return ring[:, units2[key], :]

            def weights2(key, l):
                n = split2.index(key)
                pe.wait_ge(low2_done.sem, low2_done.at(l, n + 1))
                return [a[:, 0:used(key)].rearrange("p (k n) -> p k n", k=4 if key[0] in COL2 else 2)
                        for a in (high[:, n % HIGH, :], ring[:, units2[key], :])]

            def fill(mm, key):
                mm.then_inc(filled[banks2[key]], 1)

            def project2(c, l):
                width = COL2[c][1]
                for u in range(2):
                    w = weights2((c, u), l)
                    for t in range(TT):
                        acc = (claim2((c, t), l) if u == 0 else bank2((c, t)))[:, 0:width]
                        for k in range(4):
                            mm = product3(acc, X(4 * u + k, slice(t * P, (t + 1) * P)), [a[:, k, :] for a in w],
                                          start=(u == 0 and k == 0), stop=(u == 1 and k == 3))
                        if u == 1:
                            fill(mm, (c, t))
                    if u == 0:
                        mm.then_inc(unit_read2.sem, 1)

            def turn2(key, blocks, l):
                acc = claim2(key, l)
                for j, block_ in enumerate(blocks):
                    for t in range(TT):
                        a = block_(t)
                        mm = nc.tensor.transpose(acc[0:a.shape[1], j * SEQ + t * P:j * SEQ + (t + 1) * P], a, ident[:])
                fill(mm, key)

            def turn_stream(name, l, buf, n, split):
                for kp in range(4):
                    if split:
                        blocks = [lambda t, k=k: buf[:, t, k::8] for k in (2 * kp, 2 * kp + 1)]
                    else:
                        blocks = [lambda t, k=k: buf[:, t, k * P:(k + 1) * P] for k in (2 * kp, 2 * kp + 1)]
                    turn2((name, kp), blocks, l)
                if n < 2:
                    pe.wait_ge(bT_low.sem, bT_low.at(l, 4 * n + 4))
                else:
                    pe.wait_ge(xT2_act.sem, xT2_act.at(l, 2))
                    pe.wait_ge(xT2_dve.sem, xT2_dve.at(l, 2))

            def index_scores(h, l):
                rows = slice(h % 4 * DI, h % 4 * DI + DI)
                acc = claim2(("rel", h), l)
                nc.tensor.matmul(acc[:, 0:P], qiT[rows, h // 4, 0:P], kkT[rows, 1, 0:P], start=True, stop=True)
                fill(nc.tensor.matmul(acc[:, P:TRI], qiT[rows, h // 4, P:SEQ], kkT[rows, 1, :],
                                      start=True, stop=True), ("rel", h))

            def head_operands(j):
                if j < HM:
                    return [(mqT[0:96, j, :], mkT[0:96, j, :])]
                if j < HM + HX:
                    n = j - HM
                    rows = slice(n % 2 * HD, (n % 2 + 1) * HD)
                    return [(dsT[rows, n // 2, :], kkT[rows, 0, :])]
                out_ = []
                for c in range(len(DILATED)):
                    n = c * HX + j - HM - HX
                    rows = slice(n % 2 * HD, (n % 2 + 1) * HD)
                    out_.append((dqT[rows, n // 2, :], dkT[rows, n // 2, :]))
                return out_

            def head_scores(j, l):
                ops = head_operands(j)
                if len(ops) == 1:
                    q, k = ops[0]
                    acc = claim2(("S", j, 0), l)
                    nc.tensor.matmul(acc[:, 0:P], q[:, 0:P], k[:, 0:P], start=True, stop=True)
                    fill(nc.tensor.matmul(acc[:, P:TRI], q[:, P:SEQ], k, start=True, stop=True), ("S", j, 0))
                    return
                for part, which in enumerate(((0, 1), (2,))):
                    acc = claim2(("S", j, part), l)
                    for n, c in enumerate(which):
                        q, k = ops[c]
                        mm = nc.tensor.matmul(acc[:, n * SEQ:(n + 1) * SEQ], q[:, P:SEQ], k, start=True, stop=True)
                    fill(mm, ("S", j, part))
                acc = claim2(("S", j, 2), l)
                for c, (q, k) in enumerate(ops):
                    mm = nc.tensor.matmul(acc[:, c * P:(c + 1) * P], q[:, 0:P], k[:, 0:P], start=True, stop=True)
                fill(mm, ("S", j, 2))

            def head_turn(j, l):
                pe.wait_ge(weighed.sem, weighed.at(l, j + 1))
                n = 3 if j < HM + HX else 9
                for part in range(parts(j)):
                    acc = claim2(("E", j, part), l)
                    lo = 0 if n == 3 else (0, 4, 6)[part]
                    hi = 3 if n == 3 else (4, 6, 9)[part]
                    for i in range(lo, hi):
                        mm = nc.tensor.transpose(acc[:, (i - lo) * P:(i - lo + 1) * P],
                                                 S[:, j % 2, i * P:(i + 1) * P], ident[:])
                    fill(mm, ("E", j, part))

            def head_out(j, l):
                signal_, k = read2["E", j, parts(j) - 1]
                pe.wait_ge(signal_.sem, signal_.at(l, k))
                if j >= HM + HX:
                    pe.wait_ge(ET_act.sem, ET_act.at(l, j - HM - HX + 1))
                E = ET[:, j % 2, :]
                second = [] if j < HM + HX else [(i, c, kt_) for i, (c, kt_) in
                                                enumerate([(c, kt_) for c in range(3) for kt_ in range(2)])]
                if j < HM:
                    v = lambda c, kt_: mvv[:, kt_, j * VM:(j + 1) * VM]
                elif j < HM + HX:
                    v = lambda c, kt_: U[:, kt_, 736:800]
                else:
                    n = j - HM - HX
                    v = lambda c, kt_: U[:, kt_, 2632 + (c * HX + n) * HD:2632 + (c * HX + n + 1) * HD]
                cols = slice(j % 8 * HD, (j % 8 + 1) * HD)
                o = [bank2(("O", 2 * (j // 8) + t))[:, cols] for t in range(TT)]
                if j < HM + HX:
                    todo = [(0, [(0, 0, 0)]), (1, [(1, 0, 0), (2, 0, 1)])]
                else:
                    todo = [(0, [(6 + c, c, 0) for c in range(3)]),
                            (1, [(2 * c + kt_, c, kt_) for c in range(3) for kt_ in range(2)])]
                for t, terms in todo:
                    for n_, (blk, c, kt_) in enumerate(terms):
                        mm = nc.tensor.matmul(o[t], E[:, blk * P:(blk + 1) * P], v(c, kt_),
                                              start=(n_ == 0), stop=(n_ == len(terms) - 1))
                    if j % 8 == 7:
                        fill(mm, ("O", 2 * (j // 8) + t))

            with pe.Fori(0, LAYERS) as l:
                pe.wait_ge(x_ready.sem, x_ready.at(l, 0))
                turn_stream("xT", l, H, 0, True)
                project2("C", l)
                project2("A", l)
                project2("B", l)
                project2("q0", l)
                pe.wait_ge(r_add.sem, r_add.at(l, 1))
                turn2(("qiT", 0), [lambda t: U[:, t, 800:928], lambda t: U[:, t, 928:1056]], l)
                pe.wait_ge(kcopy.sem, kcopy.at(l, 3))
                turn2(("kkT", 0), [lambda t: kk[:, t, :], lambda t: ki4[:, t, :]], l)
                pe.wait_ge(latent_done.sem, latent_done.at(l, 1))
                turn2(("cT", 0), [lambda t: U[:, t, 0:128], lambda t: U[:, t, 128:256]], l)
                turn2(("cT", 1), [lambda t: U[:, t, 256:384]], l)
                project2("q1", l)
                pe.wait_ge(qiT_in.sem, qiT_in.at(l, 1))
                pe.wait_ge(kkT_in.sem, kkT_in.at(l, 1))
                for h in range(HI):
                    index_scores(h, l)
                pe.wait_ge(cT_in.sem, cT_in.at(l, 3))
                w = unit(("uq", 0), l)[:, 0:1536].rearrange("p (k n) -> p k n", k=2)
                for i in range(4):
                    t, half = divmod(i, 2)
                    acc = claim2(("uq", i), l)
                    for k in range(2):
                        mm = nc.tensor.matmul(acc[:, 0:384], cT[:, k, t * P:(t + 1) * P],
                                              w[:, k, half * 384:(half + 1) * 384], start=(k == 0), stop=(k == 1))
                    fill(mm, ("uq", i))
                w = unit(("ukv", 0), l)
                for i in range(4):
                    t, half = divmod(i, 2)
                    fill(nc.tensor.matmul(claim2(("ukv", i), l), cT[:, 2, t * P:(t + 1) * P],
                                          w[:, half * 512:(half + 1) * 512], start=True, stop=True), ("ukv", i))
                project2("k0", l)
                project2("k1", l)
                project2("v0", l)
                pe.wait_ge(r_add.sem, r_add.at(l, 4))
                for b in range(4):
                    turn2(("mqT", b), [lambda t, h=h: mq[:, t, h * 96:(h + 1) * 96] for h in (2 * b, 2 * b + 1)], l)
                pe.wait_ge(mk_in.sem, mk_in.at(l, 4))
                for b in range(4):
                    turn2(("mkT", b), [lambda t, h=h: mk[:, t, h * 96:(h + 1) * 96] for h in (2 * b, 2 * b + 1)], l)
                project2("v1", l)
                turn2(("dsT", 0), [lambda t: U[:, t, 416:544], lambda t: U[:, t, 544:672]], l)
                pe.wait_ge(r_add.sem, r_add.at(l, 5))
                for name, at in (("dqT", 1096), ("dkT", 1864)):
                    for b in range(3):
                        turn2((name, b), [lambda t, c=at + (2 * b + i) * P: U[:, t, c:c + P] for i in range(2)], l)
                pe.wait_ge(mqT_in.sem, mqT_in.at(l, 4))
                pe.wait_ge(mkT_in.sem, mkT_in.at(l, 4))
                pe.wait_ge(dsT_in.sem, dsT_in.at(l, 1))
                pe.wait_ge(dqT_in.sem, dqT_in.at(l, 3))
                pe.wait_ge(dkT_in.sem, dkT_in.at(l, 3))
                for i in range(4):
                    claim2(("O", i), l)
                for j in range(JOBS + 2):
                    if j < JOBS:
                        head_scores(j, l)
                    if 1 <= j <= JOBS:
                        head_turn(j - 1, l)
                    if j >= 2:
                        head_out(j - 2, l)
                pe.wait_ge(mix_done.sem, mix_done.at(l, 4))
                turn_stream("oT", l, xn, 1, False)
                for u in range(4):
                    w = weights2(("w_o_2", u), l)
                    for j in range(2):
                        for i in range(4):
                            t, half = divmod(i, 2)
                            last = u == 3 and j == 1
                            mm = product3(bank2(("wo", i)), X(2 * u + j, slice(t * P, (t + 1) * P)),
                                          [a[:, j, half * 512:(half + 1) * 512] for a in w],
                                          start=(u == 0 and j == 0), stop=last)
                            if last:
                                fill(mm, ("wo", i))
                    if u < 3:
                        mm.then_inc(unit_read2.sem, 1)
                pe.wait_ge(x_ready.sem, x_ready.at(l, 2))
                turn_stream("xT2", l, H, 2, True)
                acc = bank2(("router", 0))
                for t in range(TT):
                    for k in range(KT):
                        mm = nc.tensor.matmul(acc[:, t * 64:t * 64 + 36], T8[:, k, t * P:(t + 1) * P], rw[:, k, :],
                                              start=(k == 0), stop=(k == KT - 1))
                fill(mm, ("router", 0))
                pe.wait_ge(hot_done.sem, hot_done.at(l, 1))
                acc = bank2(("ranks", 0))
                nc.tensor.matmul(acc[:, 0:4], before, hot[:, 0, :], start=True, stop=True)
                nc.tensor.matmul(acc[:, 4:8], before, hot[:, 1, :], start=True, stop=False)
                nc.tensor.matmul(acc[:, 4:8], ones[:], hot[:, 0, :], start=False, stop=True)
                nc.tensor.matmul(acc[:, 8:12], ones[:], hot[:, 0, :], start=True, stop=False)
                fill(nc.tensor.matmul(acc[:, 8:12], ones[:], hot[:, 1, :], start=False, stop=True), ("ranks", 0))
                wait_apart(pe, npass_done.sem, npass_done.at(l, 1))
                passes = pe.value_load(npass[0:1, 0:1], min_val=1, max_val=2)
                with pe.Fori(0, 2) as ps_:
                    lp = l * 2 + ps_

                    def fill_p(mm, name, *key):
                        mm.then_inc(filled[banks2[(name, 0) + key]], 1)

                    with pe.If(passes > ps_):
                        pe.wait_ge(pick_done.sem, pick_done.at(l, 1) + ps_)
                        for b in range(2):
                            acc = bank2(("pT", 0, b))
                            for i in range(2):
                                for t in range(TT):
                                    mm = nc.tensor.transpose(acc[:, (2 * i + t) * P:(2 * i + t + 1) * P],
                                                             pick[:, 2 * b + i, t, :], ident[:])
                            fill_p(mm, "pT", b)
                        pe.wait_ge(gate_done.sem, gate_done.at(l, 1))
                        acc = bank2(("slots", 0))
                        for g in range(GROUPS):
                            for t in range(TT):
                                mm = nc.tensor.matmul(acc[:, g * EXPERTS:(g + 1) * EXPERTS], pick[:, g, t, :],
                                                      gate[:, t, g, :], start=(t == 0), stop=(t == 1))
                        fill_p(mm, "slots")
                        wait_apart(pe, pickT_in.sem, pickT_in.at(lp, 2))

                        def turn_hidden(e, g):
                            pe.wait_ge(h2_done.sem, h2_done.at(lp, 1) + (g * EXPERTS + e))
                            acc = bank2(("hT", 0, 0, e))
                            for j in range(2):
                                mm = nc.tensor.transpose(acc[:, j * P:(j + 1) * P], hh[:, e % 2, j::2], ident[:])
                            fill_p(mm, "hT", 0, e)

                        def gate_up2(e, g):
                            pe.wait_ge(elow_done.sem, elow_done.at(lp, 2 * e + 2) + g * (2 * EXPERTS))
                            s_ = units2[("gate", 0, 0, e)]
                            w_ = [a.rearrange("p s (k n) -> p s k n", k=KT) for a in (ehigh[e % 2], slots_at(s_, 2))]
                            acc = bank2(("gu", 0, 0, e))
                            for k in range(KT):
                                if k == KT // 2 and e >= 1:
                                    turn_hidden(e - 1, g)
                                mm = product3(acc.rearrange("p (s n) -> p s n", s=2), (XG[:, k, :], XGlow[:, k, :]),
                                              [a[:, :, k, :] for a in w_], start=(k == 0), stop=(k == KT - 1))
                            fill_p(mm, "gu", 0, e)

                        def down2(e, g):
                            count = g * EXPERTS + e
                            if e == EXPERTS - 1:
                                turn_hidden(e, g)
                            pe.wait_ge(*expert_landed("down", e, l, ps_, g))
                            w_ = slots_at(units2["down", 0, 0, e], 1)[:, 0, :]
                            pe.wait_ge(hT_in.sem, hT_in.at(lp, 1) + count)
                            for j in range(2):
                                for half in range(2):
                                    mm = nc.tensor.matmul(bank2(("yg", 0, 0, half)), hT[:, e % 2, j * P:(j + 1) * P],
                                                          w_[:, j * D + half * 512:j * D + (half + 1) * 512],
                                                          start=(e == 0 and j == 0),
                                                          stop=(e == EXPERTS - 1 and j == 1))
                                    if e == EXPERTS - 1 and j == 1:
                                        fill_p(mm, "yg", 0, half)
                            if e < EXPERTS - 1:
                                mm.then_inc(unit_read2.sem, 1)

                        with pe.Fori(0, GROUPS) as g:
                            for b in range(2):
                                acc = bank2(("xg", 0, 0, b))
                                for k in range(4):
                                    for t in range(TT):
                                        mm = nc.tensor.matmul(acc[:, k * P:(k + 1) * P], H[:, t, 4 * b + k::8],
                                                              pick[:, bass.ds(g, 1), t, :].rearrange("p a n -> p (a n)"),
                                                              start=(t == 0), stop=(t == 1))
                                fill_p(mm, "xg", 0, b)
                            pe.wait_ge(xg_low.sem, xg_low.at(lp, 2) + g * 2)
                            gate_up2(0, g)
                            pe.wait_ge(yg_in.sem, yg_in.at(lp, 0) + g * 2)
                            pe.wait_ge(gslot_in.sem, gslot_in.at(lp, 1))
                            for e in range(1, EXPERTS):
                                gate_up2(e, g)
                                down2(e - 1, g)
                            down2(EXPERTS - 1, g)
                        pe.wait_ge(yg_in.sem, yg_in.at(lp, 2 * GROUPS))
                        for i in range(4):
                            t, half = divmod(i, 2)
                            for g in range(GROUPS):
                                mm = nc.tensor.matmul(bank2(("sc", 0, i)), pickT[:, g, t * P:(t + 1) * P],
                                                      YG[:, g, half * 512:(half + 1) * 512],
                                                      start=(g == 0), stop=(g == GROUPS - 1))
                            fill_p(mm, "sc", i)
                        wait_apart(pe, sc_added.sem, sc_added.at(lp, 4))
                    with pe.Else():
                        pe.drain()
                        for b in range(BANKS):
                            n = sum(k[0] in PASS_KEYS and k[1] == 0 and r == b for k, (r, _) in banks2.place.items())
                            pe.sem_inc(filled[b], n)
                        pe.sem_inc(unit_read2.sem, GROUPS * (EXPERTS - 1))

        @block.scalar
        def _(act):
            def content(key, l, more=0):
                act.wait_ge(filled[banks[key]], banks.before(key, l, more) + 1)
                return bank_of(key)

            def square_sums(l, k0):
                for t in range(TT):
                    act.wait_ge(h_added.sem, h_added.at(l, 2 * k0 - 2 + 2 * t))
                    nc.scalar.activation(xn[:, t, :], H[:, t, :], ACT.Square,
                                         accum_out=stat[:, t:t + 1]).then_inc(sumsq.sem, 1)

            def norm_turned(name, l, w):
                for kp in range(4):
                    acc = content((name, kp), l)
                    for j in range(2):
                        nc.scalar.activation(split(T8[:, 2 * kp + j, :]), acc[:, j * SEQ:(j + 1) * SEQ], ACT.Copy,
                                             scale=gains[:, w, 2 * kp + j:2 * kp + j + 1]).then_inc(nT_act.sem, 1)

            def leave(key, l, to, signal_, scale=1.0):
                nc.scalar.activation(to, content(key, l), ACT.Copy, scale=scale).then_inc(signal_.sem, 1)

            def leave_high(key, l, to, signal_):
                nc.scalar.activation(split(to), content(key, l)[:, 0:to.shape[1]],
                                     ACT.Copy).then_inc(signal_.sem, 1)

            def flat(a):
                return a.rearrange("p a n -> p (a n)")

            act.wait_ge(table_done, 1)
            nc.scalar.activation(rotation[1], turns_[:, 0], ACT.Sin).then_inc(table_done, 1)
            nc.scalar.activation(rotation[0], turns_[:, 1], ACT.Sin).then_inc(table_done, 1)
            with act.Fori(0, LAYERS) as l:
                def high_parts(first, last):
                    for n in range(first, last + 1):
                        high_part(n, l)

                act.sem_clear(act_step)
                square_sums(l, 0)
                high_parts(0, 1)
                act.wait_ge(gains_in.sem, gains_in.at(l, 32))
                norm_turned("nT", l, 0)
                high_parts(2, 7)
                for name, to, scale in (("sq", sqT, DS ** -0.5), ("sk", skT, 1.0)):
                    for b in range(2):
                        leave((name, b), l, flat(to[:, 2 * b:2 * b + 2, :]), sqk_in, scale)
                    high_parts(*{"sq": (8, 9), "sk": (10, 11)}[name])
                for t in range(TT):
                    leave(("rv0", t), l, rv[:, t, 0:512], rv_in)
                for b in range(2):
                    leave(("qT", b), l, flat(qT[:, 2 * b:2 * b + 2, :]), qT_in)
                high_parts(12, 13)
                for t in range(TT):
                    leave(("rv1", t), l, rv[:, t, 512:D], rv_in)
                nc.scalar.preload_act_table_set("natural_log_exp_and_others")
                for h in range(HS + 1):
                    if h == 3:
                        high_part(14, l)
                    if h == 6:
                        high_part(15, l)
                    if h < HS:
                        nc.scalar.activation(z[:, h, :], content(("z", h), l)[:, 0:TRI],
                                             ACT.Copy).then_inc(z_in.sem, 1)
                    if h >= 1:
                        g = h - 1
                        act.wait_ge(negabs.sem, negabs.at(l, g + 1))
                        if g >= 2:
                            act.wait_ge(sp_done.sem, sp_done.at(l, g - 1))
                        nc.scalar.activation(lnt[:, g % 2, :], sp[:, g, :], ACT.Exp).then_inc(act_step, 1)
                        act.wait_ge(act_step, g + 1)
                        nc.scalar.activation(lnt[:, g % 2, :], lnt[:, g % 2, :], ACT.Ln,
                                             bias=ones[:, 0:1]).then_inc(ln_done.sem, 1)
                for t in range(TT):
                    leave(("sv", t), l, sv[:, t, :], sv_in)
                high_parts(16, 19)
                for h in range(HS):
                    act.wait_ge(logw.sem, logw.at(l, h + 1))
                    nc.scalar.activation(sp[:, h, :], z[:, h, :], ACT.Exp).then_inc(w_exp.sem, 1)
                    if h == 3:
                        high_part(20, l)
                high_parts(21, 21)
                for half in range(2):
                    for t in range(TT):
                        leave((f"gr{half}", t), l, gr[:, t, half * 512:(half + 1) * 512], gr_in)
                    if half == 0:
                        high_parts(22, 23)
                for hp in range(HS // 2):
                    leave_high(("so", hp), l, sbT[:, hp, :], sbT_high)
                high_parts(24, 24)
                act.wait_ge(rg_in.sem, rg_in.at(l, 4))
                for t in range(TT):
                    nc.scalar.activation(rg[:, t, :], rg[:, t, :], ACT.Silu).then_inc(rg_silu.sem, 1)
                high_parts(25, 25)
                act.wait_ge(gr_in.sem, gr_in.at(l, 4))
                for t in range(TT):
                    nc.scalar.activation(gr[:, t, :], gr[:, t, :], ACT.Sigmoid).then_inc(gates.sem, 1)
                high_parts(26, 27)
                for kp in range(4):
                    leave_high(("rT", kp), l, flat(retT[:, 2 * kp:2 * kp + 2, :]), rT_act)
                high_parts(28, 28)
                act.wait_ge(gs_in.sem, gs_in.at(l, 4))
                for t in range(TT):
                    nc.scalar.activation(gs[:, t, :], gs[:, t, :], ACT.Sigmoid).then_inc(gates.sem, 1)
                high_parts(29, 33)
                for kp in range(4):
                    leave_high(("mT", kp), l, flat(T8[:, 2 * kp:2 * kp + 2, :]), mT_act)
                high_parts(34, 37)
                square_sums(l, 2)
                high_parts(38, 38)
                norm_turned("nT2", l, 1)

                def gate(p, step):
                    for i in (2 * p, 2 * p + 1):
                        acc = content(("gu", i), l, step)
                        if i >= 4:
                            act.wait_ge(gu_mul.sem, gu_mul.at(l, i - 3) + step * 4)
                        nc.scalar.activation(silu_g[:, i % 4, :], acc[:, 0:SEQ], ACT.Silu).then_inc(g_silu.sem, 1)

                first = order.index(("gate", 2))
                high_parts(first - 2, first - 2)
                gate(0, 0)
                high_parts(first - 1, first)
                gate(1, 0)
                with act.Fori(0, (PAIRS - 3) // 2) as it:
                    for p in (2, 3):
                        for n in range(3):
                            high_part(first + 1 + 3 * (p - 2) + n, l, it)
                        gate(p, it)
                high_parts(len(order) - 3, len(order) - 1)
                gate(PAIRS - 1, 0)
            square_sums(LAYERS, 0)

            def content2(key, l):
                act.wait_ge(filled[banks2[key]], banks2.before(key, l) + 1)
                return bank2(key)

            def leave2(key, l, to, signal_, rows=P, width=512, scale=1.0, at=0):
                acc = content2(key, l)[0:rows, at:at + width]
                nc.scalar.activation(to, acc, ACT.Copy, scale=scale).then_inc(signal_.sem, 1)

            def high_parts2(first, last, l):
                for n in range(first, last + 1):
                    high_part2(n, l)

            def leave_high2(name, l):
                for kp in range(4):
                    nc.scalar.activation(split(flat(T8[:, 2 * kp:2 * kp + 2, :])), content2((name, kp), l),
                                         ACT.Copy).then_inc(bT_high.sem, 1)

            act.sem_inc(yg_in.sem, 1)
            with act.Fori(0, LAYERS) as l:
                high_parts2(0, 2, l)
                leave_high2("xT", l)
                high_parts2(3, 3, l)

                def chunk(name):
                    at, width = COL2[name]
                    for t in range(TT):
                        leave2((name, t), l, U[:, t, at:at + width], u_act, width=width)

                chunk("C")
                high_parts2(4, 5, l)
                act.wait_ge(u_dve.sem, u_dve.at(l, 2))
                for n, (lo, hi) in enumerate(((0, 256), (256, 384))):
                    for t in range(TT):
                        nc.scalar.activation(relu[:, t, lo:hi], U[:, t, lo:hi], ACT.Square,
                                             accum_out=lstat[:, 0, 2 * n + t:2 * n + t + 1]).then_inc(latent_sq.sem, 1)
                high_parts2(6, 7, l)
                chunk("B")
                high_parts2(8, 9, l)
                leave2(("qiT", 0), l, flat(qiT), qiT_in)
                act.wait_ge(params_in.sem, params_in.at(l, 16 * N_PARAMS))
                for k in range(2):
                    leave2(("cT", 0), l, cT[:, k, :], cT_in, width=SEQ, scale=cgain[:, k:k + 1], at=k * SEQ)
                leave2(("cT", 1), l, cT[:, 2, :], cT_in, width=SEQ, scale=cgain[:, 2:3])
                high_parts2(10, 11, l)
                chunk("q1")
                high_parts2(12, 12, l)
                for h in range(HI):
                    acc = content2(("rel", h), l)[:, 0:TRI]
                    if h >= 2:
                        act.wait_ge(score_in.sem, score_in.at(l, h - 1))
                    nc.scalar.activation(relu[:, h % 2, :], acc, ACT.Relu).then_inc(relu_in.sem, 1)
                for i in range(4):
                    t, half = divmod(i, 2)
                    leave2(("uq", i), l, mq[:, t, half * 384:(half + 1) * 384], mq_in, width=384)
                high_parts2(13, 15, l)
                chunk("k1")
                high_parts2(16, 17, l)
                for b in range(4):
                    leave2(("mqT", b), l, flat(mqT[0:96, 2 * b:2 * b + 2, :]), mqT_in, rows=96)
                high_parts2(18, 19, l)
                chunk("v1")
                leave2(("dsT", 0), l, flat(dsT), dsT_in)
                for b in range(3):
                    leave2(("dqT", b), l, flat(dqT[:, 2 * b:2 * b + 2, :]), dqT_in)
                high_parts2(20, 20, l)
                for j in range(JOBS + 1):
                    if j < JOBS:
                        act.wait_ge(masked.sem, masked.at(l, 3 * j + 3))
                        first = (0, P, TRI) if j < HM + HX else (2 * TRI, 3 * TRI, 2 * TRI)
                        second = (P, TRI) if j < HM + HX else (0, 2 * TRI)
                        for t, (lo, hi) in enumerate((first[0:2], second)):
                            last = nc.scalar.activation(S[:, j % 2, lo:hi], S[:, j % 2, lo:hi], ACT.Exp, scale=-1.0,
                                                        bias=nmx[:, j, t:t + 1], accum_out=lsum[:, j, t:t + 1])
                        last.then_inc(weighed.sem, 1)
                    if j > HM + HX:
                        leave2(("E", j - 1, 0), l, ET[:, (j - 1) % 2, 0:512], ET_act)
                leave_high2("oT", l)
                high_parts2(21, 21, l)
                act.wait_ge(x_ready.sem, x_ready.at(l, 2))
                for t in range(TT):
                    nc.scalar.activation(xn[:, t, :], H[:, t, :], ACT.Copy, scale=ALPHA).then_inc(resid_in.sem, 1)
                for kp in (0, 2):
                    leave2(("xT2", kp), l, flat(T8[:, 2 * kp:2 * kp + 2, :]), xT2_act)
                act.wait_ge(shift_done.sem, shift_done.at(l, 1))
                nc.scalar.activation(gexp, shifted, ACT.Exp).then_inc(gexp_done.sem, 1)
                act.wait_ge(diff_done.sem, diff_done.at(l, 1))
                nc.scalar.activation(diff[:, 1, :], diff[:, 0, :], ACT.Exp).then_inc(eexp_done.sem, 1)
                wait_apart(act, npass_done.sem, npass_done.at(l, 1))
                passes = act.value_load(npass[0:1, 0:1], min_val=1, max_val=2)
                with act.Fori(0, 2) as ps_:
                    lp = l * 2 + ps_

                    def content_p(g, name, *key):
                        act.wait_ge(filled[banks2[(name, 0) + key]],
                                    pass_turn(name, key, l, ps_, g) + 1)
                        return bank2((name, 0) + key)

                    def expert_high(e, g, kinds=(0, 1)):
                        for n in kinds:
                            name = KINDS[n]
                            act.wait_ge(*expert_landed(name, e, l, ps_, g))
                            nc.scalar.activation(split(ehigh[e % 2][:, n, :]),
                                                 slots_at(units2[name, 0, 0, e], 1)[:, 0, :],
                                                 ACT.Copy).then_inc(ehigh_done.sem, 1)

                    def group(g, last):
                        for b in range(2):
                            nc.scalar.activation(split(flat(XG[:, 4 * b:4 * b + 4, :])),
                                                 content_p(g, "xg", 0, b), ACT.Copy).then_inc(xg_high.sem, 1)
                        for e in range(EXPERTS + 1):
                            following = (e + 1, g) if e < EXPERTS - 1 else (0, g + 1) if e < EXPERTS and not last else None
                            if following:
                                expert_high(*following, kinds=(0,))
                            if e >= 1:
                                acc = content_p(g, "hT", 0, e - 1)
                                nc.scalar.activation(hT[:, (e - 1) % 2, :], acc[:, 0:2 * P],
                                                     ACT.Copy).then_inc(hT_in.sem, 1)
                            if following:
                                expert_high(*following, kinds=(1,))
                            if e < EXPERTS:
                                acc = content_p(g, "gu", 0, e)
                                if e >= 2:
                                    act.wait_ge(h2_done.sem, h2_done.at(lp, e - 1) + g * EXPERTS)
                                nc.scalar.activation(sg[:, e % 2, :], acc[:, 0:EH],
                                                     ACT.Silu).then_inc(g2_silu.sem, 1)
                        for half in range(2):
                            nc.scalar.activation(
                                YG[:, bass.ds(g, 1), half * 512:(half + 1) * 512].rearrange("p a n -> p (a n)"),
                                content_p(g, "yg", 0, half), ACT.Copy).then_inc(yg_in.sem, 1)

                    with act.If(passes > ps_):
                        nc.scalar.activation(flat(pickT[:, 0:2, :]), content_p(0, "pT", 0),
                                             ACT.Copy).then_inc(pickT_in.sem, 1)
                        expert_high(0, 0)
                        with act.Fori(0, GROUPS - 1) as g:
                            group(g, False)
                        group(GROUPS - 1, True)
                    with act.Else():
                        act.drain()
                        for signal_, n in ((pickT_in, 1), (xg_high, 2 * GROUPS),
                                           (ehigh_done, 2 * GROUPS * EXPERTS), (g2_silu, GROUPS * EXPERTS),
                                           (hT_in, GROUPS * EXPERTS), (yg_in, 2 * GROUPS)):
                            act.sem_inc(signal_.sem, n)

        @block.vector
        def _(dve):
            def content(key, l, more=0):
                dve.wait_ge(filled[banks[key]], banks.before(key, l, more) + 1)
                return bank_of(key)

            def normalise(l, k0):
                dve.wait_ge(sumsq.sem, sumsq.at(l, k0 + 2))
                nc.vector.tensor_scalar(stat[:, 2:4], stat[:, 0:2], 1.0 / D, EPS, ALU.mult,
                                        ALU.add).then_inc(meansq.sem, 1)
                dve.wait_ge(rms.sem, rms.at(l, k0 // 2 + 1))
                for t in range(TT):
                    nc.vector.tensor_scalar(xn[:, t, :], H[:, t, :], stat[:, 4 + t:5 + t], None,
                                            ALU.mult).then_inc(xn_done.sem, 1)

            def norm_turned(name, l, w):
                content((name, 3), l)
                for kp in range(4):
                    acc = content((name, kp), l)
                    for j in range(2):
                        k = 2 * kp + j
                        if j == 0:
                            dve.wait_ge(nT_act.sem, nT_act.at(l, 8 * w + k + 2))
                        nc.vector.scalar_tensor_tensor(out=split(T8low[:, k, :]),
                                                       in0=acc[:, j * SEQ:(j + 1) * SEQ],
                                                       scalar=gains[:, w, k:k + 1], in1=split(T8[:, k, :]), op0=ALU.mult,
                                                       op1=ALU.subtract).then_inc(nT_dve.sem, 1)

            def leave_low(key, l, to, high_, high_signal, k, signal_):
                dve.wait_ge(high_signal.sem, high_signal.at(l, k))
                nc.vector.tensor_tensor(split(to), content(key, l)[:, 0:to.shape[1]], split(high_),
                                        ALU.subtract).then_inc(signal_.sem, 1)

            def leave(key, l, to, signal_):
                nc.vector.tensor_copy(to, content(key, l)).then_inc(signal_.sem, 1)

            def rotate(name, which, t, l):
                n = 2 * which + t
                acc = content((name, t), l).rearrange("p (h d) -> p h d", h=HR)
                half = DK // 2
                if n >= 2:
                    dve.wait_ge(roped.sem, roped.at(l, n - 1))
                o = rot[:, t, :].rearrange("p (h d) -> p h d", h=HR)
                nc.vector.tensor_tensor(qk[:, which, t, :].rearrange("p (h d) -> p h d", h=HR), acc,
                                        rope1[:, t, 0:DK].unsqueeze(1).to_broadcast([P, HR, DK]), ALU.mult)
                nc.vector.tensor_tensor(o[:, :, 0:half], acc[:, :, half:DK],
                                        rope1[:, t, DK:DK + half].unsqueeze(1).to_broadcast([P, HR, half]), ALU.mult)
                nc.vector.tensor_tensor(o[:, :, half:DK], acc[:, :, 0:half],
                                        rope1[:, t, DK + half:2 * DK].unsqueeze(1).to_broadcast([P, HR, half]),
                                        ALU.mult).then_inc(rotated.sem, 1)

            def flat(a):
                return a.rearrange("p a n -> p (a n)")

            nc.vector.memset(ones[:], 1.0)
            nc.vector.memset(minus_half[:], -0.5).then_inc(const_set, 1)
            dve.wait_ge(first_in, N_FIRST * 16)
            two_pi = 2 * np.pi
            c1 = 6.28125
            c2 = float(np.float32(np.round((two_pi - c1) * 2 ** 20) / 2 ** 20))
            c3 = float(np.float32(two_pi - c1 - c2))
            n_steps = [0]

            def table(ins):
                n_steps[0] += 1
                ins.then_inc(table_step, 1)
                dve.wait_ge(table_step, n_steps[0])

            ang, whole, over = turns_[:, 0], turns_[:, 1], turns_[:, 2]
            edge = 3.1415925
            table(nc.vector.tensor_copy(pos[:], pos_i[:]))
            for t in range(TT):
                table(nc.vector.tensor_scalar(ang[:, t, :], freq[:, 0, :], pos[:, t:t + 1], None, ALU.mult))
            table(nc.vector.tensor_scalar(whole, ang, 1.0 / two_pi, MAGIC, ALU.mult, ALU.add))
            table(nc.vector.tensor_scalar(whole, whole, -MAGIC, None, ALU.add))
            for c in (c1, c2, c3):
                table(nc.vector.scalar_tensor_tensor(out=ang, in0=whole, scalar=-c, in1=ang, op0=ALU.mult, op1=ALU.add))
            table(nc.vector.tensor_scalar(ang, ang, -edge, edge, ALU.max, ALU.min))
            table(nc.vector.tensor_scalar(whole, ang, np.pi / 2, None, ALU.add))
            table(nc.vector.tensor_scalar(over, whole, np.pi, -two_pi, ALU.is_gt, ALU.mult))
            table(nc.vector.tensor_tensor(whole, whole, over, ALU.add))
            nc.vector.tensor_scalar(whole, whole, -edge, edge, ALU.max, ALU.min).then_inc(table_done, 1)
            dve.wait_ge(x_in, 16)
            dve.sem_inc(h_added.sem, 3)
            dve.wait_ge(table_done, 3)
            for t in range(TT):
                table(nc.vector.tensor_tensor(rotation[1][:, t, :], rotation[1][:, t, :], freq[:, 1, :], ALU.mult))
            with dve.Fori(0, LAYERS) as l:
                def low_parts(first, last):
                    for n in range(first, last + 1):
                        low_part(n, l)

                dve.sem_clear(dve_step)
                normalise(l, 0)
                low_parts(0, 0)
                dve.wait_ge(gains_in.sem, gains_in.at(l, 32))
                norm_turned("nT", l, 0)
                low_parts(1, 2)
                dve.wait_ge(const_in, N_CONST * 16)
                for which, name in enumerate(("rq", "rk")):
                    low_parts(*((3, 3), (4, 5))[which])
                    for t in range(TT):
                        rotate(name, which, t, l)
                low_parts(6, 11)
                for b in range(2):
                    leave(("kT", b), l, flat(kT[:, 2 * b:2 * b + 2, :]), kT_in)
                low_parts(12, 13)
                for h in range(HR):
                    nc.vector.tensor_tensor(ST[:, h, :], content(("rs", h), l)[:, 0:TRI], decay[:, h, :],
                                            ALU.mult).then_inc(st_in.sem, 1)
                for h in range(HS + 1):
                    if h < HS:
                        dve.wait_ge(z_in.sem, z_in.at(l, h + 1))
                        nc.vector.scalar_tensor_tensor(out=sp[:, h, :], in0=z[:, h, :], scalar=-1.0,
                                                       in1=z[:, h, :], op0=ALU.mult,
                                                       op1=ALU.min).then_inc(negabs.sem, 1)
                    if h >= 1:
                        g = h - 1
                        dve.wait_ge(ln_done.sem, ln_done.at(l, g + 1))
                        nc.vector.scalar_tensor_tensor(out=sp[:, g, :], in0=z[:, g, :], scalar=0.0,
                                                       in1=lnt[:, g % 2, :], op0=ALU.max,
                                                       op1=ALU.add).then_inc(sp_done.sem, 1)
                    if h == 3:
                        low_part(14, l)
                    if h == 6:
                        low_part(15, l)
                for t in range(TT):
                    leave(("rg0", t), l, rg[:, t, 0:512], rg_in)
                low_parts(16, 17)
                steps = 0
                for h in range(HR + 1):
                    if h < HR:
                        acc = content(("ro", h), l)
                        for t in range(TT):
                            nc.vector.bn_stats(moments[:, h, t, :], acc[:, t * DV:(t + 1) * DV]).then_inc(dve_step, 1)
                            steps += 1
                        dve.wait_ge(dve_step, steps)
                        for t in range(TT):
                            last = nc.vector.bn_aggr(mv[:, h, t, :], moments[:, h, t, :])
                        last.then_inc(head_var.sem, 1)
                    if h >= 1:
                        g = h - 1
                        dve.wait_ge(head_rstd.sem, head_rstd.at(l, g + 1))
                        acc = bank_of(("ro", g))
                        for t in range(TT):
                            last = nc.vector.tensor_scalar(retn[:, t, g * DV:(g + 1) * DV],
                                                           acc[:, t * DV:(t + 1) * DV], mv[:, g, t, 0:1],
                                                           rstd[:, g, t:t + 1], ALU.subtract, ALU.mult)
                        last.then_inc(ret_normed.sem, 1)
                for t in range(TT):
                    leave(("rg1", t), l, rg[:, t, 512:D], rg_in)
                low_parts(18, 19)
                for h in range(HS):
                    nc.vector.tensor_tensor(z[:, h, :], z[:, h, :], content(("c", h), l)[:, 0:TRI],
                                            ALU.subtract).then_inc(logw.sem, 1)
                    if h == 3:
                        low_part(20, l)
                low_parts(21, 23)
                for hp in range(HS // 2):
                    leave_low(("so", hp), l, sbTlow[:, hp, :], sbT[:, hp, :], sbT_high, hp + 1, sbT_in)
                low_parts(24, 24)
                dve.wait_ge(ret_normed.sem, ret_normed.at(l, HR))
                for t in range(TT):
                    dve.wait_ge(rg_silu.sem, rg_silu.at(l, t + 1))
                    nc.vector.tensor_tensor(retn[:, t, :], retn[:, t, :], rg[:, t, :],
                                            ALU.mult).then_inc(ret_gated.sem, 1)
                low_parts(25, 25)
                for half in range(2):
                    for t in range(TT):
                        leave((f"gs{half}", t), l, gs[:, t, half * 512:(half + 1) * 512], gs_in)
                    if half == 0:
                        low_parts(26, 26)
                for kp in range(4):
                    leave_low(("rT", kp), l, flat(retTlow[:, 2 * kp:2 * kp + 2, :]),
                              flat(retT[:, 2 * kp:2 * kp + 2, :]), rT_act, kp + 1, rT_dve)
                low_parts(27, 31)
                dve.wait_ge(gates.sem, gates.at(l, 4))
                for i in range(4):
                    t, cols = i // 2, slice(i % 2 * 512, (i % 2 + 1) * 512)
                    nc.vector.tensor_tensor(xn[:, t, cols], content(("ret", i), l), gr[:, t, cols],
                                            ALU.mult).then_inc(ret_out.sem, 1)
                low_parts(32, 33)
                for i in range(4):
                    t, cols = i // 2, slice(i % 2 * 512, (i % 2 + 1) * 512)
                    nc.vector.tensor_tensor(gs[:, t, cols], content(("sb", i), l), gs[:, t, cols],
                                            ALU.mult).then_inc(sb_gated.sem, 1)
                for t in range(TT):
                    dve.wait_ge(ret_out.sem, ret_out.at(l, 2 * t + 2))
                    dve.wait_ge(sb_gated.sem, sb_gated.at(l, 2 * t + 2))
                    nc.vector.tensor_tensor(xn[:, t, 512:D], xn[:, t, 512:D], gs[:, t, 512:D],
                                            ALU.add).then_inc(merged.sem, 1)
                content(("mT", 3), l)
                for kp in range(4):
                    leave_low(("mT", kp), l, flat(T8low[:, 2 * kp:2 * kp + 2, :]),
                              flat(T8[:, 2 * kp:2 * kp + 2, :]), mT_act, kp + 1, mT_dve)
                low_parts(34, 37)

                def add_to_h(name):
                    for i in range(4):
                        t, cols = i // 2, slice(i % 2 * 512, (i % 2 + 1) * 512)
                        nc.vector.tensor_tensor(H[:, t, cols], content((name, i), l), H[:, t, cols],
                                                ALU.add).then_inc(h_added.sem, 1)

                add_to_h("wo")
                normalise(l, 2)
                norm_turned("nT2", l, 1)
                low_parts(38, 38)

                def gate_times_up(p, step):
                    for i in (2 * p, 2 * p + 1):
                        if i >= 4:
                            dve.wait_ge(gu_done.sem, gu_done.at(l, i - 3) + step * 4)
                        dve.wait_ge(g_silu.sem, g_silu.at(l, i + 1) + step * 4)
                        nc.vector.tensor_tensor(gu_full[:, i % 4, :], bank_of(("gu", i))[:, SEQ:2 * SEQ],
                                                silu_g[:, i % 4, :], ALU.mult).then_inc(gu_mul.sem, 1)

                first = order.index(("gate", 2))
                low_parts(first - 2, first - 2)
                gate_times_up(0, 0)
                low_parts(first - 1, first)
                gate_times_up(1, 0)
                with dve.Fori(0, (PAIRS - 3) // 2) as it:
                    for p in (2, 3):
                        for n in range(3):
                            low_part(first + 1 + 3 * (p - 2) + n, l, it)
                        gate_times_up(p, it)
                low_parts(len(order) - 3, len(order) - 1)
                gate_times_up(PAIRS - 1, 0)
                add_to_h("ffn")
            dve.wait_ge(h_added.sem, h_added.at(LAYERS, 0))
            normalise(LAYERS, 0)
            dve.wait_ge(xn_done.sem, xn_done.at(LAYERS, 2))
            for t in range(TT):
                nc.vector.tensor_tensor(H[:, t, :], xn[:, t, :], gfinal, ALU.mult).then_inc(x_ready.sem, 1)

            def content2(key, l):
                dve.wait_ge(filled[banks2[key]], banks2.before(key, l) + 1)
                return bank2(key)

            def leave2(key, l, to, signal_, rows=P, width=512):
                nc.vector.tensor_copy(to, content2(key, l)[0:rows, 0:width]).then_inc(signal_.sem, 1)

            def rotate2(x, table, n, l):
                at, half = ROT[table]
                heads = x.shape[2]
                if n > 1:
                    dve.wait_ge(r_add.sem, r_add.at(l, n - 1))
                a, b = (buf[:, 0:TT * heads * 2 * half].rearrange("p (t h d) -> p t h d", t=TT, h=heads)
                        for buf in (ra, rbuf))

                def tab(which, lo, hi):
                    return rotation[which][:, :, at + lo:at + hi].unsqueeze(2).to_broadcast([P, TT, heads, hi - lo])

                nc.vector.tensor_tensor(a, x[:, :, :, 0:2 * half], tab(0, 0, 2 * half), ALU.mult)
                nc.vector.tensor_tensor(b[:, :, :, 0:half], x[:, :, :, half:2 * half], tab(1, 0, half), ALU.mult)
                nc.vector.tensor_tensor(b[:, :, :, half:2 * half], x[:, :, :, 0:half], tab(1, half, 2 * half),
                                        ALU.mult).then_inc(r_mul.sem, 1)

            with dve.Fori(0, LAYERS) as l:
                dve.sem_clear(dve_step)
                steps = [0]

                def step(ins):
                    steps[0] += 1
                    ins.then_inc(dve_step, 1)
                    dve.wait_ge(dve_step, steps[0])

                def low_parts2(first, last):
                    for n in range(first, last + 1):
                        low_part2(n, l)

                def leave_low2(name, n):
                    content2((name, 3), l)
                    for kp in range(4):
                        dve.wait_ge(bT_high.sem, bT_high.at(l, 4 * n + kp + 1))
                        nc.vector.tensor_tensor(split(flat(T8low[:, 2 * kp:2 * kp + 2, :])),
                                                content2((name, kp), l), split(flat(T8[:, 2 * kp:2 * kp + 2, :])),
                                                ALU.subtract).then_inc(bT_low.sem, 1)

                low_parts2(0, 0)
                leave_low2("xT", 0)
                low_parts2(1, 3)

                def chunk(name):
                    at, width = COL2[name]
                    for t in range(TT):
                        leave2((name, t), l, U[:, t, at:at + width], u_dve, width=width)

                dve.wait_ge(u_act.sem, u_act.at(l, 2))
                rotate2(U[:, :, 800:1088].rearrange("p t (h d) -> p t h d", h=9), "idx", 1, l)
                low_parts2(4, 5)
                chunk("A")
                dve.wait_ge(latent_sq.sem, latent_sq.at(l, 4))
                for n, width in enumerate((QR, KVR)):
                    last = nc.vector.tensor_scalar(lstat[:, 1, 2 * n:2 * n + 2], lstat[:, 0, 2 * n:2 * n + 2],
                                                   1.0 / width, EPS, ALU.mult, ALU.add)
                last.then_inc(latent_ms.sem, 1)
                rotate2(U[:, :, 384:416].unsqueeze(2), "mla", 2, l)
                dve.wait_ge(latent_rms.sem, latent_rms.at(l, 1))
                for n, (lo, hi) in enumerate(((0, 256), (256, 384))):
                    for t in range(TT):
                        last = nc.vector.tensor_scalar(U[:, t, lo:hi], U[:, t, lo:hi],
                                                       lstat[:, 2, 2 * n + t:2 * n + t + 1], None, ALU.mult)
                last.then_inc(latent_done.sem, 1)
                low_parts2(6, 7)
                dve.wait_ge(u_act.sem, u_act.at(l, 4))
                rotate2(U[:, :, 416:736].rearrange("p t (h d) -> p t h d", h=5), "head", 3, l)
                low_parts2(8, 9)
                chunk("q0")
                leave2(("kkT", 0), l, flat(kkT), kkT_in)
                low_parts2(10, 12)
                dve.wait_ge(wi_done.sem, wi_done.at(l, 1))
                for h in range(HI):
                    if h >= 1:
                        dve.wait_ge(score_in.sem, score_in.at(l, h))
                    dve.wait_ge(relu_in.sem, relu_in.at(l, h + 1))
                    for t, (lo, hi) in enumerate(((0, P), (P, TRI))):
                        w = U[:, t, 1088 + h:1089 + h]
                        if h == 0:
                            last = nc.vector.tensor_scalar(score[:, lo:hi], relu[:, 0, lo:hi], w, None, ALU.mult)
                        else:
                            last = nc.vector.scalar_tensor_tensor(out=score[:, lo:hi], in0=relu[:, h % 2, lo:hi],
                                                                  scalar=w, in1=score[:, lo:hi], op0=ALU.mult,
                                                                  op1=ALU.add)
                    last.then_inc(score_in.sem, 1)
                for i in range(4):
                    t, half = divmod(i, 2)
                    acc = content2(("ukv", i), l).rearrange("p (h d) -> p h d", h=4)
                    nc.vector.tensor_copy(mk[:, t, half * 384:(half + 1) * 384].rearrange(
                        "p (h d) -> p h d", h=4)[:, :, 0:NOPE], acc[:, :, 0:NOPE])
                    nc.vector.tensor_copy(mvv[:, t, half * 256:(half + 1) * 256].rearrange(
                        "p (h d) -> p h d", h=4), acc[:, :, NOPE:NOPE + VM]).then_inc(mk_in.sem, 1)
                dve.wait_ge(mq_in.sem, mq_in.at(l, 4))
                rotate2(mq.rearrange("p t (h d) -> p t h d", h=HM)[:, :, :, NOPE:NOPE + ROPE], "mla", 4, l)
                chunk("k0")
                low_parts2(13, 13)
                wait_apart(dve, score_masked.sem, score_masked.at(l, 1))
                tiles = ((0, P), (P, TRI))
                for round_ in range(TOP_K // 8):
                    if round_ in (2, 5):
                        low_part2(14 + round_ // 5, l)
                    for t, (lo, hi) in enumerate(tiles):
                        last = nc.vector.max(best[:, t, :], score[:, lo:hi])
                    step(last)
                    for t, (lo, hi) in enumerate(tiles):
                        last = nc.vector.match_replace(score[:, lo:hi], best[:, t, :], score[:, lo:hi], TAKEN)
                    step(last)
                nc.vector.tensor_scalar(nm, score, TAKEN / 2, FAR, ALU.is_gt, ALU.mult).then_inc(topk_done.sem, 1)
                low_parts2(16, 17)
                chunk("v0")
                dve.wait_ge(u_act.sem, u_act.at(l, 8))
                dve.wait_ge(u_dve.sem, u_dve.at(l, 6))
                rotate2(U[:, :, 1096:2632].rearrange("p t (h d) -> p t h d", h=24), "head", 5, l)
                for b in range(4):
                    leave2(("mkT", b), l, flat(mkT[0:96, 2 * b:2 * b + 2, :]), mkT_in, rows=96)
                low_parts2(18, 19)
                for b in range(3):
                    leave2(("dkT", b), l, flat(dkT[:, 2 * b:2 * b + 2, :]), dkT_in)
                low_parts2(20, 20)
                dve.wait_ge(nm_masked.sem, nm_masked.at(l, 1))
                for j in range(JOBS + 1):
                    if j < JOBS:
                        if j >= 2:
                            key = ("E", j - 2, parts(j - 2) - 1)
                            dve.wait_ge(filled[banks2[key]], banks2.before(key, l) + 1)
                        scale = -((NOPE + ROPE) ** -0.5) if j < HM else -(HD ** -0.5)
                        if j < HM + HX:
                            m = causal_m if j < HM else nm
                            acc = content2(("S", j, 0), l)
                            dve.sem_inc(passed, 1)
                            for t, (lo, hi) in enumerate(tiles):
                                last = nc.vector.tensor_tensor_reduce(S[:, j % 2, lo:hi], acc[:, lo:hi], m[:, lo:hi],
                                                                      scale, 3e38, ALU.add, ALU.min,
                                                                      nmx[:, j, t:t + 1])
                            last.then_inc(masked.sem, 3)
                        else:
                            for part, lo, hi, least, start in ((0, 0, 512, 2, None), (1, 512, 768, 1, 2),
                                                               (2, 768, 1152, 0, None)):
                                acc = content2(("S", j, part), l)
                                if start is not None:
                                    dve.wait_ge(masked.sem, masked.at(l, 3 * j + 1))
                                dve.sem_inc(passed, 1)
                                nc.vector.tensor_tensor_reduce(
                                    S[:, j % 2, lo:hi], acc[:, 0:hi - lo], near_m[:, lo:hi], scale,
                                    3e38 if start is None else nmx[:, j, start:start + 1], ALU.add, ALU.min,
                                    nmx[:, j, least:least + 1]).then_inc(masked.sem, 1)
                    if j >= 1:
                        i = j - 1
                        if i < HM + HX:
                            leave2(("E", i, 0), l, ET[:, i % 2, 0:TRI], ET_dve, width=TRI)
                        else:
                            leave2(("E", i, 1), l, ET[:, i % 2, 512:768], ET_dve, width=256)
                            leave2(("E", i, 2), l, ET[:, i % 2, 768:1152], ET_dve, width=TRI)
                dve.wait_ge(weighed.sem, weighed.at(l, JOBS))
                step(nc.vector.reciprocal(rinv, lsum))
                for i in range(4):
                    g8, t = divmod(i, 2)
                    nc.vector.tensor_tensor(
                        xn[:, t, g8 * 512:(g8 + 1) * 512].rearrange("p (h d) -> p h d", h=8),
                        content2(("O", i), l).rearrange("p (h d) -> p h d", h=8),
                        rinv[:, 8 * g8:8 * g8 + 8, t:t + 1].to_broadcast([P, 8, HD]), ALU.mult).then_inc(mix_done.sem, 1)
                leave_low2("oT", 1)
                low_parts2(21, 21)
                for i in range(4):
                    t, cols = i // 2, slice(i % 2 * 512, (i % 2 + 1) * 512)
                    nc.vector.scalar_tensor_tensor(out=H[:, t, cols], in0=H[:, t, cols], scalar=ALPHA,
                                                   in1=content2(("wo", i), l), op0=ALU.mult,
                                                   op1=ALU.add).then_inc(wo_in.sem, 1)

                def moments_of(buf, i):
                    t, a = divmod(i, 2)
                    return nc.vector.bn_stats(moments2[:, t, a, :], buf[:, t, a * 512:(a + 1) * 512])

                def layer_norm(buf, n):
                    for t in range(TT):
                        last = nc.vector.bn_aggr(mv2[:, t, :], moments2[:, t, :, :])
                    last.then_inc(stat_done.sem, 1)
                    dve.wait_ge(stat_done.sem, stat_done.at(l, n + 1))
                    for t in range(TT):
                        nc.vector.scalar_tensor_tensor(out=H[:, t, :], in0=buf[:, t, :], scalar=mv2[:, t, 0:1],
                                                       in1=lng[:, 0, :], op0=ALU.subtract,
                                                       op1=ALU.mult).then_inc(gained.sem, 1)
                    dve.wait_ge(rstd_done.sem, rstd_done.at(l, n + 1))
                    for t in range(TT):
                        dve.wait_ge(gained.sem, gained.at(l, 2 * n + t + 1))
                        nc.vector.scalar_tensor_tensor(out=H[:, t, :], in0=H[:, t, :], scalar=rstd2[:, t:t + 1],
                                                       in1=lng[:, 1, :], op0=ALU.mult,
                                                       op1=ALU.add).then_inc(x_ready.sem, 1)

                for i in range(4):
                    dve.wait_ge(wo_in.sem, wo_in.at(l, i + 1))
                    last = moments_of(H, i)
                step(last)
                layer_norm(H, 0)
                for kp in (1, 3):
                    leave2(("xT2", kp), l, flat(T8[:, 2 * kp:2 * kp + 2, :]), xT2_dve)

                acc = content2(("router", 0), l)[:, 0:128].rearrange("p (t n) -> p t n", t=TT)
                nc.vector.tensor_tensor(logit, acc[:, :, 0:36], rb.unsqueeze(1).to_broadcast([P, TT, 36]),
                                        ALU.add).then_inc(logit_in.sem, 1)
                dve.wait_ge(logit_in.sem, logit_in.at(l, 1))
                step(nc.vector.tensor_reduce(hot_max, logit[:, :, 0:GROUPS], AX_X, ALU.max))
                nc.vector.tensor_tensor(shifted, logit[:, :, 0:GROUPS],
                                        hot_max.unsqueeze(2).to_broadcast([P, TT, GROUPS]),
                                        ALU.subtract).then_inc(shift_done.sem, 1)
                dve.wait_ge(shift_done.sem, shift_done.at(l, 1))
                step(nc.vector.tensor_scalar(eq, shifted, 0.0, None, ALU.is_ge))
                for t in range(TT):
                    last = nc.vector.tensor_tensor_scan(prefix[:, t, :], ones[:, 0:GROUPS], eq[:, t, :], 0.0,
                                                        ALU.mult, ALU.add)
                step(last)
                nc.vector.scalar_tensor_tensor(out=hot, in0=prefix, scalar=1.0, in1=eq, op0=ALU.is_equal,
                                               op1=ALU.mult).then_inc(hot_done.sem, 1)
                dve.wait_ge(hot_done.sem, hot_done.at(l, 1))
                step(nc.vector.tensor_tensor(sel4, logit[:, :, GROUPS:36].rearrange("p t (g e) -> p t e g", g=GROUPS),
                                             hot.unsqueeze(2).to_broadcast([P, TT, EXPERTS, GROUPS]), ALU.mult))
                step(nc.vector.tensor_reduce(sel, sel4, AX_X, ALU.add))
                for t in range(TT):
                    last = nc.vector.max(top[:, t, :], sel[:, t, :])
                step(last)
                nc.vector.tensor_tensor(diff[:, 0, :], top[:, :, 1], top[:, :, 0],
                                        ALU.subtract).then_inc(diff_done.sem, 1)
                acc = content2(("ranks", 0), l)
                step(nc.vector.tensor_tensor(crank, acc[:, 0:8].rearrange("p (t g) -> p t g", t=TT), hot, ALU.mult))
                nc.vector.tensor_reduce(rank, crank, AX_X, ALU.add).then_inc(rank_ready.sem, 1)
                step(nc.vector.tensor_reduce(npass_f[:, 0:1], acc[:, 8:12], AX_X, ALU.max))
                step(nc.vector.tensor_scalar(npass_f[:, 1:2], npass_f[:, 0:1], SLOTS + 0.5, 1.0, ALU.is_gt, ALU.add))
                nc.vector.tensor_copy(npass, npass_f[:, 1:2]).then_inc(npass_done.sem, 1)

                def make_picks(done):
                    dve.wait_ge(rank_ready.sem, rank_ready.at(l, 1) + done)
                    for g in range(GROUPS):
                        for t in range(TT):
                            last = nc.vector.tensor_scalar(pick[:, g, t, :], iota, rank[:, t:t + 1],
                                                           hot[:, t, g:g + 1], ALU.is_equal, ALU.mult)
                    last.then_inc(pick_done.sem, 1)

                make_picks(0)
                for t in range(TT):
                    last = nc.vector.max_index(topi[:, t, :], top[:, t, :], sel[:, t, :])
                step(last)
                step(nc.vector.tensor_copy(topf, topi))
                dve.wait_ge(gexp_done.sem, gexp_done.at(l, 1))
                dve.wait_ge(eexp_done.sem, eexp_done.at(l, 1))
                step(nc.vector.tensor_reduce(ptop[:, 0, :], gexp, AX_X, ALU.add))
                step(nc.vector.tensor_scalar(diff[:, 2, :], diff[:, 1, :], 1.0, None, ALU.add))
                step(nc.vector.reciprocal(ptop[:, 1, :], ptop[:, 0, :]))
                step(nc.vector.reciprocal(ptop[:, 0, :], diff[:, 2, :]))
                step(nc.vector.tensor_tensor(ptop[:, 2, :], ptop[:, 0, :], ptop[:, 1, :], ALU.mult))
                step(nc.vector.tensor_tensor(ptop[:, 3, :], ptop[:, 2, :], diff[:, 1, :], ALU.mult))
                for t in range(TT):
                    nc.vector.tensor_scalar(ge[:, t, :], iota[:, 0:EXPERTS], topf[:, t, 0:1], ptop[:, 2, t:t + 1],
                                            ALU.is_equal, ALU.mult)
                    last = nc.vector.tensor_scalar(ge2[:, t, :], iota[:, 0:EXPERTS], topf[:, t, 1:2],
                                                   ptop[:, 3, t:t + 1], ALU.is_equal, ALU.mult)
                step(last)
                step(nc.vector.tensor_tensor(ge, ge, ge2, ALU.add))
                nc.vector.tensor_tensor(gate, ge.unsqueeze(2).to_broadcast([P, TT, GROUPS, EXPERTS]),
                                        hot.unsqueeze(3).to_broadcast([P, TT, GROUPS, EXPERTS]),
                                        ALU.mult).then_inc(gate_done.sem, 1)
                wait_apart(dve, npass_done.sem, npass_done.at(l, 1))
                passes = dve.value_load(npass[0:1, 0:1], min_val=1, max_val=2)
                with dve.Fori(0, 2) as ps_:
                    lp = l * 2 + ps_

                    def content_p(g, name, *key):
                        dve.wait_ge(filled[banks2[(name, 0) + key]], pass_turn(name, key, l, ps_, g) + 1)
                        return bank2((name, 0) + key)

                    def expert_low(e, g):
                        for n, name in enumerate(("gate", "up")):
                            dve.wait_ge(ehigh_done.sem, ehigh_done.at(lp, 2 * e + n + 1) + g * (2 * EXPERTS))
                            slot = slots_at(units2[name, 0, 0, e], 1)[:, 0, :]
                            nc.vector.tensor_tensor(split(slot), slot, split(ehigh[e % 2][:, n, :]),
                                                    ALU.subtract).then_inc(elow_done.sem, 1)

                    def group(g, last):
                        for b in range(2):
                            dve.wait_ge(xg_high.sem, xg_high.at(lp, b + 1) + g * 2)
                            nc.vector.tensor_tensor(split(flat(XGlow[:, 4 * b:4 * b + 4, :])),
                                                    content_p(g, "xg", 0, b),
                                                    split(flat(XG[:, 4 * b:4 * b + 4, :])),
                                                    ALU.subtract).then_inc(xg_low.sem, 1)
                        dve.wait_ge(gslot_in.sem, gslot_in.at(lp, 1))
                        for e in range(EXPERTS):
                            if e < EXPERTS - 1:
                                expert_low(e + 1, g)
                            elif not last:
                                expert_low(0, g + 1)
                            acc = content_p(g, "gu", 0, e)
                            dve.wait_ge(g2_silu.sem, g2_silu.at(lp, e + 1) + g * EXPERTS)
                            at = g * EXPERTS + e
                            gate_ = gslot[:, at:at + 1] if isinstance(g, int) else gslot[:, bass.ds(at, 1)]
                            nc.vector.scalar_tensor_tensor(out=hh[:, e % 2, :], in0=sg[:, e % 2, :], scalar=gate_,
                                                           in1=acc[:, EH:2 * EH], op0=ALU.mult,
                                                           op1=ALU.mult).then_inc(h2_done.sem, 1)

                    with dve.If(passes > ps_):
                        nc.vector.tensor_copy(flat(pickT[:, 2:4, :]), content_p(0, "pT", 1)).then_inc(pickT_in.sem, 1)
                        expert_low(0, 0)
                        nc.vector.tensor_copy(gslot, content_p(0, "slots")[:, 0:GROUPS * EXPERTS]).then_inc(
                            gslot_in.sem, 1)
                        with dve.Fori(0, GROUPS - 1) as g:
                            group(g, False)
                        group(GROUPS - 1, True)
                        nc.vector.tensor_scalar(rank, rank, -float(SLOTS), None, ALU.add).then_inc(rank_ready.sem, 1)
                        make_picks(ps_ + 1)
                        dve.wait_ge(resid_in.sem, resid_in.at(l, TT))
                        for i in range(4):
                            t, cols = i // 2, slice(i % 2 * 512, (i % 2 + 1) * 512)
                            nc.vector.tensor_tensor(xn[:, t, cols], content_p(0, "sc", i), xn[:, t, cols],
                                                    ALU.add).then_inc(sc_added.sem, 1)
                            dve.wait_ge(sc_added.sem, sc_added.at(lp, i + 1))
                            moments_of(xn, i).then_inc(moe_moments.sem, 1)
                    with dve.Else():
                        dve.drain()
                        for signal_, n in ((pick_done, 1), (pickT_in, 1), (gslot_in, 1), (xg_low, 2 * GROUPS),
                                           (elow_done, 2 * GROUPS * EXPERTS),
                                           (h2_done, GROUPS * EXPERTS), (sc_added, 4), (moe_moments, 4), (rank_ready, 1)):
                            dve.sem_inc(signal_.sem, n)
                dve.wait_ge(moe_moments.sem, moe_moments.at(2 * l + 1, 4))
                wait_apart(dve, ln2_in.sem, ln2_in.at(l, 32))
                layer_norm(xn, 1)

        @block.gpsimd
        def _(pool):
            def inverse_rms(l, n):
                pool.wait_ge(meansq.sem, meansq.at(l, n + 1))
                nc.gpsimd.tensor_tensor(stat[:, 4:6], stat[:, 2:4], minus_half[:, 0:2], ALU.pow).then_inc(rms.sem, 1)

            def causal(h, wait, signal_, l):
                wait_apart(pool, wait.sem, wait.at(l, h + 1))
                blocks = sp[:, h, :].rearrange("p (a n) -> p a n", n=P)[:, 0:3:2, :]
                nc.gpsimd.affine_select(out=blocks, in_=blocks, pattern=[[0, 2], [1, P]], compare_op=ALU.is_gt,
                                        fill=0.0, base=0, channel_multiplier=-1).then_inc(signal_.sem, 1)

            pool.wait_ge(const_set, 1)
            with pool.Fori(0, LAYERS) as l:
                pool.sem_clear(pool_step)
                inverse_rms(l, 0)
                for which in range(2):
                    for t in range(TT):
                        pool.wait_ge(rotated.sem, rotated.at(l, 2 * which + t + 1))
                        nc.gpsimd.tensor_tensor(qk[:, which, t, :], qk[:, which, t, :], rot[:, t, :],
                                                ALU.add).then_inc(roped.sem, 1)
                for h in range(HS):
                    causal(h, sp_done, sp_masked, l)
                for h in range(HR):
                    wait_apart(pool, head_var.sem, head_var.at(l, h + 1))
                    nc.gpsimd.tensor_scalar(rstd[:, h, :], mv[:, h, :, 1], EPS, None, ALU.add).then_inc(pool_step, 1)
                    pool.wait_ge(pool_step, h + 1)
                    nc.gpsimd.tensor_tensor(rstd[:, h, :], rstd[:, h, :], minus_half[:, 0:2],
                                            ALU.pow).then_inc(head_rstd.sem, 1)
                for h in range(HS):
                    causal(h, w_exp, w_masked, l)
                for i in (0, 2):
                    t, cols = i // 2, slice(i % 2 * 512, (i % 2 + 1) * 512)
                    pool.wait_ge(ret_out.sem, ret_out.at(l, i + 1))
                    pool.wait_ge(sb_gated.sem, sb_gated.at(l, i + 1))
                    nc.gpsimd.tensor_tensor(xn[:, t, cols], xn[:, t, cols], gs[:, t, cols],
                                            ALU.add).then_inc(merged.sem, 1)
                inverse_rms(l, 1)

                def split_product(i, step):
                    if i >= 4:
                        pool.wait_ge(unit_read.sem, unit_read.at(l, said_at["down", (i - 4) // 2])
                                     + step * said_per_step)
                    wait_apart(pool, gu_mul.sem, gu_mul.at(l, i + 1) + step * 4)
                    nc.gpsimd.tensor_copy(split(guT[:, i % 4, :]), gu_full[:, i % 4, :]).then_inc(gu_high.sem, 1)
                    pool.wait_ge(gu_high.sem, gu_high.at(l, i + 1) + step * 4)
                    nc.gpsimd.tensor_tensor(split(guTlow[:, i % 4, :]), gu_full[:, i % 4, :], split(guT[:, i % 4, :]),
                                            ALU.subtract).then_inc(gu_done.sem, 1)

                for i in range(4):
                    split_product(i, 0)
                with pool.Fori(0, (PAIRS - 3) // 2) as it:
                    for i in range(4, 8):
                        split_product(i, it)
                for i in range(2 * PAIRS - 2, 2 * PAIRS):
                    split_product(i, 0)
            inverse_rms(LAYERS, 0)

            def add_rotation(x, n, half, l):
                heads = x.shape[2]
                a, b = (buf[:, 0:TT * heads * 2 * half].rearrange("p (t h d) -> p t h d", t=TT, h=heads)
                        for buf in (ra, rbuf))
                pool.wait_ge(r_mul.sem, r_mul.at(l, n))
                nc.gpsimd.tensor_tensor(x[:, :, :, 0:2 * half], a, b, ALU.add).then_inc(r_add.sem, 1)
                wait_apart(pool, r_add.sem, r_add.at(l, n))

            def diagonal(buf, signal_):
                blocks = buf.rearrange("p (a n) -> p a n", n=P)[:, 0:3:2, :]
                nc.gpsimd.affine_select(out=blocks, in_=blocks, pattern=[[0, 2], [-1, P]], compare_op=ALU.is_ge,
                                        fill=FAR, base=0, channel_multiplier=1).then_inc(signal_.sem, 1)

            def both(a, b):
                return U[:, :, a:b]

            with pool.Fori(0, LAYERS) as l:
                add_rotation(both(800, 1088).rearrange("p t (h d) -> p t h d", h=9), 1, 4, l)
                nc.gpsimd.tensor_copy(ki4.rearrange("p t (a d) -> p t a d", a=4),
                                      both(1056, 1088).unsqueeze(2).to_broadcast([P, TT, 4, DI])).then_inc(kcopy.sem, 1)
                nc.gpsimd.tensor_scalar(both(1088, 1096), both(1088, 1096), DI ** -0.5 * HI ** -0.5, None,
                                        ALU.mult).then_inc(wi_done.sem, 1)
                pool.wait_ge(latent_ms.sem, latent_ms.at(l, 1))
                nc.gpsimd.tensor_tensor(lstat[:, 2, :], lstat[:, 1, :], minus_half[:], ALU.pow).then_inc(
                    latent_rms.sem, 1)
                add_rotation(both(384, 416).unsqueeze(2), 2, 16, l)
                nc.gpsimd.tensor_copy(mk.rearrange("p t (h d) -> p t h d", h=HM)[:, :, :, NOPE:NOPE + ROPE],
                                      both(384, 416).unsqueeze(2).to_broadcast([P, TT, HM, ROPE])).then_inc(
                                          kcopy.sem, 1)
                add_rotation(both(416, 736).rearrange("p t (h d) -> p t h d", h=5), 3, 8, l)
                nc.gpsimd.tensor_copy(kk.rearrange("p t (a d) -> p t a d", a=2),
                                      both(672, 736).unsqueeze(2).to_broadcast([P, TT, 2, HD])).then_inc(kcopy.sem, 1)
                wait_apart(pool, score_in.sem, score_in.at(l, HI))
                diagonal(score, score_masked)
                add_rotation(mq.rearrange("p t (h d) -> p t h d", h=HM)[:, :, :, NOPE:NOPE + ROPE], 4, 16, l)
                wait_apart(pool, topk_done.sem, topk_done.at(l, 1))
                diagonal(nm, nm_masked)
                add_rotation(both(1096, 2632).rearrange("p t (h d) -> p t h d", h=24), 5, 8, l)
                for n in range(2):
                    wait_apart(pool, stat_done.sem, stat_done.at(l, n + 1))
                    nc.gpsimd.tensor_scalar(rstd2, mv2[:, :, 1], LN_EPS, None, ALU.add).then_inc(ln_step, 1)
                    pool.wait_ge(ln_step, n + 1)
                    nc.gpsimd.tensor_tensor(rstd2, rstd2, minus_half[:, 0:2], ALU.pow).then_inc(rstd_done.sem, 1)
                pool.sem_clear(ln_step)


N_FIRST = 4
N_CONST = 4
N_PARAMS = 15
SLOTS = P
PASS_KEYS = ("pT", "slots", "xg", "gu", "hT", "yg", "sc")
ARENA = 27500


def kernel(**inputs):
    from concourse import bacc
    from concourse.bass_utils import run_bass_kernel_spmd

    nc = bacc.Bacc("TRN2", target_bir_lowering=False, num_devices=1)
    arrays = {name: np.ascontiguousarray(a) for name, a in inputs.items()}
    arrays.update(constants())
    src = {name: nc.dram_tensor(f"in_{name}", a.shape, mybir.dt.from_np(a.dtype), kind="ExternalInput").ap()
           for name, a in arrays.items()}
    out = nc.dram_tensor("out", (1, SEQ, D), F32, kind="ExternalOutput").ap()
    build(nc, src, out)
    r = run_bass_kernel_spmd(nc, [{f"in_{name}": a for name, a in arrays.items()}], core_ids=[0])
    return r.results[0]["out"]
```
